# Optimizing a Trainium2 kernel written in Bass

```python
import jax, jax.numpy as jnp
from jax import lax
import numpy as np

D_MODEL = 1024
BATCH = 1
SEQ = 512
DEPTH = 1

N_MIXERS = 2
N_META = 16
FOX_HEADS = 16
FOX_HEAD_DIM = D_MODEL // FOX_HEADS
FOX_Q_BLOCK = 128
HGRN_EXPAND = 128
HGRN_HEADS = D_MODEL // HGRN_EXPAND
HGRN_DK = HGRN_EXPAND
HGRN_DV = D_MODEL // HGRN_HEADS
HGRN_CHUNK = 64
FFN_HIDDEN = -(-8 * D_MODEL // (3 * 256)) * 256
N_FOX = (DEPTH + N_MIXERS - 1) // N_MIXERS
N_HGRN = DEPTH // N_MIXERS
EPS = 1e-6


def rms_norm(x, gain):
    xf = x.astype(jnp.float32)
    y = xf * lax.rsqrt(jnp.mean(xf * xf, axis=-1, keepdims=True) + EPS)
    return (y * gain.astype(jnp.float32)).astype(x.dtype)

def _fox_attend(q_blk, c_q, pos_q, k, v, c_k, pos_k):
    s = jnp.einsum('bhqd,bhkd->bhqk', q_blk, k).astype(jnp.float32) * (FOX_HEAD_DIM ** -0.5)
    s = s + (c_q[..., :, None] - c_k[..., None, :])
    s = jnp.where(pos_k[None, :] <= pos_q[:, None], s, -jnp.inf)
    p = jax.nn.softmax(s, axis=-1)
    return jnp.einsum('bhqk,bhkd->bhqd', p, v.astype(jnp.float32))

def fox_mixer(h, w_in, b_f, q_gain, k_gain, w_out):
    B, L, D = h.shape
    n_blk = (L - N_META) // FOX_Q_BLOCK
    proj = h @ w_in
    q, k, v, gate, f_logit = jnp.split(proj, [D, 2 * D, 3 * D, 4 * D], axis=-1)
    q = rms_norm(q.reshape(B, L, FOX_HEADS, FOX_HEAD_DIM), q_gain)
    k = rms_norm(k.reshape(B, L, FOX_HEADS, FOX_HEAD_DIM), k_gain)
    v = v.reshape(B, L, FOX_HEADS, FOX_HEAD_DIM)
    log_f = jax.nn.log_sigmoid(f_logit.astype(jnp.float32) + b_f.astype(jnp.float32))
    c = jnp.cumsum(log_f, axis=1).transpose(0, 2, 1)
    q, k, v = (t.transpose(0, 2, 1, 3) for t in (q, k, v))
    pos = jnp.arange(L)
    o_meta = _fox_attend(q[:, :, :N_META], c[:, :, :N_META], pos[:N_META],
                         k[:, :, :N_META], v[:, :, :N_META], c[:, :, :N_META], pos[:N_META])
    qb = q[:, :, N_META:].reshape(B, FOX_HEADS, n_blk, FOX_Q_BLOCK, FOX_HEAD_DIM).transpose(2, 0, 1, 3, 4)
    cb = c[:, :, N_META:].reshape(B, FOX_HEADS, n_blk, FOX_Q_BLOCK).transpose(2, 0, 1, 3)
    pb = pos[N_META:].reshape(n_blk, FOX_Q_BLOCK)
    o_real = lax.map(lambda a: _fox_attend(a[0], a[1], a[2], k, v, c, pos), (qb, cb, pb))
    o_real = o_real.transpose(1, 2, 0, 3, 4).reshape(B, FOX_HEADS, L - N_META, FOX_HEAD_DIM)
    o = jnp.concatenate([o_meta, o_real], axis=2).transpose(0, 2, 1, 3).reshape(B, L, D)
    o = o * jax.nn.sigmoid(gate.astype(jnp.float32))
    return (o.astype(h.dtype) @ w_out).astype(h.dtype)

def _hgrn_chunk(S, inp):
    q, k, v, g = inp
    C = q.shape[2]
    b = jnp.cumsum(g, axis=2)
    causal = jnp.tril(jnp.ones((C, C), dtype=bool))
    diff = b[:, :, :, None, :] - b[:, :, None, :, :]
    decay = jnp.exp(jnp.where(causal[..., None], diff, -jnp.inf))
    attn = jnp.einsum('bhtd,bhsd,bhtsd->bhts', q, k, decay)
    o = jnp.einsum('bhts,bhsv->bhtv', attn, v) + jnp.einsum('bhtd,bhdv->bhtv', q * jnp.exp(b), S)
    b_last = b[:, :, -1:, :]
    S_new = jnp.exp(b_last[:, :, 0, :])[..., None] * S + jnp.einsum(
        'bhsd,bhsv->bhdv', k * jnp.exp(b_last - b), v)
    return S_new, o

def hgrn2_mixer(h, w_in, lb, g_gain, w_out):
    B, L, D = h.shape
    n_chunk = (L - N_META) // HGRN_CHUNK
    proj = h @ w_in
    q, f_logit, i, g_out = jnp.split(proj, 4, axis=-1)
    z = f_logit.astype(jnp.float32)
    lbf = lb.astype(jnp.float32)
    log_f = jnp.logaddexp(jnp.log(lbf), jnp.log1p(-lbf) + jax.nn.log_sigmoid(z))
    k = (1.0 - lbf) * jax.nn.sigmoid(-z)
    q = jax.nn.silu(q.astype(jnp.float32))
    v = i.astype(jnp.float32)
    heads = lambda t, d: t.reshape(B, L, HGRN_HEADS, d).transpose(0, 2, 1, 3)
    q, k, log_f, v = heads(q, HGRN_DK), heads(k, HGRN_DK), heads(log_f, HGRN_DK), heads(v, HGRN_DV)
    S0 = jnp.zeros((B, HGRN_HEADS, HGRN_DK, HGRN_DV), jnp.float32)
    S_meta, o_meta = _hgrn_chunk(S0, (q[:, :, :N_META], k[:, :, :N_META], v[:, :, :N_META], log_f[:, :, :N_META]))
    chunks = lambda t: t[:, :, N_META:].reshape(B, HGRN_HEADS, n_chunk, HGRN_CHUNK, t.shape[-1]).transpose(2, 0, 1, 3, 4)
    _, o_real = lax.scan(_hgrn_chunk, S_meta, (chunks(q), chunks(k), chunks(v), chunks(log_f)))
    o_real = o_real.transpose(1, 2, 0, 3, 4).reshape(B, HGRN_HEADS, L - N_META, HGRN_DV)
    o = jnp.concatenate([o_meta, o_real], axis=2).transpose(0, 2, 1, 3)
    o = rms_norm(o, g_gain) * jax.nn.silu(g_out.astype(jnp.float32).reshape(B, L, HGRN_HEADS, HGRN_DV))
    return (o.reshape(B, L, D).astype(h.dtype) @ w_out).astype(h.dtype)

def swiglu(h, w_in, w_out):
    gate, up = jnp.split(h @ w_in, 2, axis=-1)
    return ((jax.nn.silu(gate) * up) @ w_out).astype(h.dtype)

def first_inputs(seed: int = 0) -> dict:
    key = jax.random.key(seed)
    ks = jax.random.split(key, 18)
    D = D_MODEL
    nrm = lambda k, shape, fan: jax.random.normal(k, shape, jnp.float32) * fan ** -0.5
    gain = lambda k, shape: 1.0 + 0.02 * jax.random.normal(k, shape, jnp.float32)
    return {
        "x": jax.random.normal(ks[0], (BATCH, SEQ, D), jnp.float32),
        "meta_tokens": jax.random.normal(ks[1], (N_META, D), jnp.float32),
        "attn_norm": gain(ks[2], (DEPTH, D)),
        "ffn_norm": gain(ks[3], (DEPTH, D)),
        "final_norm": gain(ks[4], (D,)),
        "fox_w_in": nrm(ks[5], (N_FOX, D, 4 * D + FOX_HEADS), D),
        "fox_b_f": jax.random.uniform(ks[6], (N_FOX, FOX_HEADS), jnp.float32, 1.0, 4.0),
        "fox_q_norm": gain(ks[7], (N_FOX, FOX_HEAD_DIM)),
        "fox_k_norm": gain(ks[8], (N_FOX, FOX_HEAD_DIM)),
        "fox_w_out": nrm(ks[9], (N_FOX, D, D), D),
        "hgrn_w_in": nrm(ks[10], (N_HGRN, D, 4 * D), D),
        "hgrn_lower_bounds": 0.1 * jax.random.normal(ks[11], (DEPTH, D), jnp.float32),
        "hgrn_g_norm": gain(ks[12], (N_HGRN, HGRN_DV)),
        "hgrn_w_out": nrm(ks[13], (N_HGRN, D, D), D),
        "ffn_w_in": nrm(ks[14], (DEPTH, D, 2 * FFN_HIDDEN), D),
        "ffn_w_out": nrm(ks[15], (DEPTH, FFN_HIDDEN, D), FFN_HIDDEN),
    }

def first_block(x, meta_tokens, attn_norm, ffn_norm, final_norm, fox_w_in, fox_b_f, fox_q_norm,
              fox_k_norm, fox_w_out, hgrn_w_in, hgrn_lower_bounds, hgrn_g_norm, hgrn_w_out,
              ffn_w_in, ffn_w_out):
    B = x.shape[0]
    meta = jnp.broadcast_to(meta_tokens[None].astype(x.dtype), (B, N_META, D_MODEL))
    h = jnp.concatenate([meta, x], axis=1)
    lb_soft = jax.nn.softmax(hgrn_lower_bounds.astype(jnp.float32), axis=0)
    lower_bounds = jnp.cumsum(lb_soft, axis=0) - lb_soft[0]
    for i in range(DEPTH):
        hn = rms_norm(h, attn_norm[i])
        j = i // N_MIXERS
        if i % N_MIXERS == 0:
            h = h + fox_mixer(hn, fox_w_in[j], fox_b_f[j], fox_q_norm[j], fox_k_norm[j], fox_w_out[j])
        else:
            h = h + hgrn2_mixer(hn, hgrn_w_in[j], lower_bounds[i], hgrn_g_norm[j], hgrn_w_out[j])
        h = h + swiglu(rms_norm(h, ffn_norm[i]), ffn_w_in[i], ffn_w_out[i])
    h = rms_norm(h, final_norm)
    return h[:, N_META:]


GLA_HEADS = 4
GLA_DK = D_MODEL // 2 // GLA_HEADS
GLA_DV = D_MODEL // GLA_HEADS
GLA_GATE_RANK = 16
GLA_GATE_TAU = 16.0
GLA_CHUNK = 64
GLA_IN = 2 * GLA_HEADS * GLA_DK + GLA_HEADS * GLA_DV + GLA_GATE_RANK + GLA_HEADS * GLA_DV
MLA_HEADS = 8
MLA_NOPE = 128
MLA_ROPE = 64
MLA_V = D_MODEL // MLA_HEADS
MLA_Q_LORA = D_MODEL // 4
MLA_KV_LORA = D_MODEL // 8
MLA_IN = MLA_Q_LORA + MLA_KV_LORA + MLA_ROPE
MLA_SCALE = (MLA_NOPE + MLA_ROPE) ** -0.5
ROPE_THETA = 10000.0
Q_BLOCK = 128
MOE_GROUPS = 8
MOE_PER_GROUP = 8
MOE_EXPERTS = MOE_GROUPS * MOE_PER_GROUP
MOE_TOPK = 2
MOE_FF = D_MODEL // 4
MOE_BLOCK = 128


def rmsnorm(x, g):
    x32 = x.astype(jnp.float32)
    y = x32 * lax.rsqrt(jnp.mean(x32 * x32, axis=-1, keepdims=True) + EPS)
    return (y * g.astype(jnp.float32)).astype(x.dtype)

def rope_tables(positions):
    inv_freq = 1.0 / (ROPE_THETA ** (jnp.arange(0, MLA_ROPE, 2, dtype=jnp.float32) / MLA_ROPE))
    ang = positions.astype(jnp.float32)[..., None] * inv_freq
    return jnp.cos(ang), jnp.sin(ang)

def apply_rope(t, cos, sin):
    t32 = t.astype(jnp.float32)
    t1, t2 = jnp.split(t32, 2, axis=-1)
    return jnp.concatenate([t1 * cos - t2 * sin, t2 * cos + t1 * sin], axis=-1).astype(t.dtype)

def gla_mixer(h, w_in, w_gate, b_gate, out_norm, w_o):
    bsz, seq, _ = h.shape
    nc = seq // GLA_CHUNK
    qk = GLA_HEADS * GLA_DK
    vd = GLA_HEADS * GLA_DV
    proj = h @ w_in
    q, k, v, a_lr, r = jnp.split(proj, [qk, 2 * qk, 2 * qk + vd, 2 * qk + vd + GLA_GATE_RANK], axis=-1)
    log_a = jax.nn.log_sigmoid((a_lr @ w_gate + b_gate).astype(jnp.float32)) / GLA_GATE_TAU

    def chunks(t, d):
        return t.reshape(bsz, nc, GLA_CHUNK, GLA_HEADS, d).transpose(0, 3, 1, 2, 4).astype(jnp.float32)

    qc = chunks(q, GLA_DK) * (GLA_DK ** -0.5)
    kc = chunks(k, GLA_DK)
    vc = chunks(v, GLA_DV)
    g = jnp.cumsum(chunks(log_a, GLA_DK), axis=3)
    g_mid = g[:, :, :, GLA_CHUNK // 2:GLA_CHUNK // 2 + 1]
    g_last = g[:, :, :, -1:]
    causal = jnp.tril(jnp.ones((GLA_CHUNK, GLA_CHUNK), dtype=bool))
    a_intra = jnp.einsum('bhnid,bhnjd->bhnij', qc * jnp.exp(g - g_mid), kc * jnp.exp(g_mid - g))
    o_intra = jnp.einsum('bhnij,bhnjv->bhniv', jnp.where(causal, a_intra, 0.0), vc)
    q_inter = jnp.moveaxis(qc * jnp.exp(g), 2, 0)
    k_state = jnp.moveaxis(kc * jnp.exp(g_last - g), 2, 0)
    decay = jnp.moveaxis(jnp.exp(g_last[:, :, :, 0]), 2, 0)
    v_s = jnp.moveaxis(vc, 2, 0)

    def step(state, inp):
        q_i, k_i, v_i, d_i = inp
        o_i = jnp.einsum('bhid,bhdv->bhiv', q_i, state)
        state = state * d_i[..., None] + jnp.einsum('bhjd,bhjv->bhdv', k_i, v_i)
        return state, o_i

    s0 = jnp.zeros((bsz, GLA_HEADS, GLA_DK, GLA_DV), jnp.float32)
    _, o_inter = lax.scan(step, s0, (q_inter, k_state, v_s, decay))
    o = o_intra + jnp.moveaxis(o_inter, 0, 2)
    o = o.transpose(0, 2, 3, 1, 4).reshape(bsz, seq, GLA_HEADS, GLA_DV)
    o = o * lax.rsqrt(jnp.mean(o * o, axis=-1, keepdims=True) + EPS) * out_norm.astype(jnp.float32)
    o = o.reshape(bsz, seq, vd) * jax.nn.silu(r.astype(jnp.float32))
    return o.astype(h.dtype) @ w_o

def mla_mixer(h, cos, sin, w_in, q_norm, w_uq, kv_norm, w_uk, w_uv, w_o):
    bsz, seq, _ = h.shape
    nqb = seq // Q_BLOCK
    proj = h @ w_in
    c_q, c_kv, k_rope = jnp.split(proj, [MLA_Q_LORA, MLA_Q_LORA + MLA_KV_LORA], axis=-1)
    c_q = rmsnorm(c_q, q_norm)
    c_kv = rmsnorm(c_kv, kv_norm)
    q = jnp.einsum('bsc,chd->bshd', c_q, w_uq)
    q_nope, q_rope = q[..., :MLA_NOPE], q[..., MLA_NOPE:]
    q_rope = apply_rope(q_rope, cos[:, :, None, :], sin[:, :, None, :])
    k_rope = apply_rope(k_rope, cos, sin)
    q_lat = jnp.einsum('bshn,chn->bshc', q_nope, w_uk)
    q_cat = jnp.concatenate([q_lat, q_rope], axis=-1) * MLA_SCALE
    k_cat = jnp.concatenate([c_kv, k_rope], axis=-1)
    q_blocks = q_cat.reshape(bsz, nqb, Q_BLOCK, MLA_HEADS, MLA_KV_LORA + MLA_ROPE).transpose(1, 0, 2, 3, 4)
    k_pos = jnp.arange(seq)

    def attend(args):
        q_b, b_idx = args
        s = jnp.einsum('bqhc,bkc->bhqk', q_b, k_cat).astype(jnp.float32)
        q_pos = b_idx * Q_BLOCK + jnp.arange(Q_BLOCK)
        s = jnp.where(k_pos[None, :] <= q_pos[:, None], s, -jnp.inf)
        p = jax.nn.softmax(s, axis=-1).astype(c_kv.dtype)
        return jnp.einsum('bhqk,bkc->bqhc', p, c_kv)

    o_lat = lax.map(attend, (q_blocks, jnp.arange(nqb)))
    o_lat = o_lat.transpose(1, 0, 2, 3, 4).reshape(bsz, seq, MLA_HEADS, MLA_KV_LORA)
    o = jnp.einsum('bshc,chv->bshv', o_lat, w_uv).reshape(bsz, seq, MLA_HEADS * MLA_V)
    return o @ w_o

def hier_moe(h, w_group, w_expert, w1, w3, w2):
    bsz, seq, dm = h.shape
    n_tok = bsz * seq
    xf = h.reshape(n_tok, dm)
    tok = jnp.arange(n_tok)
    g_logits = (xf @ w_group).astype(jnp.float32)
    g_prob = jax.nn.softmax(g_logits, axis=-1)
    g_sel = jnp.argmax(g_logits, axis=-1)
    g_w = g_prob[tok, g_sel]
    e_logits = (xf @ w_expert).astype(jnp.float32).reshape(n_tok, MOE_GROUPS, MOE_PER_GROUP)
    e_prob = jax.nn.softmax(e_logits[tok, g_sel], axis=-1)
    top_p, top_i = lax.top_k(e_prob, MOE_TOPK)
    gates = g_w[:, None] * top_p / jnp.sum(top_p, axis=-1, keepdims=True)
    expert_id = g_sel[:, None] * MOE_PER_GROUP + top_i
    n_asg = n_tok * MOE_TOPK
    flat_e = expert_id.reshape(n_asg)
    flat_tok = jnp.arange(n_asg) // MOE_TOPK
    flat_gate = gates.reshape(n_asg)
    order = jnp.argsort(flat_e)
    se, stok, sgate = flat_e[order], flat_tok[order], flat_gate[order]
    counts = jax.ops.segment_sum(jnp.ones_like(flat_e), flat_e, num_segments=MOE_EXPERTS)
    starts = jnp.cumsum(counts) - counts
    padded = (counts + MOE_BLOCK - 1) // MOE_BLOCK * MOE_BLOCK
    pend = jnp.cumsum(padded)
    pstarts = pend - padded
    dest = pstarts[se] + (jnp.arange(n_asg) - starts[se])
    n_slots = n_asg + MOE_EXPERTS * MOE_BLOCK
    n_blocks = n_slots // MOE_BLOCK
    slot_tok = jnp.full((n_slots,), n_tok, dtype=jnp.int32).at[dest].set(stok.astype(jnp.int32))
    slot_gate = jnp.zeros((n_slots,), jnp.float32).at[dest].set(sgate)
    block_e = jnp.minimum(jnp.searchsorted(pend, jnp.arange(n_blocks) * MOE_BLOCK, side='right'), MOE_EXPERTS - 1)
    x_pad = jnp.concatenate([xf, jnp.zeros((1, dm), xf.dtype)], axis=0)
    xs = x_pad[slot_tok].reshape(n_blocks, MOE_BLOCK, dm)

    def expert_block(args):
        xb, e = args
        hid = jax.nn.silu(xb @ w1[e]) * (xb @ w3[e])
        return hid @ w2[e]

    ys = lax.map(expert_block, (xs, block_e)).reshape(n_slots, dm)
    ys = ys * slot_gate[:, None].astype(ys.dtype)
    out = jnp.zeros((n_tok + 1, dm), ys.dtype).at[slot_tok].add(ys)[:n_tok]
    return out.reshape(bsz, seq, dm)

def second_inputs(seed: int = 0) -> dict:
    key = jax.random.key(seed)
    ks = jax.random.split(key, 24)
    f32 = jnp.float32
    n_gla = (DEPTH + N_MIXERS - 1) // N_MIXERS
    n_mla = DEPTH // N_MIXERS

    def nrm(k, shape, fan_in):
        return jax.random.normal(k, shape, f32) * (fan_in ** -0.5)

    def gain(k, shape):
        return 1.0 + 0.1 * jax.random.normal(k, shape, f32)

    x = jax.random.normal(ks[0], (BATCH, SEQ, D_MODEL), f32)
    offsets = jax.random.randint(ks[1], (BATCH, 1), 0, 4096, dtype=jnp.int32)
    positions = offsets + jnp.arange(SEQ, dtype=jnp.int32)[None, :]
    return {
        'x': x,
        'positions': positions,
        'attn_norm': gain(ks[2], (DEPTH, D_MODEL)),
        'ffn_norm': gain(ks[3], (DEPTH, D_MODEL)),
        'final_norm': gain(ks[4], (D_MODEL,)),
        'gla_w_in': nrm(ks[5], (n_gla, D_MODEL, GLA_IN), D_MODEL),
        'gla_w_gate': nrm(ks[6], (n_gla, GLA_GATE_RANK, GLA_HEADS * GLA_DK), GLA_GATE_RANK),
        'gla_b_gate': 0.1 * jax.random.normal(ks[7], (n_gla, GLA_HEADS * GLA_DK), f32),
        'gla_out_norm': gain(ks[8], (n_gla, GLA_DV)),
        'gla_w_o': nrm(ks[9], (n_gla, GLA_HEADS * GLA_DV, D_MODEL), GLA_HEADS * GLA_DV),
        'mla_w_in': nrm(ks[10], (n_mla, D_MODEL, MLA_IN), D_MODEL),
        'mla_q_norm': gain(ks[11], (n_mla, MLA_Q_LORA)),
        'mla_w_uq': nrm(ks[12], (n_mla, MLA_Q_LORA, MLA_HEADS, MLA_NOPE + MLA_ROPE), MLA_Q_LORA),
        'mla_kv_norm': gain(ks[13], (n_mla, MLA_KV_LORA)),
        'mla_w_uk': nrm(ks[14], (n_mla, MLA_KV_LORA, MLA_HEADS, MLA_NOPE), MLA_KV_LORA),
        'mla_w_uv': nrm(ks[15], (n_mla, MLA_KV_LORA, MLA_HEADS, MLA_V), MLA_KV_LORA),
        'mla_w_o': nrm(ks[16], (n_mla, MLA_HEADS * MLA_V, D_MODEL), MLA_HEADS * MLA_V),
        'moe_w_group': nrm(ks[17], (DEPTH, D_MODEL, MOE_GROUPS), D_MODEL),
        'moe_w_expert': nrm(ks[18], (DEPTH, D_MODEL, MOE_EXPERTS), D_MODEL),
        'moe_w1': nrm(ks[19], (DEPTH, MOE_EXPERTS, D_MODEL, MOE_FF), D_MODEL),
        'moe_w3': nrm(ks[20], (DEPTH, MOE_EXPERTS, D_MODEL, MOE_FF), D_MODEL),
        'moe_w2': nrm(ks[21], (DEPTH, MOE_EXPERTS, MOE_FF, D_MODEL), MOE_FF),
    }

def second_block(x, positions, attn_norm, ffn_norm, final_norm,
              gla_w_in, gla_w_gate, gla_b_gate, gla_out_norm, gla_w_o,
              mla_w_in, mla_q_norm, mla_w_uq, mla_kv_norm, mla_w_uk, mla_w_uv, mla_w_o,
              moe_w_group, moe_w_expert, moe_w1, moe_w3, moe_w2):
    cos, sin = rope_tables(positions)
    for i in range(DEPTH):
        j = i // N_MIXERS
        h = rmsnorm(x, attn_norm[i])
        if i % N_MIXERS == 0:
            m = gla_mixer(h, gla_w_in[j], gla_w_gate[j], gla_b_gate[j], gla_out_norm[j], gla_w_o[j])
        else:
            m = mla_mixer(h, cos, sin, mla_w_in[j], mla_q_norm[j], mla_w_uq[j], mla_kv_norm[j],
                          mla_w_uk[j], mla_w_uv[j], mla_w_o[j])
        x = x + m.astype(x.dtype)
        h = rmsnorm(x, ffn_norm[i])
        x = x + hier_moe(h, moe_w_group[i], moe_w_expert[i], moe_w1[i], moe_w3[i], moe_w2[i]).astype(x.dtype)
    return rmsnorm(x, final_norm)


def setup_inputs(seed=0):
    out = dict(first_inputs(seed))
    for name, value in second_inputs(seed + 1).items():
        if name != "x":
            out[name + "_2"] = value
    return out


def reference(
    x, meta_tokens, attn_norm, ffn_norm, final_norm, fox_w_in, fox_b_f, fox_q_norm, fox_k_norm,
    fox_w_out, hgrn_w_in, hgrn_lower_bounds, hgrn_g_norm, hgrn_w_out, ffn_w_in, ffn_w_out,
    positions_2, attn_norm_2, ffn_norm_2, final_norm_2, gla_w_in_2, gla_w_gate_2, gla_b_gate_2,
    gla_out_norm_2, gla_w_o_2, mla_w_in_2, mla_q_norm_2, mla_w_uq_2, mla_kv_norm_2, mla_w_uk_2,
    mla_w_uv_2, mla_w_o_2, moe_w_group_2, moe_w_expert_2, moe_w1_2, moe_w3_2, moe_w2_2,
):
    x = first_block(
        x, meta_tokens, attn_norm, ffn_norm, final_norm, fox_w_in, fox_b_f, fox_q_norm,
        fox_k_norm, fox_w_out, hgrn_w_in, hgrn_lower_bounds, hgrn_g_norm, hgrn_w_out, ffn_w_in,
        ffn_w_out,
    )
    return second_block(
        x, positions_2, attn_norm_2, ffn_norm_2, final_norm_2, gla_w_in_2, gla_w_gate_2,
        gla_b_gate_2, gla_out_norm_2, gla_w_o_2, mla_w_in_2, mla_q_norm_2, mla_w_uq_2,
        mla_kv_norm_2, mla_w_uk_2, mla_w_uv_2, mla_w_o_2, moe_w_group_2, moe_w_expert_2,
        moe_w1_2, moe_w3_2, moe_w2_2,
    )


_drawn_inputs = setup_inputs


def setup_inputs(seed=0):
    import zlib

    import numpy as np

    out = dict(_drawn_inputs(seed))
    spreads = {}
    factors = {'attn_norm': 3.454, 'fox_q_norm': 5.936, 'fox_k_norm': 4.235, 'ffn_norm': 4.125}
    for name, (base, spread) in spreads.items():
        noise = np.random.default_rng([zlib.crc32(name.encode()), seed]).standard_normal(out[name].shape)
        drawn = base * np.exp(spread * noise) if base else spread * noise
        out[name] = __import__('jax').numpy.asarray(drawn.astype(out[name].dtype))
    for name, factor in factors.items():
        out[name] = (out[name] * factor).astype(out[name].dtype)
    return out
```

```python
from contextlib import ExitStack

import concourse.bass as bass
from concourse import mybir

F32 = mybir.dt.float32
I32 = mybir.dt.int32
U32 = mybir.dt.uint32
ALU = mybir.AluOpType
ACT = mybir.ActivationFunctionType
AX = mybir.AxisListType.X

P = 128
EPS = 1e-6
NEG = -1e30
W_SLOTS = 3
C = 128
E_SLOTS = 4
SKIP = 1 << 20


class Count:

    def __init__(self, eng, sem):
        self.eng, self.sem, self.n = eng, sem, 0

    def inc(self, ins):
        self.n += 1
        return ins.then_inc(self.sem, 1)

    def wait(self):
        self.eng.wait_ge(self.sem, self.n)

    def link(self, ins):
        self.inc(ins)
        self.wait()


def wait(eng, sem, value):
    if not isinstance(value, int) or value > 0:
        eng.wait_ge(sem, value)


def program(nc, x, meta_tokens, attn_norm, ffn_norm, final_norm, fox_w_in, fox_b_f, fox_q_norm, fox_k_norm,
            fox_w_out, ffn_w_in, ffn_w_out, attn_norm_2, ffn_norm_2, final_norm_2, gla_w_in, gla_w_gate,
            gla_b_gate, gla_out_norm, gla_w_o, moe_w_group, moe_w_expert, moe_w1, moe_w3, moe_w2, out):
    _, SEQ, D = x.shape
    META = meta_tokens.shape[0]
    T = SEQ // P
    KD = D // P
    HEADS = fox_b_f.shape[1]
    HD = D // HEADS
    HA = HD + 2
    FH = ffn_w_out.shape[1]
    FT = FH // P
    GH = 4
    GK = gla_w_gate.shape[2] // GH
    GV = gla_out_norm.shape[1]
    RANK = gla_w_gate.shape[1]
    QK = GH * GK
    CH = 64
    NCH = SEQ // CH
    TAU = 16.0
    GROUPS = moe_w_group.shape[2]
    EXPERTS = moe_w_expert.shape[2]
    PER = EXPERTS // GROUPS
    FF = moe_w1.shape[3]
    KF = FF // P
    ASG = 2 * SEQ
    SPILL = (ASG - EXPERTS) // C
    NB = EXPERTS + SPILL
    QS = SEQ // C
    assert (META, HD, GK, GV, KF) == (16, 64, 128, 256, 2) and KD == 8 and T == 4

    hn_dram = nc.dram_tensor("hn_dram", [SEQ, D], F32)
    slot_dram = nc.dram_tensor("slot_dram", [C * NB, 1], I32)
    y_dram = nc.dram_tensor("y_dram", [ASG, D], F32)

    with ExitStack() as ctx:
        def sb(name, cols, dt=F32):
            return ctx.enter_context(nc.sbuf_tensor(name, [P, cols], dt))

        def sem(name):
            return ctx.enter_context(nc.semaphore(name))

        ps = ctx.enter_context(nc.psum_tensor("ps", [P, 8 * 512], F32))

        def bank(b, n=1):
            return ps[:, b * 512:(b + n) * 512]

        wring = sb("wring", W_SLOTS * 4096)
        big = sb("big", 16384)
        xres_t = sb("xres", T * D)
        hT_t = sb("hT", KD * SEQ)
        xn_t = sb("xn", T * D)
        mkv = sb("mkv", 2 * D)
        arena = sb("arena", 6144)
        hTm_t = sb("hTm", KD * META)
        gainrow = sb("gainrow", D)
        gcols = sb("gcols", 3 * KD)
        outn = sb("outn", GV)
        qgain = sb("qgain", 1)
        kgain = sb("kgain", 1)
        bf = sb("bf", HEADS)
        bgate = sb("bgate", GH)
        wgate = sb("wgate", QK)
        ident = sb("ident", P)
        tri = sb("tri", P)
        strict = sb("strict", P)
        ones = sb("ones", P)
        amask = sb("amask", P)
        gmask = sb("gmask", P)
        ss = sb("ss", 8)
        rstd = sb("rstd", 8)
        ssq = sb("ssq", 9 * HEADS)
        rsq = sb("rsq", 9 * HEADS)
        zf = sb("zf", 5 * HEADS)
        zt = sb("zt", 5 * HEADS)
        cc = sb("cc", 5 * HEADS)
        ncc = sb("ncc", 5 * HEADS)
        mxn = sb("mxn", 2 * 64)
        rsum = sb("rsum", 64)
        rinv = sb("rinv", 64)
        decay = sb("decay", GH * NCH)
        ssg = sb("ssg", 3 * GH * T)
        half = sb("half", 9 * HEADS)

        alrT = xn_t[:, 0:SEQ]
        reset = xn_t[:, SEQ:2 * SEQ]
        xres = xres_t[:, :].rearrange("p (t d) -> p t d", t=T)
        hT = hT_t[:, :].rearrange("p (k s) -> p k s", k=KD)
        xn = xn_t[:, :].rearrange("p (t d) -> p t d", t=T)
        hTm = hTm_t[:, :].rearrange("p (k s) -> p k s", k=KD)
        qkvg = big[:, :].rearrange("p (t n) -> p t n", t=T)
        metax = big[0:META, 0:D]
        metan = big[0:META, D:2 * D]

        at = [0]

        def part(n):
            at[0] += n
            return arena[:, at[0] - n:at[0]]

        qa = [part(T * HA).rearrange("p (t d) -> p t d", t=T) for _ in range(2)]
        ka = [part(T * HA).rearrange("p (t d) -> p t d", t=T) for _ in range(2)]
        kam = [part(HA) for _ in range(2)]
        QT = [part(SEQ) for _ in range(2)]
        KT = [part(META + SEQ) for _ in range(2)]
        Pb = [part(META + SEQ) for _ in range(3)]
        PT = [part(5 * P) for _ in range(2)]
        scr = [arena[:, 4096:5120], arena[:, 5120:6144]]
        sg = [arena[:, 0:512], arena[:, 512:1024]]
        actT = big[:, 0:FT * SEQ].rearrange("p (f s) -> p f s", f=FT)

        qT = big[:, 0:2048].rearrange("p (h s) -> p h s", h=GH)
        kT = big[:, 2048:4096].rearrange("p (h s) -> p h s", h=GH)
        gz = big[:, 4096:6144].rearrange("p (h s) -> p h s", h=GH)
        gg = big[:, 6144:8192].rearrange("p (h s) -> p h s", h=GH)
        gv = big[:, 8192:12288].rearrange("p (t n) -> p t n", t=T)
        gr = big[:, 12288:16384].rearrange("p (t n) -> p t n", t=T)
        qiT = hT_t[:, 0:2048].rearrange("p (h s) -> p h s", h=GH)
        ksT = hT_t[:, 2048:4096].rearrange("p (h s) -> p h s", h=GH)
        kst = mkv[:, :].rearrange("p (h t d) -> p h t d", h=GH, t=T)
        tmp1 = arena[:, 0:512]
        D1, D2 = arena[:, 1024:1536], arena[:, 1536:2048]
        Ex = [arena[:, 2048 + 512 * i:2560 + 512 * i] for i in range(4)]
        atm = arena[:, 0:2048].rearrange("p (h t s) -> p h t s", h=GH, t=T)
        St = arena[:, 4096:6144].rearrange("p (h b v) -> p h b v", h=GH, b=2)

        s_w = [sem(f"weights_in_{i}") for i in range(W_SLOTS)]
        s_x = [sem(f"x_in_{t}") for t in range(T)]
        s_meta = sem("meta_in")
        s_small = sem("small_in")
        s_row = sem("gainrow_in")
        s_row2 = sem("later_gainrow_in")
        s_cst = sem("constants_made")
        s_pool = sem("pool_self")
        s_ms = sem("mean_square_ready")
        s_pw = sem("root_taken")
        s_dve = sem("dve_self")
        s_act = sem("act_self")
        s_ss = sem("squares_summed")
        s_xn = sem("normed")
        s_tp = sem("transposed")
        s_tpA = sem("transposed_out_act")
        s_tpD = sem("transposed_out_dve")
        s_mB = sem("proj_done")
        s_eA = sem("proj_out_act")
        s_eD = sem("proj_out_dve")
        s_sqh = sem("head_squares")
        s_rs = sem("head_rstd")
        s_lf = sem("forget_log")
        s_cps = sem("decay_sums")
        s_c = sem("decay_ready")
        s_stage = sem("head_staged")
        s_qkt = sem("head_transposed")
        s_qkA = sem("head_qT_ready")
        s_S = sem("scores_ready")
        s_mx = sem("row_max_ready")
        s_exp = sem("probs_ready")
        s_T = sem("probs_transposed")
        s_ptA = sem("probsT_out_act")
        s_pv = sem("pv_done")
        s_o = sem("attn_out_ready")
        s_mO = sem("outproj_done")
        s_res = sem("residual_added")
        s_mH = sem("gate_up_done")
        s_silu = sem("silu_done")
        s_hid = sem("hidden_ready")
        s_x2 = sem("x2_ready")
        s_mG = sem("gla_proj_done")
        s_gA = sem("gla_proj_out_act")
        s_gD = sem("gla_proj_out_dve")
        s_gdv = sem("gla_dve_step")
        s_gac = sem("gla_act_step")
        s_gpl = sem("gla_pool_step")
        s_gr = sem("gla_gate_gained")
        s_reset = sem("chunk_starts_set")
        s_gU = sem("gla_units")
        s_kst = sem("k_state_ready")
        s_atm = sem("attn_masked")
        s_U = sem("state_update_ready")
        s_S2 = sem("state_ready")
        s_in = sem("chunk_out_done")
        s_gss = sem("gla_squares")
        s_go = sem("gla_out_ready")
        s_hnrow = sem("moe_input_ready")
        s_hnd = sem("moe_input_stored")
        s_rt = sem("router_logits")
        s_rte = sem("router_exp")
        s_oh = sem("one_hots_ready")
        s_pre = sem("prefix_ready")
        s_idx = sem("slots_ready")
        s_fill = sem("slot_table_filled")
        s_scat = sem("slot_scattered")
        s_tab = sem("slot_table_in")
        s_tabs = sem("tables_ready")
        s_xz = sem("xe_zeroed")
        s_ew = [sem(f"expert_in_{i}") for i in range(E_SLOTS)]
        s_xe = [sem(f"tokens_in_{i}") for i in range(E_SLOTS)]
        s_ic = sem("index_copied")
        s_mx1 = sem("moe_xT")
        s_mxA = sem("moe_xT_out_act")
        s_mxD = sem("moe_xT_out_dve")
        s_gu = sem("moe_gate_up")
        s_msl = sem("moe_silu")
        s_mhid = sem("moe_hidden")
        s_mhT = sem("moe_hiddenT")
        s_mhTe = sem("moe_hiddenT_out")
        s_my = sem("moe_y")
        s_myA = sem("moe_y_out_act")
        s_myD = sem("moe_y_out_dve")
        s_ys = [sem(f"y_stored_{i}") for i in range(2)]
        s_yl = sem("y_loaded")
        s_tick = sem("waits_taken")
        s_fin = sem("final_ready")
        s_out = sem("out_stored")

        W0 = fox_w_in[0].rearrange("(k p) n -> p k n", p=P)
        WO = fox_w_out[0].rearrange("(k p) n -> p k n", p=P)
        WI = ffn_w_in[0].rearrange("(k p) n -> p k n", p=P)
        W2 = ffn_w_out[0].rearrange("(k p) n -> p k n", p=P)
        WG = gla_w_in[0].rearrange("(k p) n -> p k n", p=P)
        WGO = gla_w_o[0].rearrange("(k p) n -> p k n", p=P)
        tiles, tile_at, tile_ready = [], {}, {}
        slot_count = [0] * W_SLOTS

        def add_tile(name, cols, parts, release):
            w = len(tiles)
            slot = w % W_SLOTS
            k = max(a + n for a, n, _, _ in parts)
            view = wring[:, slot * 4096:slot * 4096 + k * cols].rearrange("p (k n) -> p k n", k=k)
            slot_count[slot] += 16 * len(parts)
            tiles.append((slot, [(view[:, a:a + n, c:c + s.shape[2]], s) for a, n, c, s in parts], release))
            tile_at[name], tile_ready[name] = view, (s_w[slot], slot_count[slot])

        unitsB = []
        for name, c0, n in (("k", D, 2), ("q", 0, 2), ("f", 4 * D, 1), ("v", 2 * D, 2), ("g", 3 * D, 2)):
            for j in range(n):
                if name == "f":
                    unitsB.append((name, j, 0, "D"))
                else:
                    for t in range(T + (name in "kv")):
                        eng = "A" if name == "g" else "D" if name == "q" and t % 4 else "AD"[t % 2]
                        unitsB.append((name, j, t, eng))
                cols = HEADS if name == "f" else 512
                add_tile(f"{name}{j}", cols, [(0, KD, 0, W0[:, :, c0 + j * 512:c0 + j * 512 + cols])],
                         (s_mB, len(unitsB)))
        for j in range(2):
            add_tile(f"wo{j}", 512, [(0, KD, 0, WO[:, :, j * 512:(j + 1) * 512])], (s_mO, 4 * (j + 1)))
        for j in range(FT // 2):
            add_tile(f"in{j}", 512, [(0, KD, 0, WI[:, :, j * 256:(j + 1) * 256]),
                                     (0, KD, 256, WI[:, :, FH + j * 256:FH + (j + 1) * 256])], (s_mH, 2 * (j + 1)))
        FK = [(a, min(8, FT - a)) for a in range(0, FT, 8)]
        for j in range(2):
            for i, (a, n) in enumerate(FK):
                add_tile(f"out{j}{i}", 512, [(0, n, 0, W2[:, a:a + n, j * 512:(j + 1) * 512])],
                         (s_mO, 8 + (j * len(FK) + i + 1) * 4))
        MO_FFN = 8 + 2 * len(FK) * 4
        unitsG = []
        for name, c0, n in (("a", 2 * QK + D, 1), ("q", 0, 1), ("k", QK, 1), ("v", 2 * QK, 2), ("r", 2 * QK + D + RANK, 2)):
            for j in range(n):
                if name == "a":
                    unitsG.append((name, 0, 0, "D"))
                else:
                    for t in range(T):
                        eng = {"q": "A", "k": "D", "v": "D", "r": "A"}[name]
                        unitsG.append((name, j, t, eng))
                cols = RANK if name == "a" else 512
                add_tile(f"g{name}{j}", cols, [(0, KD, 0, WG[:, :, c0 + j * 512:c0 + j * 512 + cols])],
                         (s_mG, len(unitsG)))
                if name == "q":
                    unitsG += [("z", 0, h, "A") for h in range(GH)]
        for j in range(2):
            add_tile(f"gwo{j}", 512, [(0, KD, 0, WGO[:, :, j * 512:(j + 1) * 512])],
                     (s_mO, MO_FFN + 4 * (j + 1)))
        NR = GROUPS + EXPERTS
        add_tile("rt", NR, [(0, KD, 0, moe_w_group[0].rearrange("(k p) n -> p k n", p=P)),
                            (0, KD, GROUPS, moe_w_expert[0].rearrange("(k p) n -> p k n", p=P))], (s_rt, 1))

        def obank(h, t):
            b = (t % 2) * 2 + h // 2
            return bank(b)[:, (h % 2) * GV:(h % 2 + 1) * GV]

        def ubank(h, c):
            b = 4 + (c % 2) * 2 + h // 2
            return bank(b)[:, (h % 2) * GV:(h % 2 + 1) * GV]

        def evacs(units, u):
            return sum(v[3] == units[u][3] for v in units[:u + 1])

        def tile_wait(pe, name):
            s, n = tile_ready[name]
            pe.wait_ge(s, n)

        def sbank(s, a, b):
            return ps[:, 512 * (s % 2) + a:512 * (s % 2) + b]

        PTB, OB, QB = 3 * 512, 5, 7

        block = ctx.enter_context(nc.Block())

        def eslot(i):
            base = (big if i < 2 else wring)[:, (i % 2) * 6144:(i % 2) * 6144 + 6144]
            return (base[:, 0:2048].rearrange("p (k n) -> p k n", k=KD),
                    base[:, 2048:4096].rearrange("p (k n) -> p k n", k=KD),
                    base[:, 4096:6144].rearrange("p (k n) -> p k n", k=KF))

        W1 = moe_w1[0].rearrange("e (p k) n -> e p (k n)", k=KD)
        W3 = moe_w3[0].rearrange("e (p k) n -> e p (k n)", k=KD)
        WW2 = moe_w2[0].rearrange("e (p k) n -> e p (k n)", k=KF)

        xe = [hT_t[:, i * D:(i + 1) * D] for i in range(4)]
        ye = [xn_t[:, i * D:(i + 1) * D] for i in range(2)]
        xeT = [xn_t[:, (2 + i) * D:(3 + i) * D].rearrange("p (k c) -> p k c", k=KD) for i in range(2)]
        msg = [arena[:, i * FF:(i + 1) * FF] for i in range(2)]
        mhid = [arena[:, 512 + i * FF:512 + (i + 1) * FF] for i in range(2)]
        mhT = [arena[:, 1024 + i * 256:1280 + i * 256].rearrange("p (k c) -> p k c", k=KF) for i in range(2)]
        lg = arena[:, 1536:1536 + T * NR].rearrange("p (t n) -> p t n", t=T)
        oh = [arena[:, 2048 + i * 256:2304 + i * 256].rearrange("p (t n) -> p t n", t=T) for i in range(3)]
        em = arena[:, 2816:3072].rearrange("p (t n) -> p t n", t=T)
        pre = arena[:, 3072:3328].rearrange("p (t n) -> p t n", t=T)
        cnt = arena[:, 3328:3392]
        ob = arena[:, 3392:3456]
        obe = arena[:, 3456:3520]
        obs = arena[:, 3520:3584]
        iog = arena[:, 3584:3648]
        ioe = arena[:, 3648:3712]
        one64 = arena[:, 3712:3776]
        rtm = arena[:, 3776:3840]
        gm8 = arena[:, 3840:3840 + 32].rearrange("p (t n) -> p t n", t=T)
        em8 = arena[:, 3872:3904].rearrange("p (t n) -> p t n", t=T)
        gsel = arena[:, 3904:3908]
        esel = arena[:, 3908:3916].rearrange("p (t k) -> p t k", t=T)
        gates = arena[:, 3916:3924].rearrange("p (t k) -> p t k", t=T)
        gwt = arena[:, 3924:3928]
        rs8 = arena[:, 3928:3960]
        xw = arena[:, 3960:3968]
        rk = arena[:, 3968:3976].rearrange("p (t k) -> p t k", t=T)
        stt = arena[:, 3976:3984].rearrange("p (t k) -> p t k", t=T)
        qq = arena[:, 3984:3992].rearrange("p (t k) -> p t k", t=T)
        bl = arena[:, 3992:4000].rearrange("p (t k) -> p t k", t=T)
        q1 = arena[:, 4000:4008].rearrange("p (t k) -> p t k", t=T)
        ovf = arena[:, 4008:4008 + SPILL + 1]
        osel = arena[:, 4016:4080]
        gi_u = sb("gi_u", 8 * T, U32)
        ei_u = sb("ei_u", 8 * T, U32)
        slot_i = sb("slot_i", 2 * T, I32)
        dest_i = sb("dest_i", 2 * T, I32)
        skip_i = arena[:, 4096:4096 + NB].bitcast(I32)
        dtab = arena[:, 4224:4224 + NB].bitcast(I32)
        ttab = arena[:, 4352:4352 + NB].bitcast(I32)
        ttf = arena[:, 4480:4480 + 2 * NB]
        ovf_i = sb("ovf_i", SPILL + 1, I32)
        gidx = sb("gidx", 4, I32)
        sidx = sb("sidx", 4, I32)

        @block.sync
        def _(sp):
            for t in range(T):
                sp.dma_start(xres[:, t, :], x[0, t * P:(t + 1) * P, :]).then_inc(s_x[t], 16)
            for w, (slot, dmas, release) in enumerate(tiles):
                if w >= W_SLOTS:
                    sp.wait_ge(*tiles[w - W_SLOTS][2])
                for dst, src in dmas:
                    sp.dma_start(dst, src).then_inc(s_w[slot], 16)

            def expert(e, j):
                a, b, c = eslot(j)
                for dst, src in ((a, W1), (b, W3), (c, WW2)):
                    sp.dma_start(dst.rearrange("p k n -> p (k n)"), src[e]).then_inc(s_ew[j], 16)

            sp.wait_ge(s_rt, 1)
            sp.wait_ge(s_go, GH * T)
            for j in range(E_SLOTS):
                expert(j, j)
            with sp.Fori(1, EXPERTS // E_SLOTS) as it:
                for j in range(E_SLOTS):
                    sp.wait_ge(s_my, it * E_SLOTS + (j + 1 - E_SLOTS))
                    expert(it * E_SLOTS + j, j)
            n_over = sp.value_load(ovf_i[0:1, SPILL:SPILL + 1], min_val=0, max_val=SPILL)
            with sp.If(n_over > 0):
                with sp.Fori(0, SPILL) as i:
                    sp.wait_ge(s_my, i + EXPERTS)
                    e = sp.value_load(ovf_i[0:1, bass.ds(i, 1)], min_val=0, max_val=EXPERTS - 1)
                    expert(e, 0)
            sp.wait_ge(s_fin, 1)
            for t in range(T):
                sp.wait_ge(s_fin, t + 1)
                sp.dma_start(out[0, t * P:(t + 1) * P, :], xres[:, t, :]).then_inc(s_out, 16)
            sp.wait_ge(s_out, 16 * T)

        @block.scalar
        def _(act):
            me = Count(act, s_act)
            small = [
                (gcols[:, 0:KD], attn_norm[0].rearrange("(k p) -> p k", p=P)),
                (gcols[:, KD:2 * KD], ffn_norm[0].rearrange("(k p) -> p k", p=P)),
                (gcols[:, 2 * KD:3 * KD], attn_norm_2[0].rearrange("(k p) -> p k", p=P)),
                (qgain[0:HD, :], fox_q_norm.rearrange("a p -> p a")),
                (kgain[0:HD, :], fox_k_norm.rearrange("a p -> p a")),
                (bgate[:, :], gla_b_gate[0].rearrange("(k p) -> p k", p=P)),
                (bf[:, :], fox_b_f.to_broadcast([P, HEADS])),
                (outn[:, :], gla_out_norm.to_broadcast([P, GV])),
                (wgate[0:RANK, :], gla_w_gate[0]),
            ]
            act.dma_start(metax, meta_tokens).then_inc(s_meta, 16)
            with nc.allow_non_contiguous_dma("small gains, once"):
                for dst, src in small:
                    act.dma_start(dst, src).then_inc(s_small, 16)
            act.dma_start(gainrow[:, :], final_norm.rearrange("(a n) -> a n", a=1).to_broadcast([P, D])).then_inc(s_row, 16)

            squared = [0]

            def squares(n, t, src, rows=P):
                n = squared[0]
                squared[0] += 1
                wait(act, s_ss, n - 1)
                act.activation(scr[n % 2][0:rows, :], src, ACT.Square, accum_out=ss[0:rows, t:t + 1]).then_inc(s_ss, 1)

            def tp_out(n, gain):
                for k in range(0, KD, 2):
                    act.wait_ge(s_tp, KD * n + (n > 0) + k + 1)
                    act.activation(hT[:, k, :], bank(k), ACT.Copy, scale=gain[:, k:k + 1] if gain is not None else 1.0).then_inc(s_tpA, 1)

            for t in range(T):
                act.wait_ge(s_x[t], 16)
                squares(0, t, xres[:, t, :])
            act.wait_ge(s_meta, 16)
            squares(0, T, metax, META)
            act.wait_ge(s_small, 16 * len(small))
            tp_out(0, gcols[:, 0:KD])

            def headsq(n, src, rows=P):
                if n >= 2:
                    act.wait_ge(s_rs, n - 1)
                act.activation(scr[n % 2][0:rows, :], src, ACT.Square).then_inc(s_sqh, 1)

            for u, (name, j, t, eng) in enumerate(unitsB):
                if eng == "A":
                    act.wait_ge(s_mB, u + 1)
                    o = {"q": 0, "k": D, "v": 2 * D, "g": 3 * D}[name] + j * 512
                    b = bank(u % 8)
                    if t == T:
                        o = (o - D if name == "k" else o - D)
                        act.copy(mkv[0:META, o:o + 512], b[0:META, :]).then_inc(s_eA, 1)
                    else:
                        act.activation(qkvg[:, t, o:o + 512], b, ACT.Sigmoid if name == "g" else ACT.Copy).then_inc(s_eA, 1)
                if (name, j) == ("f", 0):
                    act.wait_ge(s_eA, evacs(unitsB, max(v for v in range(u) if unitsB[v][3] == "A")))
                    act.wait_ge(s_eD, evacs(unitsB, max(v for v in range(u) if unitsB[v][3] == "D")))
                    for t2 in range(T):
                        headsq(t2, qkvg[:, t2, 0:D])
                    for t2 in range(T):
                        headsq(T + t2, qkvg[:, t2, D:2 * D])
                    headsq(2 * T, mkv[0:META, 0:D], META)
            act.wait_ge(s_lf, 1)
            act.activation(zt[:, :], zt[:, :], ACT.Exp).then_inc(s_lf, 1)
            act.wait_ge(s_lf, 2)
            act.activation(zt[:, :], zt[:, :], ACT.Ln, bias=1.0).then_inc(s_lf, 1)

            NS = HEADS * T

            def qk_out(h, i):
                act.wait_ge(s_qkt, 3 * h + i + 1)
                if h >= 2 and i == 0:
                    act.wait_ge(s_S, T * (h - 1))
                dst, gain, n = ((QT[h % 2][0:HA, :], qgain, SEQ), (KT[h % 2][0:HA, META:META + SEQ], kgain, SEQ),
                                (KT[h % 2][0:HA, 0:META], kgain, META))[i]
                act.activation(dst, bank(QB)[0:HA, 0:n], ACT.Copy, scale=gain[0:HA, :]).then_inc(s_qkA, 1)

            def exps(s):
                i = s % T
                n = META + P * (i + 1)
                act.wait_ge(s_mx, s + 1)
                if s >= 3:
                    act.wait_ge(s_T, s - 2)
                act.activation(Pb[s % 3][:, 0:n], sbank(s, 0, n), ACT.Exp,
                               bias=mxn[:, 64 + s:65 + s], accum_out=rsum[:, s:s + 1]).then_inc(s_exp, 1)

            def pt_out(s):
                i = s % T
                act.wait_ge(s_T, s + 1)
                if s >= 2:
                    act.wait_ge(s_pv, s - 1)
                act.copy(PT[s % 2][0:META, 0:P], ps[0:META, PTB:PTB + P])
                act.copy(PT[s % 2][:, P:P * (i + 2)], ps[:, PTB + P:PTB + P * (i + 2)]).then_inc(s_ptA, 1)

            act.wait_ge(s_rs, 9)
            act.wait_ge(s_c, 1)
            for i in range(3):
                qk_out(0, i)
            exps(0)
            for s in range(NS):
                if s % T < 3 and s // T + 1 < HEADS:
                    qk_out(s // T + 1, s % T)
                if s + 1 < NS:
                    exps(s + 1)
                pt_out(s)
            tp_out(1, None)

            def norm(n, done):
                for t in range(T):
                    act.wait_ge(*done(t))
                    if t == 0:
                        act.wait_ge(s_hid, FT if n >= 3 else 0) if n >= 3 else None
                    squares(n, t, xres[:, t, :])

            norm(2, lambda t: (s_res, 5 + t))
            tp_out(2, gcols[:, KD:2 * KD])
            for f in range(FT):
                act.wait_ge(s_mH, f + 1)
                if f >= 2:
                    act.wait_ge(s_hid, f - 1)
                act.activation(sg[f % 2], bank((2 * f) % 8), ACT.Silu).then_inc(s_silu, 1)
            norm(3, lambda t: (s_res, 13 + t))
            for t in range(T):
                act.wait_ge(s_x2, t + 1)
                squares(4, t, xres[:, t, :])
            tp_out(3, gcols[:, 2 * KD:3 * KD])

            for u, (name, j, t, eng) in enumerate(unitsG):
                if eng != "A":
                    continue
                act.wait_ge(s_mG, u + 1)
                b = bank(u % 8)
                if name == "q":
                    act.activation(qT[:, t, :], b, ACT.Copy, scale=float(GK) ** -0.5).then_inc(s_gA, 1)
                elif name == "z":
                    act.activation(gz[:, t, :], b, ACT.Identity, bias=bgate[:, t:t + 1]).then_inc(s_gA, 1)
                elif name == "r":
                    act.activation(gr[:, t, j * 512:(j + 1) * 512], b, ACT.Silu).then_inc(s_gA, 1)
                if name == "z" and t == GH - 1:
                    last_z = True
            for h in range(GH):
                act.wait_ge(s_gdv, 3 * h + 1)
                act.activation(tmp1, tmp1, ACT.Exp).then_inc(s_gac, 1)
                act.wait_ge(s_gac, 7 * h + 1)
                act.activation(tmp1, tmp1, ACT.Ln, bias=1.0).then_inc(s_gac, 1)
                act.wait_ge(s_gdv, 3 * h + 3)
                if h >= 1:
                    act.wait_ge(s_gpl, h)
                act.activation(Ex[0], D1, ACT.Exp, scale=1 / TAU).then_inc(s_gac, 1)
                act.activation(Ex[1], D1, ACT.Exp, scale=-1 / TAU).then_inc(s_gac, 1)
                act.activation(Ex[2], gg[:, h, :], ACT.Exp, scale=1 / TAU).then_inc(s_gac, 1)
                act.activation(Ex[3], D2, ACT.Exp, scale=1 / TAU).then_inc(s_gac, 1)
                act.activation(decay[:, h * NCH:(h + 1) * NCH].rearrange("p (c a) -> p c a", a=1),
                               gg[:, h, :].rearrange("p (c s) -> p c s", c=NCH)[:, :, CH - 1:CH],
                               ACT.Exp, scale=1 / TAU).then_inc(s_gac, 1)
            for h in range(GH):
                act.wait_ge(s_gU, 2 * h + 1)
                act.copy(kst[:, h, :, :], bank(2 * h).rearrange("p (t d) -> p t d", t=T)).then_inc(s_kst, 1)
            for t in range(T):
                for h in range(GH):
                    act.wait_ge(s_in, (2 * t + 2) * GH)
                    n = t * GH + h
                    wait(act, s_gss, n - 1)
                    act.activation(arena[:, 2048 + (n % 2) * GV:2048 + (n % 2 + 1) * GV], obank(h, t), ACT.Square,
                                   accum_out=ssg[:, n:n + 1]).then_inc(s_gss, 1)
            tp_out(4, None)
            for t in range(T):
                act.wait_ge(s_res, 21 + t)
                squares(5, t, xres[:, t, :])
            tp_out(5, None)

            for t in range(T):
                act.wait_ge(s_oh, t + 1)
                act.activation(rs8[:, t * 8:t * 8 + 8], lg[:, t, 0:GROUPS], ACT.Exp, bias=xw[:, t:t + 1],
                               accum_out=gwt[:, t:t + 1]).then_inc(s_rte, 1)
                act.activation(xw[:, 4 + t:5 + t], xw[:, 4 + t:5 + t], ACT.Exp).then_inc(s_rte, 1)
            act.wait_ge(s_pre, 1)
            act.copy(pre.rearrange("p t n -> p (t n)"), bank(1)[:, 0:T * EXPERTS]).then_inc(s_rte, 1)

            def xT_out(b, j):
                act.wait_ge(s_mx1, b + 1)
                wait(act, s_gu, b - 1)
                act.copy(xeT[j % 2][:, 0:4, :].rearrange("p k c -> p (k c)"), bank(0)).then_inc(s_mxA, 1)

            def silu(b, j):
                act.wait_ge(s_gu, b + 1)
                wait(act, s_mhid, b - 1)
                act.activation(msg[j % 2], bank(2 + j % 2)[:, 0:FF], ACT.Silu).then_inc(s_msl, 1)

            def y_out(b, j):
                act.wait_ge(s_my, b + 1)
                act.wait_ge(s_ys[j % 2], 16 * ((b - j % 2) // 2) if isinstance(b, int) else ys_wait(b, j)) if not isinstance(b, int) or b >= 2 else None
                act.copy(ye[j % 2][:, 0:512], bank(5)).then_inc(s_myA, 1)

            def ys_wait(b, j):
                return (b - j % 2) * 8

            def block_(base, j, first):
                silu(base + j, j)
                xT_out(base + j + 1, j + 1)
                if not first:
                    y_out(base + j - 1, j - 1)

            xT_out(0, 0)
            for j in range(E_SLOTS):
                block_(0, j, j == 0)
            with act.Fori(1, EXPERTS // E_SLOTS) as it:
                for j in range(E_SLOTS):
                    block_(it * E_SLOTS, j, False)
            y_out(EXPERTS - 1, E_SLOTS - 1)

            n_over = act.value_load(ovf_i[0:1, SPILL:SPILL + 1], min_val=0, max_val=SPILL)
            with act.If(n_over > 0):
                with act.Fori(0, SPILL) as i:
                    act.wait_ge(s_mx1, i + (EXPERTS + 2))
                    act.copy(xeT[0][:, 0:4, :].rearrange("p k c -> p (k c)"), bank(0)).then_inc(s_mxA, 1)
                    act.wait_ge(s_gu, i + (EXPERTS + 1))
                    act.activation(msg[0], bank(2)[:, 0:FF], ACT.Silu).then_inc(s_msl, 1)
                    act.wait_ge(s_my, i + (EXPERTS + 1))
                    act.wait_ge(s_ys[0], i * 16 + 8 * EXPERTS)
                    act.copy(ye[0][:, 0:512], bank(5)).then_inc(s_myA, 1)
            for t in range(T):
                act.wait_ge(s_fin, 0) if False else None
                act.wait_ge(s_x2, T + t + 1)
                squares(6, t, xres[:, t, :])

        @block.tensor
        def _(pe):
            def transposes(n, ready):
                pe.wait_ge(*ready)
                for k in range(KD):
                    for t in range(T):
                        last = pe.transpose(bank(k)[:, t * P:(t + 1) * P], xn[:, t, k * P:(k + 1) * P], ident[:, :])
                    last.then_inc(s_tp, 1)

            def hT_ready(n):
                pe.wait_ge(s_tpA, KD // 2 * (n + 1))
                pe.wait_ge(s_tpD, KD // 2 * (n + 1) + 1)

            pe.wait_ge(s_cst, 1)
            transposes(0, (s_xn, T))
            pe.wait_ge(s_xn, T + 1)
            pe.wait_ge(s_tpA, 1)
            for k in range(KD):
                last = pe.transpose(bank(0)[:, k * META:(k + 1) * META], metan[:, k * P:(k + 1) * P], ident[0:META, 0:META])
            last.then_inc(s_tp, 1)
            hT_ready(0)

            def free(units, u, sA, sD):
                if u >= 8:
                    v = u - 8
                    pe.wait_ge(sA if units[v][3] == "A" else sD, evacs(units, v))

            for u, (name, j, t, eng) in enumerate(unitsB):
                if t == 0:
                    tile_wait(pe, f"{name}{j}")
                w = tile_at[f"{name}{j}"]
                free(unitsB, u, s_eA, s_eD)
                b = bank(u % 8)
                if name == "f":
                    for tt in range(T + 1):
                        for k in range(KD):
                            lhs = hT[:, k, tt * P:(tt + 1) * P] if tt < T else hTm[:, k, :]
                            m = P if tt < T else META
                            last = pe.matmul(b[0:m, tt * HEADS:(tt + 1) * HEADS], lhs, w[:, k, :], start=(k == 0), stop=(k == KD - 1))
                else:
                    for k in range(KD):
                        lhs = hT[:, k, t * P:(t + 1) * P] if t < T else hTm[:, k, :]
                        m = P if t < T else META
                        last = pe.matmul(b[0:m, :], lhs, w[:, k, :], start=(k == 0), stop=(k == KD - 1))
                last.then_inc(s_mB, 1)

            def banks_free(units, sA, sD):
                pe.wait_ge(sA, sum(v[3] == "A" for v in units))
                pe.wait_ge(sD, sum(v[3] == "D" for v in units))

            banks_free(unitsB, s_eA, s_eD)
            pe.wait_ge(s_lf, 4)
            b = bank(0)
            H = HEADS
            for t in range(T):
                o = b[:, t * H:(t + 1) * H]
                pe.matmul(o, ones[0:META, :], zf[0:META, T * H:(T + 1) * H], start=True, stop=False)
                for j in range(t):
                    pe.matmul(o, ones[:, :], zf[:, j * H:(j + 1) * H], start=False, stop=False)
                pe.matmul(o, tri[:, :], zf[:, t * H:(t + 1) * H], start=False, stop=True)
            pe.matmul(b[0:META, T * H:(T + 1) * H], tri[0:META, 0:META], zf[0:META, T * H:(T + 1) * H],
                      start=True, stop=True).then_inc(s_cps, 1)
            pe.wait_ge(s_c, 1)

            NS = HEADS * T

            def qk(h, i):
                if i == 0:
                    pe.wait_ge(s_stage, h + 1)
                wait(pe, s_qkA, 3 * h + i)
                if i == 2:
                    last = pe.transpose(bank(QB)[0:HA, 0:META], kam[h % 2][0:META, :], ident[0:META, 0:META])
                else:
                    for t in range(T):
                        last = pe.transpose(bank(QB)[0:HA, t * P:(t + 1) * P], (qa, ka)[i][h % 2][:, t, :], ident[:, :])
                last.then_inc(s_qkt, 1)

            def scores(s):
                h, i = divmod(s, T)
                n = META + P * (i + 1)
                if i == 0:
                    pe.wait_ge(s_qkA, 3 * h + 3)
                if s >= 2:
                    pe.wait_ge(s_exp, s - 1)
                lhs = QT[h % 2][0:HA, i * P:(i + 1) * P]
                last = pe.matmul(sbank(s, 0, min(n, 512)), lhs, KT[h % 2][0:HA, 0:min(n, 512)], start=True, stop=True)
                if n > 512:
                    last = pe.matmul(sbank(s, 512, n), lhs, KT[h % 2][0:HA, 512:n], start=True, stop=True)
                last.then_inc(s_S, 1)

            def ptrans(s):
                i = s % T
                pe.wait_ge(s_exp, s + 1)
                if s:
                    pe.wait_ge(s_ptA, s)
                pe.transpose(ps[0:META, PTB:PTB + P], Pb[s % 3][:, 0:META], ident[:, :])
                for j in range(i + 1):
                    last = pe.transpose(ps[:, PTB + P * (j + 1):PTB + P * (j + 2)], Pb[s % 3][:, META + P * j:META + P * (j + 1)], ident[:, :])
                last.then_inc(s_T, 1)

            def pv(s):
                h, i = divmod(s, T)
                pe.wait_ge(s_ptA, s + 1)
                wait(pe, s_o, s - 1)
                o = bank(OB + s % 2)[:, 0:HD]
                pe.matmul(o, PT[s % 2][0:META, 0:P], mkv[0:META, D + h * HD:D + (h + 1) * HD], start=True, stop=False)
                for j in range(i + 1):
                    last = pe.matmul(o, PT[s % 2][:, P * (j + 1):P * (j + 2)],
                                     qkvg[:, j, 2 * D + h * HD:2 * D + (h + 1) * HD], start=False, stop=(j == i))
                last.then_inc(s_pv, 1)

            for i in range(3):
                qk(0, i)
            scores(0)
            for s in range(NS):
                if s % T < 3 and s // T + 1 < HEADS:
                    qk(s // T + 1, s % T)
                if s + 1 < NS:
                    scores(s + 1)
                ptrans(s)
                if s:
                    pv(s - 1)
            pv(NS - 1)

            transposes(1, (s_o, NS))
            hT_ready(1)

            def outproj(base, names, first):
                for j in range(2):
                    n = 0
                    for i, name in enumerate(names(j)):
                        w = tile_at[name]
                        tile_wait(pe, name)
                        for t in range(T):
                            for k in range(w.shape[1]):
                                src = first(n + k)
                                last = pe.matmul(bank(4 * j + t), src[:, t * P:(t + 1) * P], w[:, k, :],
                                                 start=(n + k == 0), stop=(i == len(names(j)) - 1 and k == w.shape[1] - 1))
                            last.then_inc(s_mO, 1)
                        n += w.shape[1]

            outproj(0, lambda j: [f"wo{j}"], lambda k: hT[:, k, :])
            transposes(2, (s_xn, 2 * T + 1))
            hT_ready(2)
            for f in range(FT):
                if f % 2 == 0:
                    tile_wait(pe, f"in{f // 2}")
                w = tile_at[f"in{f // 2}"]
                if f >= 4:
                    pe.wait_ge(s_hid, f - 3)
                for g in range(2):
                    c = g * 256 + (f % 2) * P
                    for k in range(KD):
                        last = pe.matmul(bank((2 * f + g) % 8), w[:, k, c:c + P], hT[:, k, :], start=(k == 0), stop=(k == KD - 1))
                last.then_inc(s_mH, 1)
            pe.wait_ge(s_hid, FT)
            outproj(1, lambda j: [f"out{j}{i}" for i in range(len(FK))], lambda k: actT[:, k, :])
            transposes(3, (s_xn, 3 * T + 1))
            hT_ready(3)

            for u, (name, j, t, eng) in enumerate(unitsG):
                if t == 0 and name != "z":
                    tile_wait(pe, f"g{name}{j}")
                free(unitsG, u, s_gA, s_gD)
                b = bank(u % 8)
                if name == "z":
                    pe.wait_ge(s_gD, 1)
                    last = pe.matmul(b, wgate[0:RANK, t * P:(t + 1) * P], alrT[0:RANK, :], start=True, stop=True)
                else:
                    w = tile_at[f"g{name}{j}"]
                    for k in range(KD):
                        if name == "a":
                            last = pe.matmul(b[0:RANK, :], w[:, k, :], hT[:, k, :], start=(k == 0), stop=(k == KD - 1))
                        elif name in "qk":
                            last = pe.matmul(b, w[:, k, t * P:(t + 1) * P], hT[:, k, :], start=(k == 0), stop=(k == KD - 1))
                        else:
                            last = pe.matmul(b, hT[:, k, t * P:(t + 1) * P], w[:, k, :], start=(k == 0), stop=(k == KD - 1))
                last.then_inc(s_mG, 1)
            banks_free(unitsG, s_gA, s_gD)
            for h in range(GH):
                pe.wait_ge(s_gpl, h + 1)
                for t in range(T):
                    last = pe.transpose(bank(2 * h)[:, t * P:(t + 1) * P], ksT[:, h, t * P:(t + 1) * P], ident[:, :])
                last.then_inc(s_gU, 1)
                for t in range(T):
                    last = pe.matmul(bank(2 * h + 1)[:, t * P:(t + 1) * P], kT[:, h, t * P:(t + 1) * P], qT[:, h, t * P:(t + 1) * P],
                                     start=True, stop=True)
                last.then_inc(s_gU, 1)
            pe.wait_ge(s_kst, GH)
            pe.wait_ge(s_atm, GH)
            for c in range(NCH):
                t, r = divmod(c, 2)
                rows = slice(r * CH, (r + 1) * CH)
                for h in range(GH):
                    if c < NCH - 1:
                        if c >= 2:
                            pe.wait_ge(s_S2, (c - 2) * GH + (h | 1) + 1)
                        pe.matmul(ubank(h, c), kst[rows, h, t, :],
                                  gv[rows, t, h * GV:(h + 1) * GV], start=True, stop=True).then_inc(s_U, 1)
                    o = obank(h, t)
                    if r == 0:
                        if t >= 2:
                            pe.wait_ge(s_go, (t - 2) * GH + (h | 1) + 1)
                        last = pe.matmul(o, atm[:, h, t, :], gv[:, t, h * GV:(h + 1) * GV], start=(h % 2 == 0), stop=False,
                                         skip_group_check=True)
                    if c:
                        pe.wait_ge(s_S2, (c - 1) * GH + h + 1)
                        last = pe.matmul(o[rows, :], qiT[:, h, c * CH:(c + 1) * CH], St[:, h, c % 2, :],
                                         start=False, stop=(r == 1), skip_group_check=True)
                    last.then_inc(s_in, 1)
            transposes(4, (s_go, GH * T))
            hT_ready(4)
            outproj(2, lambda j: [f"gwo{j}"], lambda k: hT[:, k, :])
            transposes(5, (s_hnrow, T))
            hT_ready(5)
            tile_wait(pe, "rt")
            w = tile_at["rt"]
            for t in range(T):
                for k in range(KD):
                    last = pe.matmul(bank(0)[:, t * NR:(t + 1) * NR], hT[:, k, t * P:(t + 1) * P], w[:, k, :], start=(k == 0), stop=(k == KD - 1))
            last.then_inc(s_rt, 1)
            pe.wait_ge(s_oh, T + 1)
            for t in range(T):
                o = bank(1)[:, t * EXPERTS:(t + 1) * EXPERTS]
                for j in range(t):
                    pe.matmul(o, ones[:, :], oh[2][:, j, :], start=(j == 0), stop=False)
                pe.matmul(o, strict[:, :], oh[2][:, t, :], start=(t == 0), stop=True)
            for t in range(T):
                last = pe.matmul(bank(1)[:, T * EXPERTS:(T + 1) * EXPERTS], ones[:, :], oh[2][:, t, :], start=(t == 0), stop=(t == T - 1))
            last.then_inc(s_pre, 1)

            def A(b, j, buf=None):
                pe.wait_ge(s_xe[j % 4], xe_wait(b, j))
                wait(pe, s_mxA, b)
                wait(pe, s_mxD, b)
                v = xe[j % 4].rearrange("p (m k) -> p k m", k=KD)
                for k in range(KD):
                    last = pe.transpose(ps[:, k * C:(k + 1) * C], v[0:C, k, :], ident[0:C, 0:C])
                last.then_inc(s_mx1, 1)

            def xe_wait(b, j):
                return 16 * (b // 4 + 1) if isinstance(b, int) else (b - j % 4) * 4 + 16

            def B(b, j, n_w):
                w1, w3, _ = eslot(j % 4)
                pe.wait_ge(s_ew[j % 4], n_w)
                pe.wait_ge(s_mxA, b + 1)
                pe.wait_ge(s_mxD, b + 1)
                wait(pe, s_mhid, b - 1)
                g = bank(2 + j % 2)
                for k in range(KD):
                    pe.matmul(g[0:C, 0:FF], xeT[j % 2][:, k, :], w1[:, k, :], start=(k == 0), stop=(k == KD - 1))
                for k in range(KD):
                    last = pe.matmul(g[0:C, FF:2 * FF], xeT[j % 2][:, k, :], w3[:, k, :], start=(k == 0), stop=(k == KD - 1))
                last.then_inc(s_gu, 1)

            def Ct(b, j):
                pe.wait_ge(s_mhid, b + 1)
                wait(pe, s_mhTe, b)
                v = mhid[j % 2].rearrange("p (m k) -> p k m", k=KF)
                for k in range(KF):
                    last = pe.transpose(bank(4)[:, k * C:(k + 1) * C], v[0:C, k, :], ident[0:C, 0:C])
                last.then_inc(s_mhT, 1)

            def Dy(b, j):
                w2 = eslot(j % 4)[2]
                pe.wait_ge(s_mhTe, b + 1)
                wait(pe, s_myA, b)
                wait(pe, s_myD, b)
                for n in range(2):
                    for k in range(KF):
                        last = pe.matmul(bank(5 + n)[0:C, :], mhT[j % 2][:, k, :], w2[:, k, n * 512:(n + 1) * 512],
                                         start=(k == 0), stop=(k == KF - 1))
                last.then_inc(s_my, 1)

            def block_(base, j, first, n_w):
                B(base + j, j, n_w)
                A(base + j + 1, j + 1) if j < 3 else A_next(base, j)
                if not first:
                    Dy(base + j - 1, j - 1)
                Ct(base + j, j)

            def A_next(base, j):
                b = base + 4
                pe.wait_ge(s_xe[0], 16 * (b // 4 + 1) if isinstance(b, int) else b * 4 + 16)
                wait(pe, s_mxA, b)
                wait(pe, s_mxD, b)
                v = xe[0].rearrange("p (m k) -> p k m", k=KD)
                for k in range(KD):
                    last = pe.transpose(ps[:, k * C:(k + 1) * C], v[0:C, k, :], ident[0:C, 0:C])
                last.then_inc(s_mx1, 1)

            pe.wait_ge(s_tabs, 1)
            A(0, 0)
            for j in range(E_SLOTS):
                block_(0, j, j == 0, 48)
            with pe.Fori(1, EXPERTS // E_SLOTS) as it:
                for j in range(E_SLOTS):
                    block_(it * E_SLOTS, j, False, it * 48 + 48)
            Dy(EXPERTS - 1, E_SLOTS - 1)
            n_over = pe.value_load(ovf_i[0:1, SPILL:SPILL + 1], min_val=0, max_val=SPILL)
            with pe.If(n_over > 0):
                with pe.Fori(0, SPILL) as i:
                    w1, w3, w2 = eslot(0)
                    pe.wait_ge(s_xe[0], i * 16 + 4 * (EXPERTS + 4) + 16)
                    pe.wait_ge(s_mxA, i + (EXPERTS + 1))
                    pe.wait_ge(s_mxD, i + (EXPERTS + 1))
                    v = xe[0].rearrange("p (m k) -> p k m", k=KD)
                    for k in range(KD):
                        last = pe.transpose(ps[:, k * C:(k + 1) * C], v[0:C, k, :], ident[0:C, 0:C])
                    last.then_inc(s_mx1, 1)
                    pe.wait_ge(s_ew[0], i * 48 + 48 * (EXPERTS // 4 + 1))
                    pe.wait_ge(s_mxA, i + (EXPERTS + 2))
                    pe.wait_ge(s_mxD, i + (EXPERTS + 2))
                    pe.wait_ge(s_mhid, i + EXPERTS)
                    g = bank(2)
                    for k in range(KD):
                        pe.matmul(g[0:C, 0:FF], xeT[0][:, k, :], w1[:, k, :], start=(k == 0), stop=(k == KD - 1))
                    for k in range(KD):
                        last = pe.matmul(g[0:C, FF:2 * FF], xeT[0][:, k, :], w3[:, k, :], start=(k == 0), stop=(k == KD - 1))
                    last.then_inc(s_gu, 1)
                    pe.wait_ge(s_mhid, i + (EXPERTS + 1))
                    v = mhid[0].rearrange("p (m k) -> p k m", k=KF)
                    for k in range(KF):
                        last = pe.transpose(bank(4)[:, k * C:(k + 1) * C], v[0:C, k, :], ident[0:C, 0:C])
                    last.then_inc(s_mhT, 1)
                    pe.wait_ge(s_mhTe, i + (EXPERTS + 1))
                    pe.wait_ge(s_myA, i + EXPERTS)
                    pe.wait_ge(s_myD, i + EXPERTS)
                    for n in range(2):
                        for k in range(KF):
                            last = pe.matmul(bank(5 + n)[0:C, :], mhT[0][:, k, :], w2[:, k, n * 512:(n + 1) * 512],
                                             start=(k == 0), stop=(k == KF - 1))
                    last.then_inc(s_my, 1)

        @block.vector
        def _(dve):
            me = Count(dve, s_dve)

            roots = Count(dve, s_ms)

            def rms_scale(dst, src, n):
                roots.inc(dve.tensor_scalar(dst, src, 1.0 / n, EPS, ALU.mult, ALU.add))
                dve.wait_ge(s_pw, roots.n)

            def tp_out(n, gain):
                for k in range(1, KD, 2):
                    dve.wait_ge(s_tp, KD * n + (n > 0) + k + 1)
                    if gain is not None:
                        dve.tensor_scalar(hT[:, k, :], bank(k), gain[:, k:k + 1], None, ALU.mult).then_inc(s_tpD, 1)
                    else:
                        dve.tensor_copy(hT[:, k, :], bank(k)).then_inc(s_tpD, 1)

            def normed(n_ss):
                for t in range(T):
                    dve.wait_ge(s_ss, n_ss + t + 1)
                    rms_scale(rstd[:, t:t + 1], ss[:, t:t + 1], D)
                    dve.tensor_scalar(xn[:, t, :], xres[:, t, :], rstd[:, t:t + 1], None, ALU.mult).then_inc(s_xn, 1)

            normed(0)
            dve.wait_ge(s_ss, T + 1)
            rms_scale(rstd[0:META, T:T + 1], ss[0:META, T:T + 1], D)
            dve.tensor_scalar(metan, metax, rstd[0:META, T:T + 1], None, ALU.mult).then_inc(s_xn, 1)
            dve.wait_ge(s_small, 16 * 9)
            tp_out(0, gcols[:, 0:KD])
            dve.wait_ge(s_tp, KD + 1)
            dve.tensor_tensor(hTm, bank(0)[:, 0:KD * META].rearrange("p (k s) -> p k s", k=KD),
                              gcols[:, 0:KD].unsqueeze(2).to_broadcast([P, KD, META]), ALU.mult).then_inc(s_tpD, 1)
            H = HEADS
            me.link(dve.memset(zf[:, :], 0.0))
            for u, (name, j, t, eng) in enumerate(unitsB):
                if eng == "D":
                    dve.wait_ge(s_mB, u + 1)
                    b = bank(u % 8)
                    if name == "f":
                        dve.tensor_tensor(zf[0:META, T * H:], b[0:META, T * H:(T + 1) * H], bf[0:META, :], ALU.add)
                        dve.tensor_tensor(zf[:, 0:T * H].rearrange("p (t h) -> p t h", t=T), b[:, 0:T * H].rearrange("p (t h) -> p t h", t=T),
                                          bf[:, :].unsqueeze(1).to_broadcast([P, T, H]), ALU.add).then_inc(s_eD, 1)
                        dve.wait_ge(s_eD, evacs(unitsB, u))
                        dve.scalar_tensor_tensor(out=zt[:, :], in0=zf[:, :], scalar=-1.0, in1=zf[:, :], op0=ALU.mult, op1=ALU.min).then_inc(s_lf, 1)
                        for n in range(9):
                            rows = P if n < 8 else META
                            dve.wait_ge(s_sqh, n + 1)
                            dve.tensor_reduce(ssq[0:rows, n * H:(n + 1) * H], scr[n % 2][0:rows, :].rearrange("p (h d) -> p h d", h=H),
                                              AX, ALU.add).then_inc(s_rs, 1)
                        continue
                    o = {"q": 0, "k": D, "v": 2 * D}[name] + j * 512
                    if t == T:
                        dve.tensor_copy(mkv[0:META, o - D:o - D + 512], b[0:META, :]).then_inc(s_eD, 1)
                    else:
                        dve.tensor_copy(qkvg[:, t, o:o + 512], b).then_inc(s_eD, 1)
            dve.wait_ge(s_rs, 9)
            rms_scale(rsq[:, 0:8 * H], ssq[:, 0:8 * H], HD)
            rms_scale(rsq[0:META, 8 * H:], ssq[0:META, 8 * H:], HD)
            me.link(dve.memset(qgain[HD:P, :], 1.0))
            me.link(dve.memset(kgain[HD:P, :], 1.0))
            me.link(dve.tensor_scalar(qgain[0:HD, :], qgain[0:HD, :], float(HD) ** -0.5, None, ALU.mult))
            dve.wait_ge(s_lf, 3)
            dve.scalar_tensor_tensor(out=zf[:, :], in0=zf[:, :], scalar=0.0, in1=zt[:, :], op0=ALU.min, op1=ALU.subtract).then_inc(s_lf, 1)
            dve.wait_ge(s_cps, 1)
            n = T * H
            me.link(dve.memset(cc[:, :], 0.0))
            me.link(dve.tensor_copy(cc[:, 0:n], bank(0)[:, 0:n]))
            me.link(dve.tensor_copy(cc[0:META, n:], bank(0)[0:META, n:n + H]))
            dve.tensor_scalar(ncc[:, :], cc[:, :], -1.0, None, ALU.mult).then_inc(s_c, 1)

            NS = HEADS * T
            dve.wait_ge(s_cst, 1)

            def rowmax(s):
                i = s % T
                n = META + P * (i + 1)
                dve.wait_ge(s_S, s + 1)
                me.link(dve.tensor_tensor(sbank(s, n - P, n), sbank(s, n - P, n), amask[:, :], ALU.add))
                me.link(dve.tensor_reduce(mxn[:, s:s + 1], sbank(s, 0, n), AX, ALU.max))
                dve.tensor_scalar(mxn[:, 64 + s:65 + s], mxn[:, s:s + 1], -1.0, None, ALU.mult).then_inc(s_mx, 1)

            def attn_out(s):
                h, i = divmod(s, T)
                me.link(dve.reciprocal(rinv[:, s:s + 1], rsum[:, s:s + 1]))
                dve.wait_ge(s_pv, s + 1)
                dve.scalar_tensor_tensor(out=xn[:, i, h * HD:(h + 1) * HD], in0=bank(OB + s % 2)[:, 0:HD],
                                         scalar=rinv[:, s:s + 1], in1=qkvg[:, i, 3 * D + h * HD:3 * D + (h + 1) * HD],
                                         op0=ALU.mult, op1=ALU.mult).then_inc(s_o, 1)

            rowmax(0)
            for s in range(NS):
                if s + 1 < NS:
                    rowmax(s + 1)
                if s:
                    attn_out(s - 1)
            attn_out(NS - 1)
            tp_out(1, None)

            def residual(base, n, last):
                for j in range(2):
                    for t in range(T):
                        dve.wait_ge(s_mO, base + (j + 1) * n * 4 - 4 + t + 1)
                        d = xres[:, t, j * 512:(j + 1) * 512]
                        dve.tensor_tensor(d, d, bank(4 * j + t), ALU.add).then_inc(s_res, 1)

            residual(0, 1, None)
            dve.wait_ge(s_res, 8)
            normed(5)
            tp_out(2, gcols[:, KD:2 * KD])
            for f in range(FT):
                dve.wait_ge(s_silu, f + 1)
                dve.tensor_tensor(actT[:, f, :], sg[f % 2], bank((2 * f + 1) % 8), ALU.mult).then_inc(s_hid, 1)
            residual(8, len(FK), None)
            dve.wait_ge(s_row, 16)
            dve.wait_ge(s_res, 16)
            for t in range(T):
                dve.wait_ge(s_ss, 9 + t + 1)
                rms_scale(rstd[:, t:t + 1], ss[:, t:t + 1], D)
                dve.scalar_tensor_tensor(out=xres[:, t, :], in0=xres[:, t, :], scalar=rstd[:, t:t + 1], in1=gainrow[:, :],
                                         op0=ALU.mult, op1=ALU.mult).then_inc(s_x2, 1)
            normed(13)
            tp_out(3, gcols[:, 2 * KD:3 * KD])

            for u, (name, j, t, eng) in enumerate(unitsG):
                if eng != "D":
                    continue
                dve.wait_ge(s_mG, u + 1)
                b = bank(u % 8)
                if name == "a":
                    dve.tensor_copy(alrT[0:RANK, :], b[0:RANK, :]).then_inc(s_gD, 1)
                elif name == "k":
                    dve.tensor_copy(kT[:, t, :], b).then_inc(s_gD, 1)
                else:
                    dve.tensor_copy(gv[:, t, j * 512:(j + 1) * 512], b).then_inc(s_gD, 1)
            zl = max(u for u, v in enumerate(unitsG) if v[0] == "z")
            dve.wait_ge(s_gA, evacs(unitsG, zl))
            dve.wait_ge(s_reset, 1)
            for h in range(GH):
                if h:
                    dve.wait_ge(s_gac, 7 * h)
                dve.scalar_tensor_tensor(out=tmp1, in0=gz[:, h, :], scalar=-1.0, in1=gz[:, h, :], op0=ALU.mult, op1=ALU.min).then_inc(s_gdv, 1)
                dve.wait_ge(s_gac, 7 * h + 2)
                me.link(dve.scalar_tensor_tensor(out=gz[:, h, :], in0=gz[:, h, :], scalar=0.0, in1=tmp1, op0=ALU.min, op1=ALU.subtract))
                me.link(dve.tensor_tensor_scan(gg[:, h, :], reset[:, :], gz[:, h, :], 0.0, ALU.mult, ALU.add))
                g3 = gg[:, h, :].rearrange("p (c s) -> p c s", c=NCH)
                dve.tensor_tensor(D1.rearrange("p (c s) -> p c s", c=NCH), g3, g3[:, :, CH // 2:CH // 2 + 1].to_broadcast([P, NCH, CH]),
                                  ALU.subtract).then_inc(s_gdv, 1)
                dve.tensor_tensor(D2.rearrange("p (c s) -> p c s", c=NCH), g3[:, :, CH - 1:CH].to_broadcast([P, NCH, CH]), g3,
                                  ALU.subtract).then_inc(s_gdv, 1)
            dve.wait_ge(s_gpl, GH)
            for h in range(GH):
                dve.wait_ge(s_gU, 2 * h + 2)
                dve.tensor_tensor(atm[:, h, :, :], bank(2 * h + 1).rearrange("p (t s) -> p t s", t=T),
                                  gmask[:, :].unsqueeze(1).to_broadcast([P, T, P]), ALU.mult).then_inc(s_atm, 1)

            def gla_out(t):
                dve.wait_ge(s_gss, (t + 1) * GH)
                rms_scale(ssg[:, 32 + t * GH:32 + (t + 1) * GH], ssg[:, t * GH:(t + 1) * GH], GV)
                for h in range(GH):
                    n = t * GH + h
                    if n == 0:
                        dve.wait_ge(s_gr, T)
                    dve.scalar_tensor_tensor(out=xn[:, t, h * GV:(h + 1) * GV], in0=obank(h, t),
                                             scalar=ssg[:, 32 + n:33 + n], in1=gr[:, t, h * GV:(h + 1) * GV],
                                             op0=ALU.mult, op1=ALU.mult).then_inc(s_go, 1)

            for c in range(NCH):
                if c < NCH - 1:
                    for h in range(GH):
                        dve.wait_ge(s_U, c * GH + (h | 1) + 1)
                        if c >= 1:
                            dve.wait_ge(s_in, (c - 1) * GH + h + 1)
                            dve.wait_ge(s_S2, (c - 1) * GH + h + 1)
                        u = ubank(h, c)
                        if c == 0:
                            dve.tensor_copy(St[:, h, 1, :], u).then_inc(s_S2, 1)
                        else:
                            dve.scalar_tensor_tensor(out=St[:, h, (c + 1) % 2, :], in0=St[:, h, c % 2, :],
                                                     scalar=decay[:, h * NCH + c:h * NCH + c + 1], in1=u,
                                                     op0=ALU.mult, op1=ALU.add).then_inc(s_S2, 1)
                if c >= 3 and c % 2 == 1:
                    gla_out(c // 2 - 1)
            gla_out(T - 1)
            tp_out(4, None)
            residual(MO_FFN, 1, None)
            dve.wait_ge(s_res, 24)
            dve.wait_ge(s_row2, 16)
            for t in range(T):
                dve.wait_ge(s_ss, 17 + t + 1)
                rms_scale(rstd[:, t:t + 1], ss[:, t:t + 1], D)
                dve.scalar_tensor_tensor(out=xn[:, t, :], in0=xres[:, t, :], scalar=rstd[:, t:t + 1], in1=gainrow[:, :],
                                         op0=ALU.mult, op1=ALU.mult).then_inc(s_hnrow, 1)
            tp_out(5, None)

            dve.wait_ge(s_rt, 1)
            me.link(dve.tensor_copy(lg.rearrange("p t n -> p (t n)"), bank(0)[:, 0:T * NR]))
            dve.wait_ge(s_cst, 2)
            for t in range(T):
                g8, e64 = lg[:, t, 0:GROUPS], lg[:, t, GROUPS:NR]
                me.link(dve.max(gm8[:, t, :], g8))
                me.link(dve.max_index(gi_u[:, t * 8:t * 8 + 8], gm8[:, t, :], g8))
                me.link(dve.tensor_copy(gsel[:, t:t + 1], gi_u[:, t * 8:t * 8 + 1]))
                me.link(dve.tensor_scalar(rtm, iog, gsel[:, t:t + 1], None, ALU.is_equal))
                me.link(dve.tensor_tensor(em[:, t, :], e64, rtm, ALU.mult))
                me.link(dve.tensor_scalar(rtm, rtm, -1.0, -NEG, ALU.add, ALU.mult))
                me.link(dve.tensor_tensor(em[:, t, :], em[:, t, :], rtm, ALU.add))
                me.link(dve.max(em8[:, t, :], em[:, t, :]))
                me.link(dve.max_index(ei_u[:, t * 8:t * 8 + 8], em8[:, t, :], em[:, t, :]))
                me.link(dve.tensor_copy(esel[:, t, :], ei_u[:, t * 8:t * 8 + 2]))
                for k in range(2):
                    me.link(dve.tensor_scalar(oh[k][:, t, :], ioe, esel[:, t, k:k + 1], None, ALU.is_equal))
                me.link(dve.tensor_tensor(oh[2][:, t, :], oh[0][:, t, :], oh[1][:, t, :], ALU.add))
                me.link(dve.tensor_scalar(xw[:, t:t + 1], gm8[:, t, 0:1], -1.0, None, ALU.mult))
                dve.tensor_tensor(xw[:, 4 + t:5 + t], em8[:, t, 1:2], em8[:, t, 0:1], ALU.subtract).then_inc(s_oh, 1)
            me.link(dve.memset(one64, 1.0))
            dve.tensor_copy(rtm, one64).then_inc(s_oh, 1)
            dve.wait_ge(s_rte, 2 * T + 1)
            x1 = xw[:, 4:8]
            gt = gates.rearrange("p t k -> p k t")
            me.link(dve.tensor_scalar(gsel, x1, 1.0, None, ALU.add))
            me.link(dve.tensor_tensor(gsel, gsel, gwt, ALU.mult))
            me.link(dve.reciprocal(gt[:, 0, :], gsel))
            me.link(dve.tensor_tensor(gt[:, 1, :], gt[:, 0, :], x1, ALU.mult))
            me.link(dve.tensor_copy(cnt, bank(1)[:, T * EXPERTS:(T + 1) * EXPERTS]))
            me.link(dve.tensor_scalar(ob, cnt, C + 0.5, None, ALU.is_ge))
            for q in range(2, QS):
                me.link(dve.tensor_scalar(rtm, cnt, C * q + 0.5, None, ALU.is_ge))
                me.link(dve.tensor_tensor(ob, ob, rtm, ALU.add))
            me.link(dve.tensor_tensor_scan(obe, one64, ob, 0.0, ALU.mult, ALU.add))
            me.link(dve.tensor_tensor(obs, obe, ob, ALU.subtract))
            for t in range(T):
                for k in range(2):
                    me.link(dve.tensor_tensor(rtm, oh[k][:, t, :], pre[:, t, :], ALU.mult))
                    me.link(dve.tensor_reduce(rk[:, t, k:k + 1], rtm, AX, ALU.add))
                    me.link(dve.tensor_tensor(rtm, oh[k][:, t, :], obs, ALU.mult))
                    me.link(dve.tensor_reduce(stt[:, t, k:k + 1], rtm, AX, ALU.add))
            me.link(dve.tensor_scalar(q1, rk, C - 0.5, None, ALU.is_ge))
            me.link(dve.tensor_copy(qq, q1))
            for q in range(2, QS):
                me.link(dve.tensor_scalar(bl, rk, C * q - 0.5, None, ALU.is_ge))
                me.link(dve.tensor_tensor(qq, qq, bl, ALU.add))
            me.link(dve.tensor_tensor(bl, stt, qq, ALU.add))
            me.link(dve.tensor_scalar(bl, bl, EXPERTS - 1.0, None, ALU.add))
            me.link(dve.tensor_tensor(bl, bl, esel, ALU.subtract))
            me.link(dve.tensor_tensor(bl, bl, q1, ALU.mult))
            me.link(dve.tensor_tensor(bl, bl, esel, ALU.add))
            me.link(dve.tensor_scalar(qq, qq, -float(C), None, ALU.mult))
            me.link(dve.tensor_tensor(qq, qq, rk, ALU.add))
            me.link(dve.tensor_scalar(qq, qq, float(NB), None, ALU.mult))
            me.link(dve.tensor_tensor(qq, qq, bl, ALU.add))
            dve.tensor_copy(slot_i[:, :], qq.rearrange("p t k -> p (t k)")).then_inc(s_idx, 1)
            for i in range(SPILL):
                me.link(dve.tensor_scalar(rtm, obs, i + 0.5, None, ALU.is_lt))
                me.link(dve.tensor_scalar(osel, obe, i + 0.5, None, ALU.is_ge))
                me.link(dve.tensor_tensor(rtm, rtm, osel, ALU.mult))
                me.link(dve.tensor_tensor(rtm, rtm, ioe, ALU.mult))
                me.link(dve.tensor_reduce(ovf[:, i:i + 1], rtm, AX, ALU.add))
            me.link(dve.tensor_copy(ovf[:, SPILL:SPILL + 1], obe[:, EXPERTS - 1:EXPERTS]))
            me.link(dve.tensor_copy(ovf_i[:, :], ovf))
            dve.wait_ge(s_tab, 16)
            me.link(dve.tensor_copy(ttf[:, 0:NB], dtab[:, :]))
            me.link(dve.tensor_scalar(ttf[:, NB:2 * NB], ttf[:, 0:NB], SEQ - 0.5, -float(SEQ), ALU.is_ge, ALU.mult))
            me.link(dve.tensor_tensor(ttf[:, 0:NB], ttf[:, 0:NB], ttf[:, NB:2 * NB], ALU.add))
            dve.tensor_copy(ttab[:, :], ttf[:, 0:NB]).then_inc(s_tabs, 1)

            def hid(b, j):
                dve.wait_ge(s_msl, b + 1)
                wait(dve, s_mhT, b - 1)
                dve.tensor_tensor(mhid[j % 2], msg[j % 2], bank(2 + j % 2)[:, FF:2 * FF], ALU.mult).then_inc(s_mhid, 1)

            def xT_out(b, j):
                dve.wait_ge(s_mx1, b + 1)
                wait(dve, s_gu, b - 1)
                dve.tensor_copy(xeT[j % 2][:, 4:8, :].rearrange("p k c -> p (k c)"), bank(1)).then_inc(s_mxD, 1)

            def y_out(b, j):
                dve.wait_ge(s_my, b + 1)
                if not isinstance(b, int) or b >= 2:
                    dve.wait_ge(s_ys[j % 2], (b - j % 2) * 8)
                dve.tensor_copy(ye[j % 2][:, 512:1024], bank(6)).then_inc(s_myD, 1)

            def hT_out(b, j):
                dve.wait_ge(s_mhT, b + 1)
                wait(dve, s_my, b - 1)
                dve.tensor_copy(mhT[j % 2].rearrange("p k c -> p (k c)"), bank(4)[:, 0:KF * C]).then_inc(s_mhTe, 1)

            def block_(base, j, first):
                hid(base + j, j)
                xT_out(base + j + 1, j + 1)
                if not first:
                    y_out(base + j - 1, j - 1)
                hT_out(base + j, j)

            xT_out(0, 0)
            for j in range(E_SLOTS):
                block_(0, j, j == 0)
            with dve.Fori(1, EXPERTS // E_SLOTS) as it:
                for j in range(E_SLOTS):
                    block_(it * E_SLOTS, j, False)
            y_out(EXPERTS - 1, E_SLOTS - 1)
            n_over = dve.value_load(ovf_i[0:1, SPILL:SPILL + 1], min_val=0, max_val=SPILL)
            with dve.If(n_over > 0):
                with dve.Fori(0, SPILL) as i:
                    dve.wait_ge(s_mx1, i + (EXPERTS + 2))
                    dve.tensor_copy(xeT[0][:, 4:8, :].rearrange("p k c -> p (k c)"), bank(1)).then_inc(s_mxD, 1)
                    dve.wait_ge(s_msl, i + (EXPERTS + 1))
                    dve.tensor_tensor(mhid[0], msg[0], bank(2)[:, FF:2 * FF], ALU.mult).then_inc(s_mhid, 1)
                    dve.wait_ge(s_mhT, i + (EXPERTS + 1))
                    dve.tensor_copy(mhT[0].rearrange("p k c -> p (k c)"), bank(4)[:, 0:KF * C]).then_inc(s_mhTe, 1)
                    dve.wait_ge(s_my, i + (EXPERTS + 1))
                    dve.wait_ge(s_ys[0], i * 16 + 8 * EXPERTS)
                    dve.tensor_copy(ye[0][:, 512:1024], bank(6)).then_inc(s_myD, 1)

            dve.wait_ge(s_row2, 32)
            dve.wait_ge(s_yl, 16 * 2 * T)
            yv = big[:, 0:2 * T * D].rearrange("p (k t d) -> p k t d", k=2, t=T)
            for t in range(T):
                me.link(dve.scalar_tensor_tensor(out=xres[:, t, :], in0=yv[:, 0, t, :], scalar=gates[:, t, 0:1], in1=xres[:, t, :],
                                                 op0=ALU.mult, op1=ALU.add))
                dve.scalar_tensor_tensor(out=xres[:, t, :], in0=yv[:, 1, t, :], scalar=gates[:, t, 1:2], in1=xres[:, t, :],
                                         op0=ALU.mult, op1=ALU.add).then_inc(s_x2, 1)
            dve.wait_ge(s_x2, 2 * T)
            for t in range(T):
                dve.wait_ge(s_ss, 21 + t + 1)
                rms_scale(rstd[:, t:t + 1], ss[:, t:t + 1], D)
                dve.scalar_tensor_tensor(out=xres[:, t, :], in0=xres[:, t, :], scalar=rstd[:, t:t + 1], in1=gainrow[:, :],
                                         op0=ALU.mult, op1=ALU.mult).then_inc(s_fin, 1)

        @block.gpsimd
        def _(pool):
            me = Count(pool, s_pool)
            me.inc(pool.memset(ident[:, :], 0.0))
            me.inc(pool.memset(tri[:, :], 1.0))
            me.inc(pool.memset(strict[:, :], 1.0))
            me.inc(pool.memset(ones[:, :], 1.0))
            me.inc(pool.memset(amask[:, :], 0.0))
            me.inc(pool.memset(gmask[:, :], 1.0))
            me.inc(pool.memset(half[:, :], -0.5))
            me.wait()
            one_row = [[1, P]]
            me.inc(pool.affine_select(out=ident[:, :], in_=ident[:, :], compare_op=ALU.not_equal, fill=1.0, base=0,
                                      pattern=[[-1, P]], channel_multiplier=1))
            me.inc(pool.affine_select(out=tri[:, :], in_=tri[:, :], compare_op=ALU.is_ge, fill=0.0, base=0,
                                      pattern=one_row, channel_multiplier=-1))
            me.inc(pool.affine_select(out=strict[:, :], in_=strict[:, :], compare_op=ALU.is_gt, fill=0.0, base=0,
                                      pattern=one_row, channel_multiplier=-1))
            me.inc(pool.affine_select(out=amask[:, :], in_=amask[:, :], compare_op=ALU.is_ge, fill=NEG, base=0,
                                      pattern=[[-1, P]], channel_multiplier=1))
            me.inc(pool.affine_select(out=gmask[:, :], in_=gmask[:, :], compare_op=ALU.is_ge, fill=0.0, base=0,
                                      pattern=one_row, channel_multiplier=-1))
            me.wait()
            me.inc(pool.memset(gmask[0:CH, CH:P], 0.0))
            me.wait()
            pool.memset(ss[:, 7:8], 0.0).then_inc(s_cst, 1)

            rooted = Count(pool, s_pw)

            def root(v):
                pool.wait_ge(s_ms, rooted.n + 1)
                rooted.inc(pool.tensor_tensor(v, v, half[0:v.shape[0], 0:v.shape[1]], ALU.pow))

            def row_roots():
                for t in range(T):
                    root(rstd[:, t:t + 1])

            row_roots()
            root(rstd[0:META, T:T + 1])

            H = HEADS
            pool.wait_ge(s_rs, 9)
            for b in range(2):
                me.inc(pool.memset(qa[b][:, :, HD:HD + 1], 1.0))
                me.inc(pool.memset(ka[b][:, :, HD + 1:HA], 1.0))
                me.inc(pool.memset(kam[b][0:META, HD + 1:HA], 1.0))
            root(rsq[:, 0:8 * H])
            root(rsq[0:META, 8 * H:])
            pool.wait_ge(s_c, 1)
            rq = rsq[:, 0:4 * H].rearrange("p (t h) -> p t h", t=T)
            rk_ = rsq[:, 4 * H:8 * H].rearrange("p (t h) -> p t h", t=T)
            c3 = cc[:, 0:T * H].rearrange("p (t h) -> p t h", t=T)
            n3 = ncc[:, 0:T * H].rearrange("p (t h) -> p t h", t=T)
            for h in range(H):
                if h >= 2:
                    pool.wait_ge(s_qkt, 3 * (h - 1))
                b = h % 2
                pool.tensor_tensor(qa[b][:, :, 0:HD], qkvg[:, :, h * HD:(h + 1) * HD],
                                   rq[:, :, h:h + 1].to_broadcast([P, T, HD]), ALU.mult)
                pool.tensor_copy(qa[b][:, :, HD + 1:HA], c3[:, :, h:h + 1])
                pool.tensor_tensor(ka[b][:, :, 0:HD], qkvg[:, :, D + h * HD:D + (h + 1) * HD],
                                   rk_[:, :, h:h + 1].to_broadcast([P, T, HD]), ALU.mult)
                pool.tensor_copy(ka[b][:, :, HD:HD + 1], n3[:, :, h:h + 1])
                pool.tensor_tensor(kam[b][0:META, 0:HD], mkv[0:META, h * HD:(h + 1) * HD],
                                   rsq[0:META, 8 * H + h:8 * H + h + 1].to_broadcast([META, HD]), ALU.mult)
                pool.tensor_copy(kam[b][0:META, HD:HD + 1], ncc[0:META, T * H + h:T * H + h + 1]).then_inc(s_stage, 1)

            for _ in range(3):
                row_roots()

            pool.wait_ge(s_tp, KD * 4 + 1)
            me.link(pool.memset(reset[:, :], 1.0))
            pool.memset(reset[:, :].rearrange("p (c s) -> p c s", c=NCH)[:, :, 0:1], 0.0).then_inc(s_reset, 1)

            kl = max(u for u, v in enumerate(unitsG) if v[0] == "k")
            pool.wait_ge(s_gD, evacs(unitsG, kl))
            pool.wait_ge(s_mG, len(unitsG))
            for h in range(GH):
                pool.wait_ge(s_gac, 7 * h + 7)
                me.inc(pool.tensor_tensor(qiT[:, h, :], qT[:, h, :], Ex[2], ALU.mult))
                me.inc(pool.tensor_tensor(ksT[:, h, :], kT[:, h, :], Ex[3], ALU.mult))
                me.wait()
                pool.tensor_tensor(qT[:, h, :], qT[:, h, :], Ex[0], ALU.mult)
                pool.tensor_tensor(kT[:, h, :], kT[:, h, :], Ex[1], ALU.mult).then_inc(s_gpl, 1)
            pool.wait_ge(s_gA, sum(v[3] == "A" for v in unitsG))
            for t in range(T):
                v = gr[:, t, :].rearrange("p (h n) -> p h n", h=GH)
                pool.tensor_tensor(v, v, outn[:, :].unsqueeze(1).to_broadcast([P, GH, GV]), ALU.mult).then_inc(s_gr, 1)

            pool.wait_ge(s_x2, T)
            pool.dma_start(gainrow[:, :], ffn_norm_2.to_broadcast([P, D])).then_inc(s_row2, 16)
            for t in range(T):
                root(ssg[:, 32 + t * GH:32 + (t + 1) * GH])
            row_roots()
            for t in range(T):
                pool.wait_ge(s_hnrow, t + 1)
                pool.dma_start(hn_dram[t * P:(t + 1) * P, :], xn[:, t, :]).then_inc(s_hnd, 16)
            pool.dma_start(gainrow[:, :], final_norm_2.rearrange("(a n) -> a n", a=1).to_broadcast([P, D])).then_inc(s_row2, 16)

            pool.wait_ge(s_go, GH * T)
            me.inc(pool.memset(skip_i[:, :], SKIP))
            me.wait()
            pool.dma_start(slot_dram[:, :].rearrange("(p n) a -> p (n a)", p=P), skip_i[:, :]).then_inc(s_fill, 16)
            me.inc(pool.iota(dest_i[:, :].rearrange("p (t k) -> p t k", t=T), pattern=[[P, T], [SEQ, 2]], base=0, channel_multiplier=1))
            me.inc(pool.iota(iog, pattern=[[1, GROUPS], [0, PER]], base=0, channel_multiplier=0, allow_small_or_imprecise_dtypes=True))
            me.inc(pool.iota(ioe, pattern=[[1, EXPERTS]], base=0, channel_multiplier=0, allow_small_or_imprecise_dtypes=True))
            me.wait()
            pool.wait_ge(s_tpA, KD // 2 * 6)
            pool.wait_ge(s_tpD, KD // 2 * 6 + 1)
            pool.memset(rk, 0.0).then_inc(s_cst, 1)
            pool.wait_ge(s_fill, 16)
            pool.wait_ge(s_idx, 1)
            for i in range(2 * T):
                pool.indirect_dma_start(out=slot_dram[:, :], out_offset=bass.IndirectOffsetOnAxis(ap=slot_i[:, i:i + 1], axis=0),
                                        in_=dest_i[:, i:i + 1], in_offset=None).then_inc(s_scat, 16)
            pool.wait_ge(s_rt, 1)
            for i in range(4):
                pool.memset(xe[i], 0.0).then_inc(s_xz, 1)
            pool.wait_ge(s_scat, 16 * 2 * T)
            pool.dma_start(dtab[:, :], slot_dram[:, :].rearrange("(p n) a -> p (n a)", p=P)).then_inc(s_tab, 16)
            pool.wait_ge(s_tabs, 1)
            pool.wait_ge(s_hnd, 16 * T)
            pool.wait_ge(s_xz, 4)
            bound_x = pool.to_reg(SEQ - 1)
            bound_y = pool.to_reg(ASG - 1)

            def gather(b, j, n):
                j = j % 4
                wait(pool, s_mx1, b - 3)
                col = ttab[:, b:b + 1] if isinstance(b, int) else ttab[:, bass.ds(b, 1)]
                pool.tensor_copy(gidx[:, j:j + 1], col).then_inc(s_ic, 1)
                pool.wait_ge(s_ic, n)
                pool.sem_inc(s_tick, 1)
                pool.indirect_dma_start(out=xe[j], out_offset=None, in_=hn_dram[:, :],
                                        in_offset=bass.IndirectOffsetOnAxis(ap=gidx[:, j:j + 1], axis=0),
                                        bounds_check=bound_x, oob_is_err=False).then_inc(s_xe[j], 16)

            def scatter(b, j, n):
                j = j % 4
                col = dtab[:, b:b + 1] if isinstance(b, int) else dtab[:, bass.ds(b, 1)]
                pool.tensor_copy(sidx[:, j:j + 1], col).then_inc(s_ic, 1)
                pool.wait_ge(s_ic, n)
                pool.wait_ge(s_myA, b + 1)
                pool.wait_ge(s_myD, b + 1)
                pool.sem_inc(s_tick, 1)
                pool.indirect_dma_start(out=y_dram[:, :], out_offset=bass.IndirectOffsetOnAxis(ap=sidx[:, j:j + 1], axis=0),
                                        in_=ye[j % 2], in_offset=None,
                                        bounds_check=bound_y, oob_is_err=False).then_inc(s_ys[j % 2], 16)

            gather(0, 0, 1)
            gather(1, 1, 2)
            n = 2
            for j in range(E_SLOTS):
                n += 1
                gather(j + 2, j + 2, n)
                if j:
                    n += 1
                    scatter(j - 1, j - 1, n)
            with pool.Fori(1, EXPERTS // E_SLOTS) as it:
                for j in range(E_SLOTS):
                    gather(it * E_SLOTS + (j + 2), j + 2, it * (2 * E_SLOTS) + (2 * j + 2))
                    scatter(it * E_SLOTS + (j - 1), j - 1, it * (2 * E_SLOTS) + (2 * j + 3))
            scatter(EXPERTS - 1, E_SLOTS - 1, 2 * EXPERTS + 2)
            n_ic = 2 * EXPERTS + 2
            n_over = pool.value_load(ovf_i[0:1, SPILL:SPILL + 1], min_val=0, max_val=SPILL)
            with pool.If(n_over > 0):
                with pool.Fori(0, SPILL) as i:
                    pool.wait_ge(s_mx1, i + (EXPERTS + 1))
                    pool.tensor_copy(gidx[:, 0:1], ttab[:, bass.ds(i + EXPERTS, 1)]).then_inc(s_ic, 1)
                    pool.wait_ge(s_ic, i * 2 + (n_ic + 1))
                    pool.sem_inc(s_tick, 1)
                    pool.indirect_dma_start(out=xe[0], out_offset=None, in_=hn_dram[:, :],
                                            in_offset=bass.IndirectOffsetOnAxis(ap=gidx[:, 0:1], axis=0),
                                            bounds_check=bound_x, oob_is_err=False).then_inc(s_xe[0], 16)
                    pool.tensor_copy(sidx[:, 0:1], dtab[:, bass.ds(i + EXPERTS, 1)]).then_inc(s_ic, 1)
                    pool.wait_ge(s_ic, i * 2 + (n_ic + 2))
                    pool.wait_ge(s_myA, i + (EXPERTS + 1))
                    pool.wait_ge(s_myD, i + (EXPERTS + 1))
                    pool.sem_inc(s_tick, 1)
                    pool.indirect_dma_start(out=y_dram[:, :], out_offset=bass.IndirectOffsetOnAxis(ap=sidx[:, 0:1], axis=0),
                                            in_=ye[0], in_offset=None,
                                            bounds_check=bound_y, oob_is_err=False).then_inc(s_ys[0], 16)
                    pool.wait_ge(s_ys[0], i * 16 + (8 * EXPERTS + 16))
            pool.wait_ge(s_ys[0], 8 * EXPERTS)
            pool.wait_ge(s_ys[1], 8 * EXPERTS)
            pool.wait_ge(s_my, EXPERTS)
            for k in range(2):
                for t in range(T):
                    o = (k * T + t) * D
                    pool.dma_start(big[:, o:o + D], y_dram[k * SEQ + t * P:k * SEQ + (t + 1) * P, :]).then_inc(s_yl, 16)
            row_roots()


_INS = ['x', 'meta_tokens', 'attn_norm', 'ffn_norm', 'final_norm', 'fox_w_in', 'fox_b_f', 'fox_q_norm', 'fox_k_norm',
        'fox_w_out', 'ffn_w_in', 'ffn_w_out', 'attn_norm_2', 'ffn_norm_2', 'final_norm_2', 'gla_w_in_2',
        'gla_w_gate_2', 'gla_b_gate_2', 'gla_out_norm_2', 'gla_w_o_2', 'moe_w_group_2', 'moe_w_expert_2',
        'moe_w1_2', 'moe_w3_2', 'moe_w2_2']


def kernel(**inputs):
    import numpy as _np
    import concourse.bacc as _bacc
    from concourse import mybir as _mybir
    from concourse.bass_utils import run_bass_kernel_spmd as _run

    nc = _bacc.Bacc("TRN2", target_bir_lowering=False, num_devices=1)
    arrays, args = {}, []
    for name in _INS:
        a = _np.ascontiguousarray(inputs[name])
        arrays[f"in_{name}_dram"] = a
        args.append(nc.dram_tensor(f"in_{name}_dram", a.shape, _mybir.dt.from_np(a.dtype), kind="ExternalInput").ap())
    args.append(nc.dram_tensor("out_0_dram", inputs["x"].shape, _mybir.dt.float32, kind="ExternalOutput").ap())
    program(nc, *args)
    r = _run(nc, [arrays], core_ids=[0])
    return r.results[0]["out_0_dram"]
```

```python
from contextlib import ExitStack

import concourse.bass as bass
from concourse import mybir

F32 = mybir.dt.float32
I32 = mybir.dt.int32
U32 = mybir.dt.uint32
ALU = mybir.AluOpType
ACT = mybir.ActivationFunctionType
AX = mybir.AxisListType.X

P = 128
EPS = 1e-6
NEG = -1e30
W_SLOTS = 3
C = 32
E_SLOTS = 4
SKIP = 1 << 20


class Count:

    def __init__(self, eng, sem):
        self.eng, self.sem, self.n = eng, sem, 0

    def inc(self, ins):
        self.n += 1
        return ins.then_inc(self.sem, 1)

    def wait(self):
        self.eng.wait_ge(self.sem, self.n)

    def link(self, ins):
        self.inc(ins)
        self.wait()


def wait(eng, sem, value):
    if not isinstance(value, int) or value > 0:
        eng.wait_ge(sem, value)


def program(nc, x, meta_tokens, attn_norm, ffn_norm, final_norm, fox_w_in, fox_b_f, fox_q_norm, fox_k_norm,
            fox_w_out, ffn_w_in, ffn_w_out, attn_norm_2, ffn_norm_2, final_norm_2, gla_w_in, gla_w_gate,
            gla_b_gate, gla_out_norm, gla_w_o, moe_w_group, moe_w_expert, moe_w1, moe_w3, moe_w2, out):
    _, SEQ, D = x.shape
    META = meta_tokens.shape[0]
    T = SEQ // P
    KD = D // P
    HEADS = fox_b_f.shape[1]
    HD = D // HEADS
    HA = HD + 2
    FH = ffn_w_out.shape[1]
    FT = FH // P
    GH = 4
    GK = gla_w_gate.shape[2] // GH
    GV = gla_out_norm.shape[1]
    RANK = gla_w_gate.shape[1]
    QK = GH * GK
    CH = 64
    NCH = SEQ // CH
    TAU = 16.0
    GROUPS = moe_w_group.shape[2]
    EXPERTS = moe_w_expert.shape[2]
    PER = EXPERTS // GROUPS
    FF = moe_w1.shape[3]
    KF = FF // P
    ASG = 2 * SEQ
    SPILL = (ASG - EXPERTS) // C
    NB = EXPERTS + SPILL
    QS = SEQ // C
    G2 = 64
    assert (META, HD, GK, GV, KF) == (16, 64, 128, 256, 2) and KD == 8 and T == 4

    hn_dram = nc.dram_tensor("hn_dram", [SEQ, D], F32)
    y_dram = nc.dram_tensor("y_dram", [ASG, D], F32)

    with ExitStack() as ctx:
        def sb(name, cols, dt=F32):
            return ctx.enter_context(nc.sbuf_tensor(name, [P, cols], dt))

        def sem(name):
            return ctx.enter_context(nc.semaphore(name))

        ps = ctx.enter_context(nc.psum_tensor("ps", [P, 8 * 512], F32))

        def bank(b, n=1):
            return ps[:, b * 512:(b + n) * 512]

        wring = sb("wring", W_SLOTS * 4096)
        big = sb("big", 16384)
        xres_t = sb("xres", T * D)
        hT_t = sb("hT", KD * SEQ)
        xn_t = sb("xn", T * D)
        mkv = sb("mkv", 2 * D)
        arena = sb("arena", 6144)
        hTm_t = sb("hTm", KD * META)
        gainrow = sb("gainrow", D)
        gcols = sb("gcols", 3 * KD)
        outn = sb("outn", GV)
        qgain = sb("qgain", 1)
        kgain = sb("kgain", 1)
        bf = sb("bf", HEADS)
        bgate = sb("bgate", GH)
        wgate = sb("wgate", QK)
        ident = sb("ident", P)
        tri = sb("tri", P)
        strict = sb("strict", P)
        ones = sb("ones", P)
        amask = sb("amask", P)
        gmask = sb("gmask", P)
        ss = sb("ss", 8)
        rstd = sb("rstd", 8)
        ssq = sb("ssq", 9 * HEADS)
        rsq = sb("rsq", 9 * HEADS)
        zf = sb("zf", 5 * HEADS)
        zt = sb("zt", 5 * HEADS)
        cc = sb("cc", 5 * HEADS)
        ncc = sb("ncc", 5 * HEADS)
        mxn = sb("mxn", 2 * 64)
        rsum = sb("rsum", 64)
        rinv = sb("rinv", 64)
        decay = sb("decay", GH * NCH)
        ssg = sb("ssg", 3 * GH * T)
        half = sb("half", 9 * HEADS)

        alrT = xn_t[:, 0:SEQ]
        reset = xn_t[:, SEQ:2 * SEQ]
        xres = xres_t[:, :].rearrange("p (t d) -> p t d", t=T)
        hT = hT_t[:, :].rearrange("p (k s) -> p k s", k=KD)
        xn = xn_t[:, :].rearrange("p (t d) -> p t d", t=T)
        hTm = hTm_t[:, :].rearrange("p (k s) -> p k s", k=KD)
        qkvg = big[:, :].rearrange("p (t n) -> p t n", t=T)
        metax = big[0:META, 0:D]
        metan = big[0:META, D:2 * D]

        at = [0]

        def part(n):
            at[0] += n
            return arena[:, at[0] - n:at[0]]

        qa = [part(T * HA).rearrange("p (t d) -> p t d", t=T) for _ in range(2)]
        ka = [part(T * HA).rearrange("p (t d) -> p t d", t=T) for _ in range(2)]
        kam = [part(HA) for _ in range(2)]
        QT = [part(SEQ) for _ in range(2)]
        KT = [part(META + SEQ) for _ in range(2)]
        Pb = [part(META + SEQ) for _ in range(3)]
        PT = [part(5 * P) for _ in range(2)]
        scr = [arena[:, 4096:5120], arena[:, 5120:6144]]
        sg = [arena[:, 0:512], arena[:, 512:1024]]
        actT = big[:, 0:FT * SEQ].rearrange("p (f s) -> p f s", f=FT)

        qT = big[:, 0:2048].rearrange("p (h s) -> p h s", h=GH)
        kT = big[:, 2048:4096].rearrange("p (h s) -> p h s", h=GH)
        gz = big[:, 4096:6144].rearrange("p (h s) -> p h s", h=GH)
        gg = big[:, 6144:8192].rearrange("p (h s) -> p h s", h=GH)
        gv = big[:, 8192:12288].rearrange("p (t n) -> p t n", t=T)
        gr = big[:, 12288:16384].rearrange("p (t n) -> p t n", t=T)
        qiT, ksT = gz, gg
        kst = mkv[:, :].rearrange("p (h t d) -> p h t d", h=GH, t=T)
        tmp1 = arena[:, 0:512]
        D1, D2 = arena[:, 1024:1536], arena[:, 1536:2048]
        Ex = [arena[:, 2048 + 512 * i:2560 + 512 * i] for i in range(4)]
        atm = arena[:, 0:2048].rearrange("p (h t s) -> p h t s", h=GH, t=T)
        St = arena[:, 4096:6144].rearrange("p (h b v) -> p h b v", h=GH, b=2)

        s_w = [sem(f"weights_in_{i}") for i in range(W_SLOTS)]
        s_x = [sem(f"x_in_{t}") for t in range(T)]
        s_meta = sem("meta_in")
        s_small = sem("small_in")
        s_row = sem("gainrow_in")
        s_row2 = sem("later_gainrow_in")
        s_cst = sem("constants_made")
        s_pool = sem("pool_self")
        s_ms = sem("mean_square_ready")
        s_pw = sem("root_taken")
        s_dve = sem("dve_self")
        s_act = sem("act_self")
        s_ss = sem("squares_summed")
        s_xn = sem("normed")
        s_tp = sem("transposed")
        s_tpA = sem("transposed_out_act")
        s_tpD = sem("transposed_out_dve")
        s_mB = sem("proj_done")
        s_eA = sem("proj_out_act")
        s_eD = sem("proj_out_dve")
        s_mg = sem("gate_proj_done")
        s_eg = sem("gate_proj_out")
        s_sig = sem("gate_sigmoid")
        s_og = sem("attn_gated")
        s_sqh = sem("head_squares")
        s_rs = sem("head_rstd")
        s_lf = sem("forget_log")
        s_cps = sem("decay_sums")
        s_c = sem("decay_ready")
        s_stage = sem("head_staged")
        s_qkt = sem("head_transposed")
        s_qkA = sem("head_qT_ready")
        s_S = sem("scores_ready")
        s_mx = sem("row_max_ready")
        s_exp = sem("probs_ready")
        s_T = sem("probs_transposed")
        s_ptA = sem("probsT_out_act")
        s_pv = sem("pv_done")
        s_o = sem("attn_out_ready")
        s_mO = sem("outproj_done")
        s_res = sem("residual_added")
        s_mH = sem("gate_up_done")
        s_silu = sem("silu_done")
        s_hid = sem("hidden_ready")
        s_x2 = sem("x2_ready")
        s_mG = sem("gla_proj_done")
        s_gA = sem("gla_proj_out_act")
        s_gD = sem("gla_proj_out_dve")
        s_mr = sem("gla_gate_done")
        s_er = sem("gla_gate_silu")
        s_gdv = sem("gla_dve_step")
        s_gac = sem("gla_act_step")
        s_gpl = sem("gla_pool_step")
        s_gr = sem("gla_gate_gained")
        s_reset = sem("chunk_starts_set")
        s_gU = sem("gla_units")
        s_kst = sem("k_state_ready")
        s_atm = sem("attn_masked")
        s_U = sem("state_update_ready")
        s_S2 = sem("state_ready")
        s_in = sem("chunk_out_done")
        s_gss = sem("gla_squares")
        s_go = sem("gla_out_ready")
        s_hnrow = sem("moe_input_ready")
        s_hnd = sem("moe_input_stored")
        s_rt = sem("router_logits")
        s_rte = sem("router_exp")
        s_oh = sem("one_hots_ready")
        s_pre = sem("prefix_ready")
        s_idx = sem("slots_ready")
        s_tab = sem("slot_table_in")
        s_tabs = sem("tables_ready")
        s_xz = sem("xe_zeroed")
        s_ew = [sem(f"expert_in_{i}") for i in range(E_SLOTS)]
        s_xe = [sem(f"tokens_in_{i}") for i in range(E_SLOTS)]
        s_ic = sem("index_copied")
        s_mx1 = sem("moe_xT")
        s_mxA = sem("moe_xT_out_act")
        s_gu = sem("moe_gate_up")
        s_msl = sem("moe_silu")
        s_mhid = sem("moe_hidden")
        s_mhT = sem("moe_hiddenT")
        s_mhTe = sem("moe_hiddenT_out")
        s_my = sem("moe_y")
        s_myA = sem("moe_y_out_act")
        s_myD = sem("moe_y_out_dve")
        s_ys = [sem(f"y_stored_{i}") for i in range(2)]
        s_yl = [sem(f"y_loaded_{t}") for t in range(T)]
        s_tick = sem("waits_taken")
        s_fin = sem("final_ready")
        s_out = sem("out_stored")

        W0 = fox_w_in[0].rearrange("(k p) n -> p k n", p=P)
        WO = fox_w_out[0].rearrange("(k p) n -> p k n", p=P)
        WI = ffn_w_in[0].rearrange("(k p) n -> p k n", p=P)
        W2 = ffn_w_out[0].rearrange("(k p) n -> p k n", p=P)
        WG = gla_w_in[0].rearrange("(k p) n -> p k n", p=P)
        WGO = gla_w_o[0].rearrange("(k p) n -> p k n", p=P)
        tiles, tile_at, tile_ready = [], {}, {}
        slot_count = [0] * W_SLOTS

        def add_tile(name, cols, parts, release):
            w = len(tiles)
            slot = w % W_SLOTS
            k = max(a + n for a, n, _, _ in parts)
            view = wring[:, slot * 4096:slot * 4096 + k * cols].rearrange("p (k n) -> p k n", k=k)
            slot_count[slot] += 16 * len(parts)
            tiles.append((slot, [(view[:, a:a + n, c:c + s.shape[2]], s) for a, n, c, s in parts], release))
            tile_at[name], tile_ready[name] = view, (s_w[slot], slot_count[slot])

        unitsB = []
        for name, c0, n in (("k", D, 2), ("q", 0, 2), ("f", 4 * D, 1), ("v", 2 * D, 2), ("g", 3 * D, 2)):
            for j in range(n):
                if name == "f":
                    unitsB.append((name, j, 0, "D"))
                else:
                    for t in range(T + (name in "kv")):
                        if name != "g":
                            unitsB.append((name, j, t, "AD"[t % 2]))
                cols = HEADS if name == "f" else 512
                add_tile(f"{name}{j}", cols, [(0, KD, 0, W0[:, :, c0 + j * 512:c0 + j * 512 + cols])],
                         (s_mB, len(unitsB)) if name != "g" else (s_mg, T * (j + 1)))
        for j in range(2):
            add_tile(f"wo{j}", 512, [(0, KD, 0, WO[:, :, j * 512:(j + 1) * 512])], (s_mO, 4 * (j + 1)))
        for j in range(FT // 2):
            add_tile(f"in{j}", 512, [(0, KD, 0, WI[:, :, j * 256:(j + 1) * 256]),
                                     (0, KD, 256, WI[:, :, FH + j * 256:FH + (j + 1) * 256])], (s_mH, 2 * (j + 1)))
        FK = [(a, min(8, FT - a)) for a in range(0, FT, 8)]
        for j in range(2):
            for i, (a, n) in enumerate(FK):
                add_tile(f"out{j}{i}", 512, [(0, n, 0, W2[:, a:a + n, j * 512:(j + 1) * 512])],
                         (s_mO, 8 + (j * len(FK) + i + 1) * 4))
        MO_FFN = 8 + 2 * len(FK) * 4
        unitsG = []
        for name, c0, n in (("a", 2 * QK + D, 1), ("q", 0, 1), ("k", QK, 1), ("v", 2 * QK, 2), ("r", 2 * QK + D + RANK, 2)):
            for j in range(n):
                if name == "a":
                    unitsG.append((name, 0, 0, "D"))
                elif name != "r":
                    for t in range(T):
                        unitsG.append((name, j, t, {"q": "A", "k": "D", "v": "D"}[name]))
                cols = RANK if name == "a" else 512
                add_tile(f"g{name}{j}", cols, [(0, KD, 0, WG[:, :, c0 + j * 512:c0 + j * 512 + cols])],
                         (s_mG, len(unitsG)) if name != "r" else (s_mr, 2 * T - 1 + j))
                if name == "q":
                    unitsG += [("z", 0, h, "A") for h in range(GH)]
        for j in range(2):
            add_tile(f"gwo{j}", 512, [(0, KD, 0, WGO[:, :, j * 512:(j + 1) * 512])],
                     (s_mO, MO_FFN + 4 * (j + 1)))
        NR = GROUPS + EXPERTS
        add_tile("rt", NR, [(0, KD, 0, moe_w_group[0].rearrange("(k p) n -> p k n", p=P)),
                            (0, KD, GROUPS, moe_w_expert[0].rearrange("(k p) n -> p k n", p=P))], (s_rt, 1))

        def obank(h, t):
            b = (t % 2) * 2 + h // 2
            return bank(b)[:, (h % 2) * GV:(h % 2 + 1) * GV]

        def ubank(h, c):
            return bank(4 + h // 2)[:, (h % 2) * GV:(h % 2 + 1) * GV]

        def evacs(units, u):
            return sum(v[3] == units[u][3] for v in units[:u + 1])

        def tile_wait(pe, name):
            s, n = tile_ready[name]
            pe.wait_ge(s, n)

        def sbank(s, a, b):
            return ps[:, 512 * (s % 2) + a:512 * (s % 2) + b]

        PTB, OB, GB, QB = 3 * 512, 5, 6, 7

        block = ctx.enter_context(nc.Block())

        def eslot(i):
            base = (big if i < 2 else wring)[:, (i % 2) * 6144:(i % 2) * 6144 + 6144]
            return (base[:, 0:4096].rearrange("p (g k n) -> p g k n", g=2, k=KD),
                    base[:, 4096:6144].rearrange("p (k n) -> p k n", k=KF))

        W1 = moe_w1[0].rearrange("e (p k) n -> e p (k n)", k=KD)
        W3 = moe_w3[0].rearrange("e (p k) n -> e p (k n)", k=KD)
        WW2 = moe_w2[0].rearrange("e (k p) n -> e p k n", k=KF)

        xe = [hT_t[:, i * D:(i + 1) * D] for i in range(4)]
        ye = [xn_t[:, i * D:(i + 1) * D] for i in range(2)]
        xeT = [xn_t[:, (2 + i) * D:(2 + i) * D + KD * C].rearrange("p (k c) -> p k c", k=KD) for i in range(2)]
        msg = [arena[:, i * P:(i + 1) * P] for i in range(2)]
        mhid = [arena[:, 256 + i * P:256 + (i + 1) * P] for i in range(2)]
        mhT = [arena[:, 512 + i * 64:512 + i * 64 + KF * C].rearrange("p (k c) -> p k c", k=KF) for i in range(2)]
        hbanks = ps[:, 4 * 512:(4 + KF) * 512].rearrange("p (k n) -> p k n", k=KF)[:, :, 0:C]
        arena_at = [640]

        def rpart(n, k=0):
            arena_at[0] += n
            v = arena[:, arena_at[0] - n:arena_at[0]]
            return v.rearrange("p (t n) -> p t n", t=k) if k else v

        lg = rpart(T * NR, T)
        oh = [rpart(T * EXPERTS, T) for _ in range(2)]
        ohs = rpart(T * EXPERTS, T)
        em = rpart(T * EXPERTS, T)
        rtm = rpart(T * EXPERTS, T)
        pre = rpart(T * EXPERTS, T)
        iog, ioe, one64 = rpart(EXPERTS), rpart(EXPERTS), rpart(EXPERTS)
        cnt, ob, obe, obs, ovt = (rpart(EXPERTS) for _ in range(5))
        gm8, em8 = rpart(8 * T, T), rpart(8 * T, T)
        gsel, gwt = rpart(T), rpart(T)
        gexp = rpart(T * GROUPS, T)
        esel, gates, rk, stt, qq, bl, q1, desf = (rpart(2 * T) for _ in range(8))
        xw = rpart(2 * T)
        iob, iow = rpart(NB), rpart(C)
        ohw = rpart(2 * T * C, 2 * T)
        tabf, tabm = rpart(NB), rpart(NB)
        ovf, ovc = rpart(SPILL + 1), rpart(SPILL)
        assert arena_at[0] <= 4096
        ohb = xn_t[:, 0:2 * T * NB].rearrange("p (a n) -> p a n", a=2 * T)
        ohall = arena[:, 640 + T * NR:640 + T * NR + 2 * T * EXPERTS].rearrange("p (a n) -> p a n", a=2 * T)
        ohp = xn_t[:, 2 * T * NB:2 * T * NB + 2 * T * EXPERTS].rearrange("p (a n) -> p a n", a=2 * T)
        ovm = xn_t[:, 2048:2048 + SPILL * EXPERTS].rearrange("p (i n) -> p i n", n=EXPERTS)
        dtab = arena[:, 4224:4224 + NB].bitcast(I32)
        ttab = arena[:, 4352:4352 + NB].bitcast(I32)
        gi_u = sb("gi_u", 8 * T, U32)
        ei_u = sb("ei_u", 8 * T, U32)
        ovf_i = sb("ovf_i", SPILL + 1, I32)
        gidx = sb("gidx", 4, I32)
        sidx = sb("sidx", 4, I32)

        @block.sync
        def _(sp):
            for t in range(T):
                sp.dma_start(xres[:, t, :], x[0, t * P:(t + 1) * P, :]).then_inc(s_x[t], 16)
            for w, (slot, dmas, release) in enumerate(tiles):
                if w >= W_SLOTS:
                    sp.wait_ge(*tiles[w - W_SLOTS][2])
                for dst, src in dmas:
                    sp.dma_start(dst, src).then_inc(s_w[slot], 16)

            def expert(e, j):
                w13, w2 = eslot(j)
                for g, src in enumerate((W1, W3)):
                    sp.dma_start(w13[:, g, :, :].rearrange("p k n -> p (k n)"), src[e]).then_inc(s_ew[j], 16)
                sp.dma_start(w2, WW2[e]).then_inc(s_ew[j], 16)

            sp.wait_ge(s_go, GH * T)
            expert(0, 0)
            expert(1, 1)
            sp.wait_ge(s_rt, 1)
            expert(2, 2)
            expert(3, 3)
            with sp.Fori(1, EXPERTS // E_SLOTS) as it:
                for j in range(E_SLOTS):
                    sp.wait_ge(s_my, it * E_SLOTS + (j + 1 - E_SLOTS))
                    expert(it * E_SLOTS + j, j)
            n_over = sp.value_load(ovf_i[0:1, SPILL:SPILL + 1], min_val=0, max_val=SPILL)
            with sp.If(n_over > 0):
                with sp.Fori(0, n_over) as i:
                    sp.wait_ge(s_my, i + EXPERTS)
                    e = sp.value_load(ovf_i[0:1, bass.ds(i, 1)], min_val=0, max_val=EXPERTS - 1)
                    expert(e, 0)
            sp.wait_ge(s_fin, 1)
            for t in range(T):
                sp.wait_ge(s_fin, t + 1)
                sp.dma_start(out[0, t * P:(t + 1) * P, :], xres[:, t, :]).then_inc(s_out, 16)
            sp.wait_ge(s_out, 16 * T)

        @block.scalar
        def _(act):
            me = Count(act, s_act)
            small = [
                (gcols[:, 0:KD], attn_norm[0].rearrange("(k p) -> p k", p=P)),
                (gcols[:, KD:2 * KD], ffn_norm[0].rearrange("(k p) -> p k", p=P)),
                (gcols[:, 2 * KD:3 * KD], attn_norm_2[0].rearrange("(k p) -> p k", p=P)),
                (qgain[0:HD, :], fox_q_norm.rearrange("a p -> p a")),
                (kgain[0:HD, :], fox_k_norm.rearrange("a p -> p a")),
                (bgate[:, :], gla_b_gate[0].rearrange("(k p) -> p k", p=P)),
                (bf[:, :], fox_b_f.to_broadcast([P, HEADS])),
                (outn[:, :], gla_out_norm.to_broadcast([P, GV])),
                (wgate[0:RANK, :], gla_w_gate[0]),
            ]
            act.dma_start(metax, meta_tokens).then_inc(s_meta, 16)
            with nc.allow_non_contiguous_dma("small gains, once"):
                for dst, src in small:
                    act.dma_start(dst, src).then_inc(s_small, 16)
            act.dma_start(gainrow[:, :], final_norm.rearrange("(a n) -> a n", a=1).to_broadcast([P, D])).then_inc(s_row, 16)

            squared = [0]

            def squares(n, t, src, rows=P):
                n = squared[0]
                squared[0] += 1
                wait(act, s_ss, n - 1)
                act.activation(scr[n % 2][0:rows, :], src, ACT.Square, accum_out=ss[0:rows, t:t + 1]).then_inc(s_ss, 1)

            def tp_out(n, gain):
                for k in range(0, KD, 2):
                    act.wait_ge(s_tp, KD * n + (n > 0) + k + 1)
                    act.activation(hT[:, k, :], bank(k), ACT.Copy, scale=gain[:, k:k + 1] if gain is not None else 1.0).then_inc(s_tpA, 1)

            for t in range(T):
                act.wait_ge(s_x[t], 16)
                squares(0, t, xres[:, t, :])
            act.wait_ge(s_meta, 16)
            squares(0, T, metax, META)
            act.wait_ge(s_small, 16 * len(small))
            tp_out(0, gcols[:, 0:KD])

            def headsq(n, src, rows=P):
                if n >= 2:
                    act.wait_ge(s_rs, n - 1)
                act.activation(scr[n % 2][0:rows, :], src, ACT.Square).then_inc(s_sqh, 1)

            for u, (name, j, t, eng) in enumerate(unitsB):
                if eng == "A":
                    act.wait_ge(s_mB, u + 1)
                    o = {"q": 0, "k": D, "v": 2 * D}[name] + j * 512
                    b = bank(u % 8)
                    if t == T:
                        o = (o - D if name == "k" else o - D)
                        act.copy(mkv[0:META, o:o + 512], b[0:META, :]).then_inc(s_eA, 1)
                    else:
                        act.copy(qkvg[:, t, o:o + 512], b).then_inc(s_eA, 1)
                if (name, j) == ("f", 0):
                    act.wait_ge(s_eA, evacs(unitsB, max(v for v in range(u) if unitsB[v][3] == "A")))
                    act.wait_ge(s_eD, evacs(unitsB, max(v for v in range(u) if unitsB[v][3] == "D")))
                    for t2 in range(T):
                        headsq(t2, qkvg[:, t2, 0:D])
                    for t2 in range(T):
                        headsq(T + t2, qkvg[:, t2, D:2 * D])
                    headsq(2 * T, mkv[0:META, 0:D], META)
            act.wait_ge(s_lf, 1)
            act.activation(zt[:, :], zt[:, :], ACT.Exp).then_inc(s_lf, 1)
            act.wait_ge(s_lf, 2)
            act.activation(zt[:, :], zt[:, :], ACT.Ln, bias=1.0).then_inc(s_lf, 1)

            NS = HEADS * T

            def qk_out(h, i):
                act.wait_ge(s_qkt, 3 * h + i + 1)
                if h >= 2 and i == 0:
                    act.wait_ge(s_S, T * (h - 1))
                dst, gain, n = ((QT[h % 2][0:HA, :], qgain, SEQ), (KT[h % 2][0:HA, META:META + SEQ], kgain, SEQ),
                                (KT[h % 2][0:HA, 0:META], kgain, META))[i]
                act.activation(dst, bank(QB)[0:HA, 0:n], ACT.Copy, scale=gain[0:HA, :]).then_inc(s_qkA, 1)

            def exps(s):
                i = s % T
                n = META + P * (i + 1)
                act.wait_ge(s_mx, s + 1)
                if s >= 3:
                    act.wait_ge(s_T, s - 2)
                act.activation(Pb[s % 3][:, 0:n], sbank(s, 0, n), ACT.Exp,
                               bias=mxn[:, 64 + s:65 + s], accum_out=rsum[:, s:s + 1]).then_inc(s_exp, 1)

            def pt_out(s):
                i = s % T
                act.wait_ge(s_T, s + 1)
                if s >= 2:
                    act.wait_ge(s_pv, s - 1)
                act.copy(PT[s % 2][0:META, 0:P], ps[0:META, PTB:PTB + P])
                act.copy(PT[s % 2][:, P:P * (i + 2)], ps[:, PTB + P:PTB + P * (i + 2)]).then_inc(s_ptA, 1)

            act.wait_ge(s_rs, 9)
            act.wait_ge(s_c, 1)
            for i in range(3):
                qk_out(0, i)
            exps(0)
            for s in range(NS):
                if s % T < 3 and s // T + 1 < HEADS:
                    qk_out(s // T + 1, s % T)
                if s + 1 < NS:
                    exps(s + 1)
                pt_out(s)
            for t in range(T):
                act.wait_ge(s_eg, T + t + 1)
                act.activation(qkvg[:, t, 3 * D:], qkvg[:, t, 3 * D:], ACT.Sigmoid).then_inc(s_sig, 1)
            tp_out(1, None)

            def norm(n, done):
                for t in range(T):
                    act.wait_ge(*done(t))
                    if t == 0:
                        act.wait_ge(s_hid, FT if n >= 3 else 0) if n >= 3 else None
                    squares(n, t, xres[:, t, :])

            norm(2, lambda t: (s_res, 5 + t))
            tp_out(2, gcols[:, KD:2 * KD])
            for f in range(FT):
                act.wait_ge(s_mH, f + 1)
                if f >= 2:
                    act.wait_ge(s_hid, f - 1)
                act.activation(sg[f % 2], bank((2 * f) % 8), ACT.Silu).then_inc(s_silu, 1)
            norm(3, lambda t: (s_res, 13 + t))
            for t in range(T):
                act.wait_ge(s_x2, t + 1)
                squares(4, t, xres[:, t, :])
            tp_out(3, gcols[:, 2 * KD:3 * KD])

            for u, (name, j, t, eng) in enumerate(unitsG):
                if eng != "A":
                    continue
                act.wait_ge(s_mG, u + 1)
                b = bank(u % 8)
                if name == "q":
                    act.activation(qT[:, t, :], b, ACT.Copy, scale=float(GK) ** -0.5).then_inc(s_gA, 1)
                elif name == "z":
                    act.activation(gz[:, t, :], b, ACT.Identity, bias=bgate[:, t:t + 1]).then_inc(s_gA, 1)
            for h in range(GH):
                act.wait_ge(s_gdv, 3 * h + 1)
                act.activation(tmp1, tmp1, ACT.Exp).then_inc(s_gac, 1)
                act.wait_ge(s_gac, 7 * h + 1)
                act.activation(tmp1, tmp1, ACT.Ln, bias=1.0).then_inc(s_gac, 1)
                act.wait_ge(s_gdv, 3 * h + 3)
                if h >= 1:
                    act.wait_ge(s_gpl, h)
                act.activation(Ex[0], D1, ACT.Exp, scale=1 / TAU).then_inc(s_gac, 1)
                act.activation(Ex[1], D1, ACT.Exp, scale=-1 / TAU).then_inc(s_gac, 1)
                act.activation(Ex[2], gg[:, h, :], ACT.Exp, scale=1 / TAU).then_inc(s_gac, 1)
                act.activation(Ex[3], D2, ACT.Exp, scale=1 / TAU).then_inc(s_gac, 1)
                act.activation(decay[:, h * NCH:(h + 1) * NCH].rearrange("p (c a) -> p c a", a=1),
                               gg[:, h, :].rearrange("p (c s) -> p c s", c=NCH)[:, :, CH - 1:CH],
                               ACT.Exp, scale=1 / TAU).then_inc(s_gac, 1)
            for h in range(GH):
                act.wait_ge(s_gU, 2 * h + 1)
                act.copy(kst[:, h, :, :], bank(h).rearrange("p (t d) -> p t d", t=T)).then_inc(s_kst, 1)
            for t in range(T):
                for j in range(2):
                    act.wait_ge(s_mr, 2 * t + j + 1)
                    act.activation(gr[:, t, j * 512:(j + 1) * 512], bank(6 + j), ACT.Silu).then_inc(s_er, 1)
                for h in range(GH):
                    act.wait_ge(s_in, (2 * t + 2) * GH)
                    n = t * GH + h
                    wait(act, s_gss, n - 1)
                    act.activation(arena[:, 2048 + (n % 2) * GV:2048 + (n % 2 + 1) * GV], obank(h, t), ACT.Square,
                                   accum_out=ssg[:, n:n + 1]).then_inc(s_gss, 1)
            tp_out(4, None)
            for t in range(T):
                act.wait_ge(s_res, 21 + t)
                squares(5, t, xres[:, t, :])
            tp_out(5, None)

            act.wait_ge(s_oh, 1)
            for t in range(T):
                act.activation(gexp[:, t, :], lg[:, t, 0:GROUPS], ACT.Exp, bias=xw[:, t:t + 1],
                               accum_out=gwt[:, t:t + 1]).then_inc(s_rte, 1)
            act.activation(xw[:, T:2 * T], xw[:, T:2 * T], ACT.Exp).then_inc(s_rte, 1)

            def xT_out(b, j):
                act.wait_ge(s_mx1, b + 1)
                wait(act, s_gu, b - 1)
                act.copy(xeT[j % 2].rearrange("p k c -> p (k c)"), bank(j % 2)[:, 0:KD * C]).then_inc(s_mxA, 1)

            def silu(b, j):
                act.wait_ge(s_gu, b + 1)
                wait(act, s_mhid, b - 1)
                act.activation(msg[j % 2][0:C, :], bank(2 + j % 2)[0:C, 0:P], ACT.Silu)
                act.activation(msg[j % 2][G2:G2 + C, :], bank(2 + j % 2)[G2:G2 + C, 0:P], ACT.Silu).then_inc(s_msl, 1)

            def y_out(b, j):
                act.wait_ge(s_my, b + 1)
                if not isinstance(b, int) or b >= 2:
                    act.wait_ge(s_ys[j % 2], (b - j % 2) * 8)
                act.copy(ye[j % 2][0:C, 0:512], bank(6 + j % 2)[0:C, :]).then_inc(s_myA, 1)

            def block_(base, j, first):
                silu(base + j, j)
                xT_out(base + j + 1, j + 1)
                if not first:
                    y_out(base + j - 1, j - 1)

            xT_out(0, 0)
            for j in range(E_SLOTS):
                block_(0, j, j == 0)
            with act.Fori(1, EXPERTS // E_SLOTS) as it:
                for j in range(E_SLOTS):
                    block_(it * E_SLOTS, j, False)
            y_out(EXPERTS - 1, E_SLOTS - 1)

            n_over = act.value_load(ovf_i[0:1, SPILL:SPILL + 1], min_val=0, max_val=SPILL)
            with act.If(n_over > 0):
                with act.Fori(0, n_over) as i:
                    act.wait_ge(s_mx1, i + (EXPERTS + 2))
                    act.copy(xeT[0].rearrange("p k c -> p (k c)"), bank(0)[:, 0:KD * C]).then_inc(s_mxA, 1)
                    act.wait_ge(s_gu, i + (EXPERTS + 1))
                    act.activation(msg[0][0:C, :], bank(2)[0:C, 0:P], ACT.Silu)
                    act.activation(msg[0][G2:G2 + C, :], bank(2)[G2:G2 + C, 0:P], ACT.Silu).then_inc(s_msl, 1)
                    act.wait_ge(s_my, i + (EXPERTS + 1))
                    act.wait_ge(s_ys[0], i * 16 + 8 * EXPERTS)
                    act.copy(ye[0][0:C, 0:512], bank(6)[0:C, :]).then_inc(s_myA, 1)
            for t in range(T):
                act.wait_ge(s_x2, T + t + 1)
                squares(6, t, xres[:, t, :])

        @block.tensor
        def _(pe):
            def transposes(n, ready):
                pe.wait_ge(*ready)
                for k in range(KD):
                    for t in range(T):
                        last = pe.transpose(bank(k)[:, t * P:(t + 1) * P], xn[:, t, k * P:(k + 1) * P], ident[:, :])
                    last.then_inc(s_tp, 1)

            def hT_ready(n):
                pe.wait_ge(s_tpA, KD // 2 * (n + 1))
                pe.wait_ge(s_tpD, KD // 2 * (n + 1) + 1)

            pe.wait_ge(s_cst, 1)
            transposes(0, (s_xn, T))
            pe.wait_ge(s_xn, T + 1)
            pe.wait_ge(s_tpA, 1)
            for k in range(KD):
                last = pe.transpose(bank(0)[:, k * META:(k + 1) * META], metan[:, k * P:(k + 1) * P], ident[0:META, 0:META])
            last.then_inc(s_tp, 1)
            hT_ready(0)

            def free(units, u, sA, sD):
                if u >= 8:
                    v = u - 8
                    pe.wait_ge(sA if units[v][3] == "A" else sD, evacs(units, v))

            for u, (name, j, t, eng) in enumerate(unitsB):
                if t == 0:
                    tile_wait(pe, f"{name}{j}")
                w = tile_at[f"{name}{j}"]
                free(unitsB, u, s_eA, s_eD)
                b = bank(u % 8)
                if name == "f":
                    for tt in range(T + 1):
                        for k in range(KD):
                            lhs = hT[:, k, tt * P:(tt + 1) * P] if tt < T else hTm[:, k, :]
                            m = P if tt < T else META
                            last = pe.matmul(b[0:m, tt * HEADS:(tt + 1) * HEADS], lhs, w[:, k, :], start=(k == 0), stop=(k == KD - 1))
                else:
                    for k in range(KD):
                        lhs = hT[:, k, t * P:(t + 1) * P] if t < T else hTm[:, k, :]
                        m = P if t < T else META
                        last = pe.matmul(b[0:m, :], lhs, w[:, k, :], start=(k == 0), stop=(k == KD - 1))
                last.then_inc(s_mB, 1)

            def banks_free(units, sA, sD):
                pe.wait_ge(sA, sum(v[3] == "A" for v in units))
                pe.wait_ge(sD, sum(v[3] == "D" for v in units))

            banks_free(unitsB, s_eA, s_eD)
            pe.wait_ge(s_lf, 4)
            b = bank(0)
            H = HEADS
            for t in range(T):
                o = b[:, t * H:(t + 1) * H]
                pe.matmul(o, ones[0:META, :], zf[0:META, T * H:(T + 1) * H], start=True, stop=False)
                for j in range(t):
                    pe.matmul(o, ones[:, :], zf[:, j * H:(j + 1) * H], start=False, stop=False)
                pe.matmul(o, tri[:, :], zf[:, t * H:(t + 1) * H], start=False, stop=True)
            pe.matmul(b[0:META, T * H:(T + 1) * H], tri[0:META, 0:META], zf[0:META, T * H:(T + 1) * H],
                      start=True, stop=True).then_inc(s_cps, 1)
            pe.wait_ge(s_c, 1)

            NS = HEADS * T

            def qk(h, i):
                if i == 0:
                    pe.wait_ge(s_stage, h + 1)
                wait(pe, s_qkA, 3 * h + i)
                if i == 2:
                    last = pe.transpose(bank(QB)[0:HA, 0:META], kam[h % 2][0:META, :], ident[0:META, 0:META])
                else:
                    for t in range(T):
                        last = pe.transpose(bank(QB)[0:HA, t * P:(t + 1) * P], (qa, ka)[i][h % 2][:, t, :], ident[:, :])
                last.then_inc(s_qkt, 1)

            def scores(s):
                h, i = divmod(s, T)
                n = META + P * (i + 1)
                if i == 0:
                    pe.wait_ge(s_qkA, 3 * h + 3)
                if s >= 2:
                    pe.wait_ge(s_exp, s - 1)
                lhs = QT[h % 2][0:HA, i * P:(i + 1) * P]
                last = pe.matmul(sbank(s, 0, min(n, 512)), lhs, KT[h % 2][0:HA, 0:min(n, 512)], start=True, stop=True)
                if n > 512:
                    last = pe.matmul(sbank(s, 512, n), lhs, KT[h % 2][0:HA, 512:n], start=True, stop=True)
                last.then_inc(s_S, 1)

            def ptrans(s):
                i = s % T
                pe.wait_ge(s_exp, s + 1)
                if s:
                    pe.wait_ge(s_ptA, s)
                pe.transpose(ps[0:META, PTB:PTB + P], Pb[s % 3][:, 0:META], ident[:, :])
                for j in range(i + 1):
                    last = pe.transpose(ps[:, PTB + P * (j + 1):PTB + P * (j + 2)], Pb[s % 3][:, META + P * j:META + P * (j + 1)], ident[:, :])
                last.then_inc(s_T, 1)

            def pv(s):
                h, i = divmod(s, T)
                pe.wait_ge(s_ptA, s + 1)
                wait(pe, s_o, s)
                o = bank(OB)[:, 0:HD]
                pe.matmul(o, PT[s % 2][0:META, 0:P], mkv[0:META, D + h * HD:D + (h + 1) * HD], start=True, stop=False)
                for j in range(i + 1):
                    last = pe.matmul(o, PT[s % 2][:, P * (j + 1):P * (j + 2)],
                                     qkvg[:, j, 2 * D + h * HD:2 * D + (h + 1) * HD], start=False, stop=(j == i))
                last.then_inc(s_pv, 1)

            def gate_step(s):
                g, k = divmod(s, KD)
                j, t = divmod(g, T)
                w = tile_at[f"g{j}"]
                if s % (T * KD) == 0:
                    tile_wait(pe, f"g{j}")
                if k == 0:
                    wait(pe, s_eg, g)
                last = pe.matmul(bank(GB), hT[:, k, t * P:(t + 1) * P], w[:, k, :], start=(k == 0), stop=(k == KD - 1))
                if k == KD - 1:
                    last.then_inc(s_mg, 1)

            for i in range(3):
                qk(0, i)
            scores(0)
            for s in range(NS):
                if s % T < 3 and s // T + 1 < HEADS:
                    qk(s // T + 1, s % T)
                if s + 1 < NS:
                    scores(s + 1)
                gate_step(s)
                ptrans(s)
                if s:
                    pv(s - 1)
            pv(NS - 1)

            transposes(1, (s_og, T))
            hT_ready(1)

            def outproj(base, names, first):
                for j in range(2):
                    n = 0
                    for i, name in enumerate(names(j)):
                        w = tile_at[name]
                        tile_wait(pe, name)
                        for t in range(T):
                            for k in range(w.shape[1]):
                                src = first(n + k)
                                last = pe.matmul(bank(4 * j + t), src[:, t * P:(t + 1) * P], w[:, k, :],
                                                 start=(n + k == 0), stop=(i == len(names(j)) - 1 and k == w.shape[1] - 1))
                            last.then_inc(s_mO, 1)
                        n += w.shape[1]

            outproj(0, lambda j: [f"wo{j}"], lambda k: hT[:, k, :])
            transposes(2, (s_xn, 2 * T + 1))
            hT_ready(2)
            for f in range(FT):
                if f % 2 == 0:
                    tile_wait(pe, f"in{f // 2}")
                w = tile_at[f"in{f // 2}"]
                if f >= 4:
                    pe.wait_ge(s_hid, f - 3)
                for g in range(2):
                    c = g * 256 + (f % 2) * P
                    for k in range(KD):
                        last = pe.matmul(bank((2 * f + g) % 8), w[:, k, c:c + P], hT[:, k, :], start=(k == 0), stop=(k == KD - 1))
                last.then_inc(s_mH, 1)
            pe.wait_ge(s_hid, FT)
            outproj(1, lambda j: [f"out{j}{i}" for i in range(len(FK))], lambda k: actT[:, k, :])
            transposes(3, (s_xn, 3 * T + 1))
            hT_ready(3)

            for u, (name, j, t, eng) in enumerate(unitsG):
                if t == 0 and name != "z":
                    tile_wait(pe, f"g{name}{j}")
                free(unitsG, u, s_gA, s_gD)
                b = bank(u % 8)
                if name == "z":
                    pe.wait_ge(s_gD, 1)
                    last = pe.matmul(b, wgate[0:RANK, t * P:(t + 1) * P], alrT[0:RANK, :], start=True, stop=True)
                else:
                    w = tile_at[f"g{name}{j}"]
                    for k in range(KD):
                        if name == "a":
                            last = pe.matmul(b[0:RANK, :], w[:, k, :], hT[:, k, :], start=(k == 0), stop=(k == KD - 1))
                        elif name in "qk":
                            last = pe.matmul(b, w[:, k, t * P:(t + 1) * P], hT[:, k, :], start=(k == 0), stop=(k == KD - 1))
                        else:
                            last = pe.matmul(b, hT[:, k, t * P:(t + 1) * P], w[:, k, :], start=(k == 0), stop=(k == KD - 1))
                last.then_inc(s_mG, 1)
            banks_free(unitsG, s_gA, s_gD)
            for h in range(GH):
                pe.wait_ge(s_gpl, h + 1)
                for t in range(T):
                    last = pe.transpose(bank(h)[:, t * P:(t + 1) * P], ksT[:, h, t * P:(t + 1) * P], ident[:, :])
                last.then_inc(s_gU, 1)
                for t in range(T):
                    last = pe.matmul(bank(4 + h)[:, t * P:(t + 1) * P], kT[:, h, t * P:(t + 1) * P], qT[:, h, t * P:(t + 1) * P],
                                     start=True, stop=True)
                last.then_inc(s_gU, 1)
            pe.wait_ge(s_kst, GH)
            pe.wait_ge(s_atm, GH)
            for c in range(NCH):
                t, r = divmod(c, 2)
                rows = slice(r * CH, (r + 1) * CH)
                for h in range(GH):
                    if c < NCH - 1:
                        if c >= 1:
                            pe.wait_ge(s_S2, (c - 1) * GH + (h | 1) + 1)
                        pe.matmul(ubank(h, c), kst[rows, h, t, :],
                                  gv[rows, t, h * GV:(h + 1) * GV], start=True, stop=True).then_inc(s_U, 1)
                    o = obank(h, t)
                    if r == 0:
                        if t >= 2:
                            pe.wait_ge(s_go, (t - 2) * GH + (h | 1) + 1)
                        last = pe.matmul(o, atm[:, h, t, :], gv[:, t, h * GV:(h + 1) * GV], start=(h % 2 == 0), stop=False,
                                         skip_group_check=True)
                    if c:
                        pe.wait_ge(s_S2, (c - 1) * GH + h + 1)
                        last = pe.matmul(o[rows, :], qiT[:, h, c * CH:(c + 1) * CH], St[:, h, c % 2, :],
                                         start=False, stop=(r == 1), skip_group_check=True)
                    last.then_inc(s_in, 1)
                    for n in (2 * (c * GH + h), 2 * (c * GH + h) + 1):
                        u, k = divmod(n, KD)
                        tr, jr = divmod(u, 2)
                        if n in (0, KD):
                            tile_wait(pe, f"gr{jr}")
                        if k == 0:
                            wait(pe, s_er, u - 1)
                        last = pe.matmul(bank(6 + jr), hT[:, k, tr * P:(tr + 1) * P], tile_at[f"gr{jr}"][:, k, :],
                                         start=(k == 0), stop=(k == KD - 1))
                    if k == KD - 1:
                        last.then_inc(s_mr, 1)
            transposes(4, (s_go, GH * T))
            hT_ready(4)
            outproj(2, lambda j: [f"gwo{j}"], lambda k: hT[:, k, :])
            transposes(5, (s_hnrow, T))
            hT_ready(5)
            tile_wait(pe, "rt")
            w = tile_at["rt"]
            for t in range(T):
                for k in range(KD):
                    last = pe.matmul(bank(0)[:, t * NR:(t + 1) * NR], hT[:, k, t * P:(t + 1) * P], w[:, k, :], start=(k == 0), stop=(k == KD - 1))
            last.then_inc(s_rt, 1)
            pe.wait_ge(s_oh, 2)
            for t in range(T):
                o = bank(1)[:, t * EXPERTS:(t + 1) * EXPERTS]
                for j in range(t):
                    pe.matmul(o, ones[:, :], ohs[:, j, :], start=(j == 0), stop=False)
                pe.matmul(o, strict[:, :], ohs[:, t, :], start=(t == 0), stop=True)
            for t in range(T):
                last = pe.matmul(bank(1)[:, T * EXPERTS:(T + 1) * EXPERTS], ones[:, :], ohs[:, t, :], start=(t == 0), stop=(t == T - 1))
            last.then_inc(s_pre, 1)
            pe.wait_ge(s_idx, 1)
            for a in range(2 * T):
                last = pe.matmul(bank(2)[0:C, 0:NB], ohw[:, a, :], ohb[:, a, :], start=(a == 0), stop=(a == 2 * T - 1))
            last.then_inc(s_tab, 1)

            def tokens(j, buf):
                pe.sem_inc(s_tick, 1)
                v = xe[buf].rearrange("p (m k) -> p k m", k=KD)
                for k in range(KD):
                    last = pe.transpose(bank(j % 2)[:, k * C:(k + 1) * C], v[0:C, k, :], ident[0:C, 0:C])
                last.then_inc(s_mx1, 1)

            def A(b, j, n):
                pe.wait_ge(s_xe[j % 4], n)
                wait(pe, s_mxA, b - 1)
                tokens(j, j % 4)

            def gate_up(j, slot):
                w13, _ = eslot(slot)
                g = bank(2 + j % 2)
                for k in range(KD):
                    for q in range(2):
                        last = pe.matmul(g[q * G2:q * G2 + C, 0:2 * P], xeT[j % 2][:, k, :], w13[:, :, k, q * P:(q + 1) * P],
                                         start=(k == 0), stop=(k == KD - 1), skip_group_check=True)
                last.then_inc(s_gu, 1)

            def B(b, j, n_w):
                pe.wait_ge(s_ew[j], n_w)
                pe.wait_ge(s_mxA, b + 1)
                wait(pe, s_mhid, b - 1)
                gate_up(j, j)

            def hidden(j):
                pe.sem_inc(s_tick, 1)
                for q in range(2):
                    r = slice(q * G2, q * G2 + C)
                    last = pe.transpose(bank(4 + q)[:, 0:C], mhid[j % 2][r, :], ident[r, r])
                last.then_inc(s_mhT, 1)

            def Ct(b, j):
                pe.wait_ge(s_mhid, b + 1)
                wait(pe, s_mhTe, b)
                hidden(j)

            def down(j, slot):
                w2 = eslot(slot)[1]
                for k in range(KF):
                    for n in range(2):
                        last = pe.matmul(bank(6 + j % 2)[n * G2:n * G2 + C, :], mhT[j % 2][:, k, :], w2[:, k, n * 512:(n + 1) * 512],
                                         start=(k == 0), stop=(k == KF - 1), skip_group_check=True)
                last.then_inc(s_my, 1)

            def Dy(b, j):
                pe.wait_ge(s_mhTe, b + 1)
                wait(pe, s_myA, b - 1)
                wait(pe, s_myD, b - 1)
                down(j, j % 4)

            def block_(base, j, first, n_w):
                B(base + j, j, n_w)
                A(base + j + 1, j + 1, n_w // 3 + (16 if j == 3 else 0) if isinstance(n_w, int) else base * 4 + (16 if j < 3 else 32))
                if not first:
                    Dy(base + j - 1, (j - 1) % 4)
                Ct(base + j, j)

            pe.wait_ge(s_tabs, 1)
            A(0, 0, 16)
            for j in range(E_SLOTS):
                block_(0, j, j == 0, 48)
            with pe.Fori(1, EXPERTS // E_SLOTS) as it:
                for j in range(E_SLOTS):
                    block_(it * E_SLOTS, j, False, it * 48 + 48)
            Dy(EXPERTS - 1, E_SLOTS - 1)
            n_over = pe.value_load(ovf_i[0:1, SPILL:SPILL + 1], min_val=0, max_val=SPILL)
            with pe.If(n_over > 0):
                with pe.Fori(0, n_over) as i:
                    pe.wait_ge(s_xe[0], i * 16 + 4 * (EXPERTS + 4) + 16)
                    pe.wait_ge(s_mxA, i + (EXPERTS + 1))
                    tokens(0, 0)
                    pe.wait_ge(s_ew[0], i * 48 + 48 * (EXPERTS // 4 + 1))
                    pe.wait_ge(s_mxA, i + (EXPERTS + 2))
                    pe.wait_ge(s_mhid, i + EXPERTS)
                    gate_up(0, 0)
                    pe.wait_ge(s_mhid, i + (EXPERTS + 1))
                    hidden(0)
                    pe.wait_ge(s_mhTe, i + (EXPERTS + 1))
                    pe.wait_ge(s_myA, i + EXPERTS)
                    pe.wait_ge(s_myD, i + EXPERTS)
                    down(0, 0)

        @block.vector
        def _(dve):
            me = Count(dve, s_dve)

            roots = Count(dve, s_ms)

            def rms_scale(dst, src, n):
                roots.inc(dve.tensor_scalar(dst, src, 1.0 / n, EPS, ALU.mult, ALU.add))
                dve.wait_ge(s_pw, roots.n)

            def tp_out(n, gain):
                for k in range(1, KD, 2):
                    dve.wait_ge(s_tp, KD * n + (n > 0) + k + 1)
                    if gain is not None:
                        dve.tensor_scalar(hT[:, k, :], bank(k), gain[:, k:k + 1], None, ALU.mult).then_inc(s_tpD, 1)
                    else:
                        dve.tensor_copy(hT[:, k, :], bank(k)).then_inc(s_tpD, 1)

            def normed(n_ss):
                for t in range(T):
                    dve.wait_ge(s_ss, n_ss + t + 1)
                    rms_scale(rstd[:, t:t + 1], ss[:, t:t + 1], D)
                    dve.tensor_scalar(xn[:, t, :], xres[:, t, :], rstd[:, t:t + 1], None, ALU.mult).then_inc(s_xn, 1)

            normed(0)
            dve.wait_ge(s_ss, T + 1)
            rms_scale(rstd[0:META, T:T + 1], ss[0:META, T:T + 1], D)
            dve.tensor_scalar(metan, metax, rstd[0:META, T:T + 1], None, ALU.mult).then_inc(s_xn, 1)
            dve.wait_ge(s_small, 16 * 9)
            tp_out(0, gcols[:, 0:KD])
            dve.wait_ge(s_tp, KD + 1)
            dve.tensor_tensor(hTm, bank(0)[:, 0:KD * META].rearrange("p (k s) -> p k s", k=KD),
                              gcols[:, 0:KD].unsqueeze(2).to_broadcast([P, KD, META]), ALU.mult).then_inc(s_tpD, 1)
            H = HEADS
            me.link(dve.memset(zf[:, :], 0.0))
            for u, (name, j, t, eng) in enumerate(unitsB):
                if eng == "D":
                    dve.wait_ge(s_mB, u + 1)
                    b = bank(u % 8)
                    if name == "f":
                        dve.tensor_tensor(zf[0:META, T * H:], b[0:META, T * H:(T + 1) * H], bf[0:META, :], ALU.add)
                        dve.tensor_tensor(zf[:, 0:T * H].rearrange("p (t h) -> p t h", t=T), b[:, 0:T * H].rearrange("p (t h) -> p t h", t=T),
                                          bf[:, :].unsqueeze(1).to_broadcast([P, T, H]), ALU.add).then_inc(s_eD, 1)
                        dve.wait_ge(s_eD, evacs(unitsB, u))
                        dve.scalar_tensor_tensor(out=zt[:, :], in0=zf[:, :], scalar=-1.0, in1=zf[:, :], op0=ALU.mult, op1=ALU.min).then_inc(s_lf, 1)
                        for n in range(9):
                            rows = P if n < 8 else META
                            dve.wait_ge(s_sqh, n + 1)
                            dve.tensor_reduce(ssq[0:rows, n * H:(n + 1) * H], scr[n % 2][0:rows, :].rearrange("p (h d) -> p h d", h=H),
                                              AX, ALU.add).then_inc(s_rs, 1)
                        continue
                    o = {"q": 0, "k": D, "v": 2 * D}[name] + j * 512
                    if t == T:
                        dve.tensor_copy(mkv[0:META, o - D:o - D + 512], b[0:META, :]).then_inc(s_eD, 1)
                    else:
                        dve.tensor_copy(qkvg[:, t, o:o + 512], b).then_inc(s_eD, 1)
            dve.wait_ge(s_rs, 9)
            rms_scale(rsq[:, 0:8 * H], ssq[:, 0:8 * H], HD)
            rms_scale(rsq[0:META, 8 * H:], ssq[0:META, 8 * H:], HD)
            me.link(dve.memset(qgain[HD:P, :], 1.0))
            me.link(dve.memset(kgain[HD:P, :], 1.0))
            me.link(dve.tensor_scalar(qgain[0:HD, :], qgain[0:HD, :], float(HD) ** -0.5, None, ALU.mult))
            dve.wait_ge(s_lf, 3)
            dve.scalar_tensor_tensor(out=zf[:, :], in0=zf[:, :], scalar=0.0, in1=zt[:, :], op0=ALU.min, op1=ALU.subtract).then_inc(s_lf, 1)
            dve.wait_ge(s_cps, 1)
            n = T * H
            me.link(dve.memset(cc[:, :], 0.0))
            me.link(dve.tensor_copy(cc[:, 0:n], bank(0)[:, 0:n]))
            me.link(dve.tensor_copy(cc[0:META, n:], bank(0)[0:META, n:n + H]))
            dve.tensor_scalar(ncc[:, :], cc[:, :], -1.0, None, ALU.mult).then_inc(s_c, 1)

            NS = HEADS * T
            dve.wait_ge(s_cst, 1)

            def rowmax(s):
                i = s % T
                n = META + P * (i + 1)
                dve.wait_ge(s_S, s + 1)
                me.link(dve.tensor_tensor(sbank(s, n - P, n), sbank(s, n - P, n), amask[:, :], ALU.add))
                me.link(dve.tensor_reduce(mxn[:, s:s + 1], sbank(s, 0, n), AX, ALU.max))
                dve.tensor_scalar(mxn[:, 64 + s:65 + s], mxn[:, s:s + 1], -1.0, None, ALU.mult).then_inc(s_mx, 1)

            def attn_out(s):
                h, i = divmod(s, T)
                me.link(dve.reciprocal(rinv[:, s:s + 1], rsum[:, s:s + 1]))
                dve.wait_ge(s_pv, s + 1)
                dve.tensor_scalar(xn[:, i, h * HD:(h + 1) * HD], bank(OB)[:, 0:HD], rinv[:, s:s + 1], None, ALU.mult).then_inc(s_o, 1)

            def gate_out(g):
                j, t = divmod(g, T)
                dve.wait_ge(s_mg, g + 1)
                dve.tensor_copy(qkvg[:, t, 3 * D + j * 512:3 * D + (j + 1) * 512], bank(GB)).then_inc(s_eg, 1)

            rowmax(0)
            for s in range(NS):
                if s + 1 < NS:
                    rowmax(s + 1)
                if s % KD == 0 and s:
                    gate_out(s // KD - 1)
                if s:
                    attn_out(s - 1)
            attn_out(NS - 1)
            gate_out(2 * T - 1)
            dve.wait_ge(s_o, NS)
            for t in range(T):
                dve.wait_ge(s_sig, t + 1)
                dve.tensor_tensor(xn[:, t, :], xn[:, t, :], qkvg[:, t, 3 * D:], ALU.mult).then_inc(s_og, 1)
            tp_out(1, None)

            def residual(base, n, norm):
                for j in range(2):
                    for t in range(T):
                        dve.wait_ge(s_mO, base + (j + 1) * n * 4 - 4 + t + 1)
                        d = xres[:, t, j * 512:(j + 1) * 512]
                        dve.tensor_tensor(d, d, bank(4 * j + t), ALU.add).then_inc(s_res, 1)
                        if j and t:
                            norm(t - 1)
                norm(T - 1)

            def norm_tile(n_ss, n_res):
                def norm(t):
                    dve.wait_ge(s_res, n_res + T + t + 1)
                    dve.wait_ge(s_ss, n_ss + t + 1)
                    rms_scale(rstd[:, t:t + 1], ss[:, t:t + 1], D)
                    dve.tensor_scalar(xn[:, t, :], xres[:, t, :], rstd[:, t:t + 1], None, ALU.mult).then_inc(s_xn, 1)
                return norm

            residual(0, 1, norm_tile(5, 0))
            tp_out(2, gcols[:, KD:2 * KD])
            for f in range(FT):
                dve.wait_ge(s_silu, f + 1)
                dve.tensor_tensor(actT[:, f, :], sg[f % 2], bank((2 * f + 1) % 8), ALU.mult).then_inc(s_hid, 1)

            def second_input(t):
                dve.wait_ge(s_row, 16)
                dve.wait_ge(s_res, 8 + T + t + 1)
                dve.wait_ge(s_ss, 9 + t + 1)
                rms_scale(rstd[:, t:t + 1], ss[:, t:t + 1], D)
                dve.scalar_tensor_tensor(out=xres[:, t, :], in0=xres[:, t, :], scalar=rstd[:, t:t + 1], in1=gainrow[:, :],
                                         op0=ALU.mult, op1=ALU.mult).then_inc(s_x2, 1)

            residual(8, len(FK), second_input)
            normed(13)
            tp_out(3, gcols[:, 2 * KD:3 * KD])

            for u, (name, j, t, eng) in enumerate(unitsG):
                if eng != "D":
                    continue
                dve.wait_ge(s_mG, u + 1)
                b = bank(u % 8)
                if name == "a":
                    dve.tensor_copy(alrT[0:RANK, :], b[0:RANK, :]).then_inc(s_gD, 1)
                elif name == "k":
                    dve.tensor_copy(kT[:, t, :], b).then_inc(s_gD, 1)
                else:
                    dve.tensor_copy(gv[:, t, j * 512:(j + 1) * 512], b).then_inc(s_gD, 1)
            zl = max(u for u, v in enumerate(unitsG) if v[0] == "z")
            dve.wait_ge(s_gA, evacs(unitsG, zl))
            dve.wait_ge(s_reset, 1)
            for h in range(GH):
                if h:
                    dve.wait_ge(s_gac, 7 * h)
                dve.scalar_tensor_tensor(out=tmp1, in0=gz[:, h, :], scalar=-1.0, in1=gz[:, h, :], op0=ALU.mult, op1=ALU.min).then_inc(s_gdv, 1)
                dve.wait_ge(s_gac, 7 * h + 2)
                me.link(dve.scalar_tensor_tensor(out=gz[:, h, :], in0=gz[:, h, :], scalar=0.0, in1=tmp1, op0=ALU.min, op1=ALU.subtract))
                me.link(dve.tensor_tensor_scan(gg[:, h, :], reset[:, :], gz[:, h, :], 0.0, ALU.mult, ALU.add))
                g3 = gg[:, h, :].rearrange("p (c s) -> p c s", c=NCH)
                dve.tensor_tensor(D1.rearrange("p (c s) -> p c s", c=NCH), g3, g3[:, :, CH // 2:CH // 2 + 1].to_broadcast([P, NCH, CH]),
                                  ALU.subtract).then_inc(s_gdv, 1)
                dve.tensor_tensor(D2.rearrange("p (c s) -> p c s", c=NCH), g3[:, :, CH - 1:CH].to_broadcast([P, NCH, CH]), g3,
                                  ALU.subtract).then_inc(s_gdv, 1)
            dve.wait_ge(s_gpl, GH)
            for h in range(GH):
                dve.wait_ge(s_gU, 2 * h + 2)
                dve.tensor_tensor(atm[:, h, :, :], bank(4 + h).rearrange("p (t s) -> p t s", t=T),
                                  gmask[:, :].unsqueeze(1).to_broadcast([P, T, P]), ALU.mult).then_inc(s_atm, 1)

            def gla_out(t):
                dve.wait_ge(s_gss, (t + 1) * GH)
                rms_scale(ssg[:, 32 + t * GH:32 + (t + 1) * GH], ssg[:, t * GH:(t + 1) * GH], GV)
                dve.wait_ge(s_gr, t + 1)
                for h in range(GH):
                    n = t * GH + h
                    dve.scalar_tensor_tensor(out=xn[:, t, h * GV:(h + 1) * GV], in0=obank(h, t),
                                             scalar=ssg[:, 32 + n:33 + n], in1=gr[:, t, h * GV:(h + 1) * GV],
                                             op0=ALU.mult, op1=ALU.mult).then_inc(s_go, 1)

            for c in range(NCH):
                if c < NCH - 1:
                    for h in range(GH):
                        dve.wait_ge(s_U, c * GH + (h | 1) + 1)
                        if c >= 1:
                            dve.wait_ge(s_in, (c - 1) * GH + h + 1)
                            dve.wait_ge(s_S2, (c - 1) * GH + h + 1)
                        u = ubank(h, c)
                        if c == 0:
                            dve.tensor_copy(St[:, h, 1, :], u).then_inc(s_S2, 1)
                        else:
                            dve.scalar_tensor_tensor(out=St[:, h, (c + 1) % 2, :], in0=St[:, h, c % 2, :],
                                                     scalar=decay[:, h * NCH + c:h * NCH + c + 1], in1=u,
                                                     op0=ALU.mult, op1=ALU.add).then_inc(s_S2, 1)
                if c >= 3 and c % 2 == 1:
                    gla_out(c // 2 - 1)
            gla_out(T - 1)
            tp_out(4, None)

            def moe_input(t):
                dve.wait_ge(s_row2, 16)
                dve.wait_ge(s_res, 16 + T + t + 1)
                dve.wait_ge(s_ss, 17 + t + 1)
                rms_scale(rstd[:, t:t + 1], ss[:, t:t + 1], D)
                dve.scalar_tensor_tensor(out=xn[:, t, :], in0=xres[:, t, :], scalar=rstd[:, t:t + 1], in1=gainrow[:, :],
                                         op0=ALU.mult, op1=ALU.mult).then_inc(s_hnrow, 1)

            residual(MO_FFN, 1, moe_input)
            tp_out(5, None)

            def over(v, n):
                return v.unsqueeze(1).to_broadcast([v.shape[0], n, v.shape[1]])

            def along(v, n):
                return v.unsqueeze(2).to_broadcast([v.shape[0], v.shape[1], n])

            dve.wait_ge(s_rt, 1)
            me.link(dve.tensor_copy(lg.rearrange("p t n -> p (t n)"), bank(0)[:, 0:T * NR]))
            dve.wait_ge(s_cst, 2)
            for t in range(T):
                me.inc(dve.max(gm8[:, t, :], lg[:, t, 0:GROUPS]))
            me.wait()
            for t in range(T):
                me.inc(dve.max_index(gi_u[:, t * 8:t * 8 + 8], gm8[:, t, :], lg[:, t, 0:GROUPS]))
            me.wait()
            me.link(dve.tensor_copy(gsel, gi_u[:, :].rearrange("p (t n) -> p t n", t=T)[:, :, 0]))
            me.link(dve.tensor_tensor(rtm, over(iog, T), along(gsel, EXPERTS), ALU.is_equal))
            me.link(dve.tensor_tensor(em, lg[:, :, GROUPS:NR], rtm, ALU.mult))
            me.link(dve.tensor_scalar(rtm, rtm, -1.0, -NEG, ALU.add, ALU.mult))
            me.link(dve.tensor_tensor(em, em, rtm, ALU.add))
            for t in range(T):
                me.inc(dve.max(em8[:, t, :], em[:, t, :]))
            me.wait()
            for t in range(T):
                me.inc(dve.max_index(ei_u[:, t * 8:t * 8 + 8], em8[:, t, :], em[:, t, :]))
            me.inc(dve.tensor_scalar(xw[:, 0:T], gm8[:, :, 0], -1.0, None, ALU.mult))
            me.wait()
            dve.tensor_tensor(xw[:, T:2 * T], em8[:, :, 1], em8[:, :, 0], ALU.subtract).then_inc(s_oh, 1)
            me.link(dve.tensor_copy(esel.rearrange("p (k t) -> p t k", k=2), ei_u[:, :].rearrange("p (t n) -> p t n", t=T)[:, :, 0:2]))
            me.link(dve.tensor_tensor(ohall, over(ioe, 2 * T), along(esel, EXPERTS), ALU.is_equal))
            dve.wait_ge(s_oh, 1)
            dve.tensor_tensor(ohs, oh[0], oh[1], ALU.add).then_inc(s_oh, 1)
            me.link(dve.memset(one64, 1.0))
            dve.wait_ge(s_pre, 1)
            me.inc(dve.tensor_copy(pre.rearrange("p t n -> p (t n)"), bank(1)[:, 0:T * EXPERTS]))
            me.link(dve.tensor_copy(cnt, bank(1)[:, T * EXPERTS:(T + 1) * EXPERTS]))
            me.link(dve.tensor_scalar(ob, cnt, C + 0.5, None, ALU.is_ge))
            for q in range(2, QS):
                me.link(dve.scalar_tensor_tensor(out=ob, in0=cnt, scalar=C * q + 0.5, in1=ob, op0=ALU.is_ge, op1=ALU.add))
            me.link(dve.tensor_tensor_scan(obe, one64, ob, 0.0, ALU.mult, ALU.add))
            me.link(dve.tensor_tensor(obs, obe, ob, ALU.subtract))
            dve.wait_ge(s_hnd, 16 * T)
            for k in range(2):
                me.inc(dve.tensor_tensor(ohp[:, k * T:(k + 1) * T, :], oh[k], pre, ALU.mult))
            me.wait()
            me.link(dve.tensor_reduce(rk, ohp, AX, ALU.add))
            me.link(dve.tensor_tensor(ohp, ohall, over(obs, 2 * T), ALU.mult))
            me.link(dve.tensor_reduce(stt, ohp, AX, ALU.add))
            me.inc(dve.tensor_scalar(q1, rk, C - 0.5, None, ALU.is_ge))
            me.link(dve.tensor_scalar(qq, rk, C - 0.5, None, ALU.is_ge))
            for q in range(2, QS):
                me.link(dve.scalar_tensor_tensor(out=qq, in0=rk, scalar=C * q - 0.5, in1=qq, op0=ALU.is_ge, op1=ALU.add))
            me.link(dve.tensor_tensor(bl, stt, qq, ALU.add))
            me.link(dve.scalar_tensor_tensor(out=bl, in0=bl, scalar=EXPERTS - 1.0, in1=esel, op0=ALU.add, op1=ALU.subtract))
            me.link(dve.tensor_tensor(bl, bl, q1, ALU.mult))
            me.inc(dve.tensor_tensor(bl, bl, esel, ALU.add))
            me.inc(dve.scalar_tensor_tensor(out=rk, in0=qq, scalar=-float(C), in1=rk, op0=ALU.mult, op1=ALU.add))
            me.wait()
            me.inc(dve.tensor_tensor(ohw, over(iow, 2 * T), along(rk, C), ALU.is_equal))
            me.link(dve.tensor_tensor(ohb, over(iob, 2 * T), along(bl, NB), ALU.is_equal))
            dve.tensor_tensor(ohb, ohb, along(desf, NB), ALU.mult).then_inc(s_idx, 1)
            dve.wait_ge(s_rte, T + 1)
            x1 = xw[:, T:2 * T]
            me.link(dve.tensor_scalar(gsel, x1, 1.0, None, ALU.add))
            me.link(dve.tensor_tensor(gsel, gsel, gwt, ALU.mult))
            me.link(dve.reciprocal(gates[:, 0:T], gsel))
            me.link(dve.tensor_tensor(gates[:, T:2 * T], gates[:, 0:T], x1, ALU.mult))
            dve.wait_ge(s_tab, 1)
            me.link(dve.tensor_copy(tabf[0:C, :], bank(2)[0:C, 0:NB]))
            me.link(dve.tensor_scalar(tabm[0:C, :], tabf[0:C, :], 0.5, float(SKIP), ALU.is_lt, ALU.mult))
            me.link(dve.scalar_tensor_tensor(out=tabf[0:C, :], in0=tabf[0:C, :], scalar=-1.0, in1=tabm[0:C, :], op0=ALU.add, op1=ALU.add))
            me.inc(dve.tensor_copy(dtab[0:C, :], tabf[0:C, :]))
            me.link(dve.tensor_scalar(tabm[0:C, :], tabf[0:C, :], SEQ - 0.5, -float(SEQ), ALU.is_ge, ALU.mult))
            me.link(dve.tensor_tensor(tabf[0:C, :], tabf[0:C, :], tabm[0:C, :], ALU.add))
            me.inc(dve.tensor_copy(ttab[0:C, :], tabf[0:C, :]))
            me.link(dve.tensor_tensor(ovm[0:1, :, :], over(obe[0:1, :], SPILL), along(ovc[0:1, :], EXPERTS), ALU.is_lt))
            me.link(dve.tensor_reduce(ovf[0:1, 0:SPILL], ovm[0:1, :, :], AX, ALU.add))
            me.inc(dve.tensor_scalar(ovf_i[0:1, 0:SPILL], ovf[0:1, 0:SPILL], EXPERTS - 1.0, None, ALU.min))
            me.inc(dve.tensor_copy(ovf_i[0:1, SPILL:SPILL + 1], obe[0:1, EXPERTS - 1:EXPERTS]))
            me.wait()
            dve.memset(ovf[0:1, 0:1], 0.0).then_inc(s_tabs, 1)

            def hid(b, j):
                dve.wait_ge(s_msl, b + 1)
                wait(dve, s_mhT, b - 1)
                hidden(j)

            def hidden(j):
                for q in range(2):
                    r = slice(q * G2, q * G2 + C)
                    last = dve.tensor_tensor(mhid[j % 2][r, :], msg[j % 2][r, :], bank(2 + j % 2)[r, P:2 * P], ALU.mult)
                last.then_inc(s_mhid, 1)

            def y_out(b, j):
                dve.wait_ge(s_my, b + 1)
                if not isinstance(b, int) or b >= 2:
                    dve.wait_ge(s_ys[j % 2], (b - j % 2) * 8)
                dve.tensor_copy(ye[j % 2][0:C, 512:1024], bank(6 + j % 2)[G2:G2 + C, :]).then_inc(s_myD, 1)

            def hT_out(b, j):
                dve.wait_ge(s_mhT, b + 1)
                wait(dve, s_my, b - 1)
                dve.tensor_copy(mhT[j % 2], hbanks).then_inc(s_mhTe, 1)

            def block_(base, j, first):
                hid(base + j, j)
                if not first:
                    y_out(base + j - 1, j - 1)
                hT_out(base + j, j)

            for j in range(E_SLOTS):
                block_(0, j, j == 0)
            with dve.Fori(1, EXPERTS // E_SLOTS) as it:
                for j in range(E_SLOTS):
                    block_(it * E_SLOTS, j, False)
            y_out(EXPERTS - 1, E_SLOTS - 1)
            n_over = dve.value_load(ovf_i[0:1, SPILL:SPILL + 1], min_val=0, max_val=SPILL)
            with dve.If(n_over > 0):
                with dve.Fori(0, n_over) as i:
                    dve.wait_ge(s_msl, i + (EXPERTS + 1))
                    hidden(0)
                    dve.wait_ge(s_mhT, i + (EXPERTS + 1))
                    dve.tensor_copy(mhT[0], hbanks).then_inc(s_mhTe, 1)
                    dve.wait_ge(s_my, i + (EXPERTS + 1))
                    dve.wait_ge(s_ys[0], i * 16 + 8 * EXPERTS)
                    dve.tensor_copy(ye[0][0:C, 512:1024], bank(6)[G2:G2 + C, :]).then_inc(s_myD, 1)

            dve.wait_ge(s_row2, 32)
            yv = big[:, 0:2 * T * D].rearrange("p (k t d) -> p k t d", k=2, t=T)
            for t in range(T):
                dve.wait_ge(s_yl[t], 32)
                me.link(dve.scalar_tensor_tensor(out=xres[:, t, :], in0=yv[:, 0, t, :], scalar=gates[:, t:t + 1], in1=xres[:, t, :],
                                                 op0=ALU.mult, op1=ALU.add))
                dve.scalar_tensor_tensor(out=xres[:, t, :], in0=yv[:, 1, t, :], scalar=gates[:, T + t:T + t + 1], in1=xres[:, t, :],
                                         op0=ALU.mult, op1=ALU.add).then_inc(s_x2, 1)
            for t in range(T):
                dve.wait_ge(s_x2, T + t + 1)
                dve.wait_ge(s_ss, 21 + t + 1)
                rms_scale(rstd[:, t:t + 1], ss[:, t:t + 1], D)
                dve.scalar_tensor_tensor(out=xres[:, t, :], in0=xres[:, t, :], scalar=rstd[:, t:t + 1], in1=gainrow[:, :],
                                         op0=ALU.mult, op1=ALU.mult).then_inc(s_fin, 1)

        @block.gpsimd
        def _(pool):
            me = Count(pool, s_pool)
            me.inc(pool.memset(ident[:, :], 0.0))
            me.inc(pool.memset(tri[:, :], 1.0))
            me.inc(pool.memset(strict[:, :], 1.0))
            me.inc(pool.memset(ones[:, :], 1.0))
            me.inc(pool.memset(amask[:, :], 0.0))
            me.inc(pool.memset(gmask[:, :], 1.0))
            me.inc(pool.memset(half[:, :], -0.5))
            me.wait()
            one_row = [[1, P]]
            me.inc(pool.affine_select(out=ident[:, :], in_=ident[:, :], compare_op=ALU.not_equal, fill=1.0, base=0,
                                      pattern=[[-1, P]], channel_multiplier=1))
            me.inc(pool.affine_select(out=tri[:, :], in_=tri[:, :], compare_op=ALU.is_ge, fill=0.0, base=0,
                                      pattern=one_row, channel_multiplier=-1))
            me.inc(pool.affine_select(out=strict[:, :], in_=strict[:, :], compare_op=ALU.is_gt, fill=0.0, base=0,
                                      pattern=one_row, channel_multiplier=-1))
            me.inc(pool.affine_select(out=amask[:, :], in_=amask[:, :], compare_op=ALU.is_ge, fill=NEG, base=0,
                                      pattern=[[-1, P]], channel_multiplier=1))
            me.inc(pool.affine_select(out=gmask[:, :], in_=gmask[:, :], compare_op=ALU.is_ge, fill=0.0, base=0,
                                      pattern=one_row, channel_multiplier=-1))
            me.wait()
            me.inc(pool.memset(gmask[0:CH, CH:P], 0.0))
            me.wait()
            pool.memset(ss[:, 7:8], 0.0).then_inc(s_cst, 1)

            rooted = Count(pool, s_pw)

            def root(v):
                pool.wait_ge(s_ms, rooted.n + 1)
                rooted.inc(pool.tensor_tensor(v, v, half[0:v.shape[0], 0:v.shape[1]], ALU.pow))

            def row_roots():
                for t in range(T):
                    root(rstd[:, t:t + 1])

            row_roots()
            root(rstd[0:META, T:T + 1])

            H = HEADS
            pool.wait_ge(s_rs, 9)
            for b in range(2):
                me.inc(pool.memset(qa[b][:, :, HD:HD + 1], 1.0))
                me.inc(pool.memset(ka[b][:, :, HD + 1:HA], 1.0))
                me.inc(pool.memset(kam[b][0:META, HD + 1:HA], 1.0))
            root(rsq[:, 0:8 * H])
            root(rsq[0:META, 8 * H:])
            pool.wait_ge(s_c, 1)
            rq = rsq[:, 0:4 * H].rearrange("p (t h) -> p t h", t=T)
            rk_ = rsq[:, 4 * H:8 * H].rearrange("p (t h) -> p t h", t=T)
            c3 = cc[:, 0:T * H].rearrange("p (t h) -> p t h", t=T)
            n3 = ncc[:, 0:T * H].rearrange("p (t h) -> p t h", t=T)
            for h in range(H):
                if h >= 2:
                    pool.wait_ge(s_qkt, 3 * (h - 1))
                b = h % 2
                pool.tensor_tensor(qa[b][:, :, 0:HD], qkvg[:, :, h * HD:(h + 1) * HD],
                                   rq[:, :, h:h + 1].to_broadcast([P, T, HD]), ALU.mult)
                pool.tensor_copy(qa[b][:, :, HD + 1:HA], c3[:, :, h:h + 1])
                pool.tensor_tensor(ka[b][:, :, 0:HD], qkvg[:, :, D + h * HD:D + (h + 1) * HD],
                                   rk_[:, :, h:h + 1].to_broadcast([P, T, HD]), ALU.mult)
                pool.tensor_copy(ka[b][:, :, HD:HD + 1], n3[:, :, h:h + 1])
                pool.tensor_tensor(kam[b][0:META, 0:HD], mkv[0:META, h * HD:(h + 1) * HD],
                                   rsq[0:META, 8 * H + h:8 * H + h + 1].to_broadcast([META, HD]), ALU.mult)
                pool.tensor_copy(kam[b][0:META, HD:HD + 1], ncc[0:META, T * H + h:T * H + h + 1]).then_inc(s_stage, 1)

            for _ in range(3):
                row_roots()

            pool.wait_ge(s_x2, T)
            pool.dma_start(gainrow[:, :], ffn_norm_2.to_broadcast([P, D])).then_inc(s_row2, 16)

            pool.wait_ge(s_tp, KD * 4 + 1)
            me.link(pool.memset(reset[:, :], 1.0))
            pool.memset(reset[:, :].rearrange("p (c s) -> p c s", c=NCH)[:, :, 0:1], 0.0).then_inc(s_reset, 1)

            kl = max(u for u, v in enumerate(unitsG) if v[0] == "k")
            pool.wait_ge(s_gD, evacs(unitsG, kl))
            for h in range(GH):
                pool.wait_ge(s_gac, 7 * h + 7)
                me.inc(pool.tensor_tensor(qiT[:, h, :], qT[:, h, :], Ex[2], ALU.mult))
                me.inc(pool.tensor_tensor(ksT[:, h, :], kT[:, h, :], Ex[3], ALU.mult))
                me.wait()
                pool.tensor_tensor(qT[:, h, :], qT[:, h, :], Ex[0], ALU.mult)
                pool.tensor_tensor(kT[:, h, :], kT[:, h, :], Ex[1], ALU.mult).then_inc(s_gpl, 1)
            for t in range(T):
                pool.wait_ge(s_er, 2 * t + 2)
                v = gr[:, t, :].rearrange("p (h n) -> p h n", h=GH)
                pool.tensor_tensor(v, v, outn[:, :].unsqueeze(1).to_broadcast([P, GH, GV]), ALU.mult).then_inc(s_gr, 1)
                root(ssg[:, 32 + t * GH:32 + (t + 1) * GH])

            row_roots()
            for t in range(T):
                pool.wait_ge(s_hnrow, t + 1)
                pool.dma_start(hn_dram[t * P:(t + 1) * P, :], xn[:, t, :]).then_inc(s_hnd, 16)
            pool.dma_start(gainrow[:, :], final_norm_2.rearrange("(a n) -> a n", a=1).to_broadcast([P, D])).then_inc(s_row2, 16)

            pool.wait_ge(s_tp, KD * 5 + 1)
            small = dict(base=0, allow_small_or_imprecise_dtypes=True)
            me.inc(pool.iota(desf.rearrange("p (k t) -> p k t", k=2), pattern=[[SEQ, 2], [P, T]], channel_multiplier=1, base=1,
                             allow_small_or_imprecise_dtypes=True))
            me.inc(pool.iota(iog, pattern=[[1, GROUPS], [0, PER]], channel_multiplier=0, **small))
            me.inc(pool.iota(ioe, pattern=[[1, EXPERTS]], channel_multiplier=0, **small))
            me.inc(pool.iota(iob, pattern=[[1, NB]], channel_multiplier=0, **small))
            me.inc(pool.iota(iow, pattern=[[1, C]], channel_multiplier=0, **small))
            me.link(pool.iota(ovc, pattern=[[1, SPILL]], channel_multiplier=0, **small))
            pool.tensor_scalar(ovc, ovc, 0.5, None, ALU.add).then_inc(s_cst, 1)
            pool.wait_ge(s_rt, 1)
            for i in range(4):
                pool.memset(xe[i], 0.0).then_inc(s_xz, 1)
            pool.wait_ge(s_tabs, 1)
            pool.wait_ge(s_hnd, 16 * T)
            pool.wait_ge(s_xz, 4)
            bound_x = pool.to_reg(SEQ - 1)
            bound_y = pool.to_reg(ASG - 1)

            def gather(b, j, n):
                j = j % 4
                wait(pool, s_mx1, b - 3)
                col = ttab[0:C, b:b + 1] if isinstance(b, int) else ttab[0:C, bass.ds(b, 1)]
                pool.tensor_copy(gidx[0:C, j:j + 1], col).then_inc(s_ic, 1)
                pool.wait_ge(s_ic, n)
                pool.sem_inc(s_tick, 1)
                pool.indirect_dma_start(out=xe[j][0:C, :], out_offset=None, in_=hn_dram[:, :],
                                        in_offset=bass.IndirectOffsetOnAxis(ap=gidx[0:C, j:j + 1], axis=0),
                                        bounds_check=bound_x, oob_is_err=False).then_inc(s_xe[j], 16)

            def scatter(b, j, n):
                j = j % 4
                col = dtab[0:C, b:b + 1] if isinstance(b, int) else dtab[0:C, bass.ds(b, 1)]
                pool.tensor_copy(sidx[0:C, j:j + 1], col).then_inc(s_ic, 1)
                pool.wait_ge(s_ic, n)
                pool.wait_ge(s_myA, b + 1)
                pool.wait_ge(s_myD, b + 1)
                pool.sem_inc(s_tick, 1)
                pool.indirect_dma_start(out=y_dram[:, :], out_offset=bass.IndirectOffsetOnAxis(ap=sidx[0:C, j:j + 1], axis=0),
                                        in_=ye[j % 2][0:C, :], in_offset=None,
                                        bounds_check=bound_y, oob_is_err=False).then_inc(s_ys[j % 2], 16)

            gather(0, 0, 1)
            gather(1, 1, 2)
            n = 2
            for j in range(E_SLOTS):
                n += 1
                gather(j + 2, j + 2, n)
                if j:
                    n += 1
                    scatter(j - 1, j - 1, n)
            with pool.Fori(1, EXPERTS // E_SLOTS) as it:
                for j in range(E_SLOTS):
                    gather(it * E_SLOTS + (j + 2), j + 2, it * (2 * E_SLOTS) + (2 * j + 2))
                    scatter(it * E_SLOTS + (j - 1), j - 1, it * (2 * E_SLOTS) + (2 * j + 3))
            scatter(EXPERTS - 1, E_SLOTS - 1, 2 * EXPERTS + 2)
            n_ic = 2 * EXPERTS + 2
            n_over = pool.value_load(ovf_i[0:1, SPILL:SPILL + 1], min_val=0, max_val=SPILL)
            with pool.If(n_over > 0):
                with pool.Fori(0, n_over) as i:
                    pool.wait_ge(s_mx1, i + (EXPERTS + 1))
                    pool.tensor_copy(gidx[0:C, 0:1], ttab[0:C, bass.ds(i + EXPERTS, 1)]).then_inc(s_ic, 1)
                    pool.wait_ge(s_ic, i * 2 + (n_ic + 1))
                    pool.sem_inc(s_tick, 1)
                    pool.indirect_dma_start(out=xe[0][0:C, :], out_offset=None, in_=hn_dram[:, :],
                                            in_offset=bass.IndirectOffsetOnAxis(ap=gidx[0:C, 0:1], axis=0),
                                            bounds_check=bound_x, oob_is_err=False).then_inc(s_xe[0], 16)
                    pool.tensor_copy(sidx[0:C, 0:1], dtab[0:C, bass.ds(i + EXPERTS, 1)]).then_inc(s_ic, 1)
                    pool.wait_ge(s_ic, i * 2 + (n_ic + 2))
                    pool.wait_ge(s_myA, i + (EXPERTS + 1))
                    pool.wait_ge(s_myD, i + (EXPERTS + 1))
                    pool.sem_inc(s_tick, 1)
                    pool.indirect_dma_start(out=y_dram[:, :], out_offset=bass.IndirectOffsetOnAxis(ap=sidx[0:C, 0:1], axis=0),
                                            in_=ye[0][0:C, :], in_offset=None,
                                            bounds_check=bound_y, oob_is_err=False).then_inc(s_ys[0], 16)
                    pool.wait_ge(s_ys[0], i * 16 + (8 * EXPERTS + 16))
            pool.wait_ge(s_ys[0], 8 * EXPERTS)
            pool.wait_ge(s_ys[1], 8 * EXPERTS)
            pool.wait_ge(s_my, EXPERTS)
            for t in range(T):
                for k in range(2):
                    o = (k * T + t) * D
                    pool.dma_start(big[:, o:o + D], y_dram[k * SEQ + t * P:k * SEQ + (t + 1) * P, :]).then_inc(s_yl[t], 16)
            row_roots()


_INS = ['x', 'meta_tokens', 'attn_norm', 'ffn_norm', 'final_norm', 'fox_w_in', 'fox_b_f', 'fox_q_norm', 'fox_k_norm',
        'fox_w_out', 'ffn_w_in', 'ffn_w_out', 'attn_norm_2', 'ffn_norm_2', 'final_norm_2', 'gla_w_in_2',
        'gla_w_gate_2', 'gla_b_gate_2', 'gla_out_norm_2', 'gla_w_o_2', 'moe_w_group_2', 'moe_w_expert_2',
        'moe_w1_2', 'moe_w3_2', 'moe_w2_2']


def kernel(**inputs):
    import numpy as _np
    import concourse.bacc as _bacc
    from concourse import mybir as _mybir
    from concourse.bass_utils import run_bass_kernel_spmd as _run

    nc = _bacc.Bacc("TRN2", target_bir_lowering=False, num_devices=1)
    arrays, args = {}, []
    for name in _INS:
        a = _np.ascontiguousarray(inputs[name])
        arrays[f"in_{name}_dram"] = a
        args.append(nc.dram_tensor(f"in_{name}_dram", a.shape, _mybir.dt.from_np(a.dtype), kind="ExternalInput").ap())
    args.append(nc.dram_tensor("out_0_dram", inputs["x"].shape, _mybir.dt.float32, kind="ExternalOutput").ap())
    program(nc, *args)
    r = _run(nc, [arrays], core_ids=[0])
    return r.results[0]["out_0_dram"]
```

```python
from contextlib import ExitStack

import concourse.bass as bass
from concourse import mybir

F32 = mybir.dt.float32
F32R = mybir.dt.float32r
I32 = mybir.dt.int32
U32 = mybir.dt.uint32
ALU = mybir.AluOpType
ACT = mybir.ActivationFunctionType
AX = mybir.AxisListType.X

P = 128
EPS = 1e-6
NEG = -1e30
W_SLOTS = 2
CK_SLOTS = 4
C = 32
E_SLOTS = 4
SKIP = 1 << 20


class Count:

    def __init__(self, eng, sem):
        self.eng, self.sem, self.n = eng, sem, 0

    def inc(self, ins):
        self.n += 1
        return ins.then_inc(self.sem, 1)

    def wait(self):
        self.eng.wait_ge(self.sem, self.n)

    def link(self, ins):
        self.inc(ins)
        self.wait()


def wait(eng, sem, value):
    if not isinstance(value, int) or value > 0:
        eng.wait_ge(sem, value)


def program(nc, x, meta_tokens, attn_norm, ffn_norm, final_norm, fox_w_in, fox_b_f, fox_q_norm, fox_k_norm,
            fox_w_out, ffn_w_in, ffn_w_out, attn_norm_2, ffn_norm_2, final_norm_2, gla_w_in, gla_w_gate,
            gla_b_gate, gla_out_norm, gla_w_o, moe_w_group, moe_w_expert, moe_w1, moe_w3, moe_w2, out):
    _, SEQ, D = x.shape
    META = meta_tokens.shape[0]
    T = SEQ // P
    KD = D // P
    HEADS = fox_b_f.shape[1]
    HD = D // HEADS
    HA = HD + 2
    FH = ffn_w_out.shape[1]
    FT = FH // P
    GH = 4
    GK = gla_w_gate.shape[2] // GH
    GV = gla_out_norm.shape[1]
    RANK = gla_w_gate.shape[1]
    QK = GH * GK
    CH = 64
    NCH = SEQ // CH
    TAU = 16.0
    GROUPS = moe_w_group.shape[2]
    EXPERTS = moe_w_expert.shape[2]
    PER = EXPERTS // GROUPS
    FF = moe_w1.shape[3]
    KF = FF // P
    ASG = 2 * SEQ
    SPILL = (ASG - 1) // C
    NB = EXPERTS + SPILL
    G2 = 64
    assert (META, HD, GK, GV, KF) == (16, 64, 128, 256, 2) and KD == 8 and T == 4

    hn_dram = nc.dram_tensor("hn_dram", [SEQ, D], F32)
    y_dram = nc.dram_tensor("y_dram", [ASG, D], F32)

    with ExitStack() as ctx:
        def sb(name, cols, dt=F32):
            return ctx.enter_context(nc.sbuf_tensor(name, [P, cols], dt))

        def sem(name):
            return ctx.enter_context(nc.semaphore(name))

        ps = ctx.enter_context(nc.psum_tensor("ps", [P, 8 * 512], F32))

        def bank(b, n=1):
            return ps[:, b * 512:(b + n) * 512]

        def with_halves(name, cols, at, n):
            plain = sb(name, cols)
            return plain, nc.alloc_sbuf_tensor_at(name + "_halves", [P, n], F32R, offset=nc.sbuf_base - 4 * (cols - at))

        wring, wsplit = with_halves("wring", W_SLOTS * 4096 + CK_SLOTS * 1024, W_SLOTS * 4096, CK_SLOTS * 1024)
        big, bigr = with_halves("big", 16384, 0, 16384)
        xres_t = sb("xres", T * D)
        hT_t, hTr = with_halves("hT", KD * SEQ, 0, KD * SEQ)
        xn_t = sb("xn", T * D)
        mkv = sb("mkv", 2 * D)
        arena, hTm2 = with_halves("arena", 6144, 3328, 2 * KD * META)
        gainrow = sb("gainrow", D)
        gcols = sb("gcols", 3 * KD)
        outn = sb("outn", GV)
        qgain = sb("qgain", 1)
        kgain = sb("kgain", 1)
        bf = sb("bf", HEADS)
        bgate = sb("bgate", GH)
        wgate = sb("wgate", QK)
        ident = sb("ident", P)
        tri = sb("tri", P)
        strict = sb("strict", P)
        ones = sb("ones", P)
        amask = sb("amask", P)
        gmask = sb("gmask", P)
        ss = sb("ss", 8)
        rstd = sb("rstd", 8)
        ssq = sb("ssq", 9 * HEADS)
        rsq = sb("rsq", 9 * HEADS)
        zf = sb("zf", 5 * HEADS)
        zt = sb("zt", 5 * HEADS)
        cc = sb("cc", 5 * HEADS)
        ncc = sb("ncc", 5 * HEADS)
        mxn = sb("mxn", 2 * 64)
        rsum = sb("rsum", 64)
        rinv = sb("rinv", 64)
        decay = sb("decay", GH * NCH)
        ssg = sb("ssg", 3 * GH * T)
        half = sb("half", 2 * GH)

        alrT = xn_t[:, 0:SEQ]
        reset = xn_t[:, SEQ:2 * SEQ]
        xres = xres_t[:, :].rearrange("p (t d) -> p t d", t=T)
        hT = wring[:, W_SLOTS * 4096:].rearrange("p (k s) -> p k s", k=KD)
        hTh = [hTr[:, k * SEQ:(k + 1) * SEQ] for k in range(KD)]
        xn = xn_t[:, :].rearrange("p (t d) -> p t d", t=T)
        hTm = big[:, 2 * D:2 * D + KD * META].rearrange("p (k s) -> p k s", k=KD)
        hTm_h, hTm_l = (hTm2[:, i * KD * META:(i + 1) * KD * META].rearrange("p (k s) -> p k s", k=KD) for i in range(2))
        qkvg = big[:, :].rearrange("p (t n) -> p t n", t=T)
        metax = big[0:META, 0:D]
        metan = big[0:META, D:2 * D]

        at = [0]

        def part(n):
            at[0] += n
            return arena[:, at[0] - n:at[0]]

        qa = [part(T * HA).rearrange("p (t d) -> p t d", t=T) for _ in range(2)]
        ka = [part(T * HA).rearrange("p (t d) -> p t d", t=T) for _ in range(2)]
        kam = [part(HA) for _ in range(2)]
        QT = [part(SEQ) for _ in range(2)]
        KT = [part(META + SEQ) for _ in range(2)]
        Pb = [part(META + SEQ) for _ in range(3)]
        PT = [part(5 * P) for _ in range(2)]
        scr = [arena[:, 4096:5120], arena[:, 5120:6144]]
        newton = arena[:, 4096:4096 + 9 * HEADS]
        sg = [arena[:, 0:512], arena[:, 512:1024]]
        prod = [arena[:, 1024:1536], arena[:, 1536:2048]]
        FA = FT // 4 * 2 + 2
        act_h = [bigr[:, f * SEQ:(f + 1) * SEQ] for f in range(FA)]
        act_l = [bigr[:, (FA + f) * SEQ:(FA + f + 1) * SEQ] for f in range(FA)]
        hTl_first = [bigr[:, (k // 2) * 4 * D + 3 * D + (k % 2) * SEQ:(k // 2) * 4 * D + 3 * D + (k % 2 + 1) * SEQ] for k in range(KD)]
        hTl_later = [bigr[:, 12288 + k * SEQ:12288 + (k + 1) * SEQ] for k in range(KD)]

        qT = big[:, 0:2048].rearrange("p (h s) -> p h s", h=GH)
        kT = big[:, 2048:4096].rearrange("p (h s) -> p h s", h=GH)
        gz = big[:, 4096:6144].rearrange("p (h s) -> p h s", h=GH)
        gg = big[:, 6144:8192].rearrange("p (h s) -> p h s", h=GH)
        gv = big[:, 8192:12288].rearrange("p (t n) -> p t n", t=T)
        gr = big[:, 12288:16384].rearrange("p (t n) -> p t n", t=T)
        qiT, ksT = gz, gg
        kst = mkv[:, :].rearrange("p (h t d) -> p h t d", h=GH, t=T)
        tmp1 = arena[:, 0:512]
        D1, D2 = arena[:, 1024:1536], arena[:, 1536:2048]
        Ex = [arena[:, 2048 + 512 * i:2560 + 512 * i] for i in range(4)]
        atm = arena[:, 0:2048].rearrange("p (h t s) -> p h t s", h=GH, t=T)
        St = arena[:, 4096:6144].rearrange("p (h b v) -> p h b v", h=GH, b=2)

        s_w = [sem(f"weights_in_{i}") for i in range(W_SLOTS)]
        s_hi = sem("chunk_high_half")
        s_lo = sem("chunk_low_half")
        s_ck = sem("chunk_used")
        s_hf = sem("halves_summed")
        s_act = sem("hidden_split")
        s_x = [sem(f"x_in_{t}") for t in range(T)]
        s_meta = sem("meta_in")
        s_small = sem("small_in")
        s_gain = sem("first_gain_in")
        s_row = sem("gainrow_in")
        s_row2 = sem("later_gainrow_in")
        s_cst = sem("constants_made")
        s_pool = sem("pool_self")
        s_ms = sem("mean_square_ready")
        s_pw = sem("root_taken")
        s_dve = sem("dve_self")
        s_act = sem("act_self")
        s_ss = sem("squares_summed")
        s_xn = sem("normed")
        s_tp = sem("transposed")
        s_tpA = sem("transposed_out_act")
        s_tpD = sem("transposed_out_dve")
        s_mB = sem("proj_done")
        s_eA = sem("proj_out_act")
        s_eD = sem("proj_out_dve")
        s_mg = sem("gate_proj_done")
        s_eg = sem("gate_proj_out")
        s_sig = sem("gate_sigmoid")
        s_og = sem("attn_gated")
        s_sqh = sem("head_squares")
        s_rs = sem("head_rstd")
        s_hr = sem("head_roots")
        s_lf = sem("forget_log")
        s_c = sem("decay_ready")
        s_stage = sem("head_staged")
        s_qkt = sem("head_transposed")
        s_qkA = sem("head_qT_ready")
        s_S = sem("scores_ready")
        s_mx = sem("row_max_ready")
        s_exp = sem("probs_ready")
        s_T = sem("probs_transposed")
        s_ptA = sem("probsT_out_act")
        s_pv = sem("pv_done")
        s_o = sem("attn_out_ready")
        s_mO = sem("outproj_done")
        s_res = sem("residual_added")
        s_mH = sem("gate_up_done")
        s_silu = sem("silu_done")
        s_hid = sem("hidden_ready")
        s_x2 = sem("x2_ready")
        s_mG = sem("gla_proj_done")
        s_gA = sem("gla_proj_out_act")
        s_gD = sem("gla_proj_out_dve")
        s_mr = sem("gla_gate_done")
        s_er = sem("gla_gate_silu")
        s_gdv = sem("gla_dve_step")
        s_gac = sem("gla_act_step")
        s_gpl = sem("gla_pool_step")
        s_gq = sem("gla_q_decayed")
        s_gr = sem("gla_gate_gained")
        s_reset = sem("chunk_starts_set")
        s_gU = sem("gla_units")
        s_kst = sem("k_state_ready")
        s_atm = sem("attn_masked")
        s_U = sem("state_update_ready")
        s_S2 = sem("state_ready")
        s_in = sem("chunk_out_done")
        s_gss = sem("gla_squares")
        s_go = sem("gla_out_ready")
        s_hnrow = sem("moe_input_ready")
        s_hnd = sem("moe_input_stored")
        s_rt = sem("router_logits")
        s_rte = sem("router_exp")
        s_lgT = sem("router_logitsT_out")
        s_lg = sem("router_logits_by_token")
        s_oh = sem("one_hots_ready")
        s_pre = sem("prefix_ready")
        s_idx = sem("slots_ready")
        s_tab = sem("slot_table_in")
        s_tabs = sem("tables_ready")
        s_xz = sem("xe_zeroed")
        s_ew = [sem(f"expert_in_{i}") for i in range(E_SLOTS)]
        s_xe = [sem(f"tokens_in_{i}") for i in range(E_SLOTS)]
        s_ic = sem("index_copied")
        s_mx1 = sem("moe_xT")
        s_mxA = sem("moe_xT_out_act")
        s_gu = sem("moe_gate_up")
        s_msl = sem("moe_silu")
        s_mhid = sem("moe_hidden")
        s_mhT = sem("moe_hiddenT")
        s_mhTe = sem("moe_hiddenT_out")
        s_my = sem("moe_y")
        s_myA = sem("moe_y_out_act")
        s_myD = sem("moe_y_out_dve")
        s_ys = [sem(f"y_stored_{i}") for i in range(2)]
        s_yl = [sem(f"y_loaded_{t}") for t in range(T)]
        s_tick = sem("waits_taken")
        s_fin = sem("final_ready")
        s_out = sem("out_stored")

        W0 = fox_w_in[0].rearrange("(k p) n -> p k n", p=P)
        WO = fox_w_out[0].rearrange("(k p) n -> p k n", p=P)
        WI = ffn_w_in[0].rearrange("(k p) n -> p k n", p=P)
        W2 = ffn_w_out[0].rearrange("(k p) n -> p k n", p=P)
        WG = gla_w_in[0].rearrange("(k p) n -> p k n", p=P)
        WGO = gla_w_o[0].rearrange("(k p) n -> p k n", p=P)
        tiles, tile_at, tile_ready = [], {}, {}
        slot_count = [0] * W_SLOTS
        chunks, chunk_at = [], {}
        released = []
        n_ck = [0]

        def add_tile(name, cols, parts, release=None, ends=None):
            w = len(tiles)
            slot = w % W_SLOTS
            k = max(a + n for a, n, _, _ in parts)
            view = wring[:, slot * 4096:slot * 4096 + k * cols].rearrange("p (k n) -> p k n", k=k)
            slot_count[slot] += 16 * len(parts)
            if release is None:
                chunk_at[name] = len(chunks)
                for c in range(k if cols == 512 else 1):
                    chunks.append((name, c) if cols == 512 else (name, None))
                    if ends is None or c < k - 1 and cols == 512:
                        n_ck[0] += 1
                        released.append((s_ck, n_ck[0]))
                    else:
                        released.append(ends)
                release = (s_lo, len(chunks))
            tiles.append((slot, [(view[:, a:a + n, c:c + s.shape[2]], s) for a, n, c, s in parts], release))
            tile_at[name], tile_ready[name] = view, (s_w[slot], slot_count[slot])

        unitsB = []
        for name, c0, n in (("k", D, 2), ("q", 0, 2), ("f", 4 * D, 1), ("v", 2 * D, 2), ("g", 3 * D, 2)):
            for j in range(n):
                if name == "f":
                    unitsB.append((name, j, 0, "D"))
                elif name == "v" and j == 1:
                    unitsB.append(("c", 0, 0, "D"))
                if name != "f":
                    for t in range(T + (name in "kv")):
                        if name != "g":
                            unitsB.append((name, j, t, "AD"[t % 2]))
                cols = HEADS if name == "f" else 512
                parts = [(0, KD, 0, W0[:, :, c0 + j * 512:c0 + j * 512 + cols])]
                if name == "g":
                    add_tile(f"{name}{j}", cols, parts, release=(s_mg, T * (j + 1)))
                else:
                    add_tile(f"{name}{j}", cols, parts, ends=(s_mB, len(unitsB)))
        attn_end = len(chunks)
        for j in range(2):
            add_tile(f"wo{j}", 512, [(0, KD, 0, WO[:, :, j * 512:(j + 1) * 512])], ends=(s_mO, 4 * (j + 1)))
        wo_end = len(chunks)
        n_ck[0] -= CK_SLOTS - 1
        n_out = 8
        halves = [(0, FA), (FA, FT)]
        out_tiles = {}
        for f0, f1 in halves:
            for j in range(f0 // 2, f1 // 2):
                add_tile(f"in{j}", 512, [(0, KD, 0, WI[:, :, j * 256:(j + 1) * 256]),
                                         (0, KD, 256, WI[:, :, FH + j * 256:FH + (j + 1) * 256])], ends=(s_mH, 2 * (j + 1)))
            for j in range(2):
                n_out += 4
                out_tiles[f0, j] = []
                for a in range(f0, f1, 8):
                    n = min(8, f1 - a)
                    add_tile(f"out{j}_{a}", 512, [(0, n, 0, W2[:, a:a + n, j * 512:(j + 1) * 512])],
                             ends=(s_mO, n_out) if a + n == f1 else None)
                    out_tiles[f0, j].append((f"out{j}_{a}", a, n))
        ffn_end = len(chunks)
        n_ck[0] -= CK_SLOTS - 1
        unitsG = []
        for name, c0, n in (("a", 2 * QK + D, 1), ("q", 0, 1), ("k", QK, 1), ("v", 2 * QK, 2), ("r", 2 * QK + D + RANK, 2)):
            for j in range(n):
                if name == "a":
                    unitsG.append((name, 0, 0, "D"))
                elif name != "r":
                    for t in range(T):
                        unitsG.append((name, j, t, {"q": "A", "k": "D", "v": "D"}[name]))
                cols = RANK if name == "a" else 512
                parts = [(0, KD, 0, WG[:, :, c0 + j * 512:c0 + j * 512 + cols])]
                if name == "r":
                    add_tile(f"g{name}{j}", cols, parts, release=(s_mr, 2 * T - 1 + j))
                else:
                    add_tile(f"g{name}{j}", cols, parts, ends=(s_mG, len(unitsG)))
                if name == "q":
                    unitsG += [("z", 0, h, "A") for h in range(GH)]
        gla_end = len(chunks)
        for j in range(2):
            add_tile(f"gwo{j}", 512, [(0, KD, 0, WGO[:, :, j * 512:(j + 1) * 512])],
                     ends=(s_mO, n_out + 4 * (j + 1)))
        NR = GROUPS + EXPERTS
        add_tile("rt", NR, [(0, KD, 0, moe_w_group[0].rearrange("(k p) n -> p k n", p=P)),
                            (0, KD, GROUPS, moe_w_expert[0].rearrange("(k p) n -> p k n", p=P))], release=(s_rt, 1))

        NORMS = [(0, 0)] + [v for t in range(1, T) for v in ((0, t), (1, t - 1))] + [(1, T - 1)]

        def last_together(end):
            for c in range(end - CK_SLOTS, end):
                released[c] = released[end - 1]

        def chunk_views(c):
            name, k = chunks[c]
            src = tile_at[name] if k is None else tile_at[name][:, k, :]
            o = (c % CK_SLOTS) * 1024
            if k is None:
                n = src.shape[1] * src.shape[2]
                return (src,) + tuple(wsplit[:, o + i * 512:o + i * 512 + n].rearrange("p (k n) -> p k n", k=src.shape[1]) for i in range(2))
            return src, wsplit[:, o:o + 512], wsplit[:, o + 512:o + 1024]

        for end in (wo_end, ffn_end, len(chunks)):
            last_together(end)

        def high_half(act, c):
            name, k = chunks[c]
            src, hi, _ = chunk_views(c)
            if c == chunk_at[name]:
                act.wait_ge(*tile_ready[name])
            if c >= CK_SLOTS:
                act.wait_ge(*released[c - CK_SLOTS])
            if c == attn_end:
                act.wait_ge(s_mg, 2 * T)
            if c == gla_end:
                act.wait_ge(s_mr, 2 * T)
            act.copy(hi, src).then_inc(s_hi, 1)

        def low_half(pool, c):
            src, hi, lo = chunk_views(c)
            pool.wait_ge(s_hi, c + 1)
            pool.tensor_tensor(lo, src, hi, ALU.subtract).then_inc(s_lo, 1)

        F_ACT = [2 * KD - 1, 2 * KD + 5, 3 * KD + 1, 3 * KD + 5]
        F_POOL = [2 * KD + 4, 3 * KD, 3 * KD + 4]

        def obank(h, t):
            b = (t % 2) * 2 + h // 2
            return bank(b)[:, (h % 2) * GV:(h % 2 + 1) * GV]

        def ubank(h, c):
            return bank(4 + h // 2)[:, (h % 2) * GV:(h % 2 + 1) * GV]

        def evacs(units, u):
            return sum(v[3] == units[u][3] for v in units[:u + 1])

        def tile_wait(pe, name):
            s, n = tile_ready[name]
            pe.wait_ge(s, n)

        def sbank(s, a, b):
            return ps[:, 512 * (s % 2) + a:512 * (s % 2) + b]

        PTB, OB, GB, QB = 3 * 512, 5, 6, 7

        block = ctx.enter_context(nc.Block())

        def eslot(i):
            base = (big if i < 2 else wring)[:, (i % 2) * 6144:(i % 2) * 6144 + 6144]
            return (base[:, 0:4096].rearrange("p (g k n) -> p g k n", g=2, k=KD),
                    base[:, 4096:6144].rearrange("p (k n) -> p k n", k=KF))

        W1 = moe_w1[0].rearrange("e (p k) n -> e p (k n)", k=KD)
        W3 = moe_w3[0].rearrange("e (p k) n -> e p (k n)", k=KD)
        WW2 = moe_w2[0].rearrange("e (k p) n -> e p k n", k=KF)

        xe = [hT_t[:, i * D:(i + 1) * D] for i in range(4)]
        ye = [xn_t[:, i * D:(i + 1) * D] for i in range(2)]
        xeT = [xn_t[:, (2 + i) * D:(2 + i) * D + KD * C].rearrange("p (k c) -> p k c", k=KD) for i in range(2)]
        msg = [arena[:, i * P:(i + 1) * P] for i in range(2)]
        mhid = [arena[:, 256 + i * P:256 + (i + 1) * P] for i in range(2)]
        mhT = [arena[:, 512 + i * 64:512 + i * 64 + KF * C].rearrange("p (k c) -> p k c", k=KF) for i in range(2)]
        hbanks = ps[:, 4 * 512:(4 + KF) * 512].rearrange("p (k n) -> p k n", k=KF)[:, :, 0:C]
        arena_at = [640]

        def rpart(n, k=0):
            arena_at[0] += n
            v = arena[:, arena_at[0] - n:arena_at[0]]
            return v.rearrange("p (t n) -> p t n", t=k) if k else v

        lg = rpart(T * NR, T)
        lgT = mkv[0:NR, 0:SEQ]
        oh = [rpart(T * EXPERTS, T) for _ in range(2)]
        ohs = rpart(T * EXPERTS, T)
        em = rpart(T * EXPERTS, T)
        rtm = rpart(T * EXPERTS, T)
        pre = rpart(T * EXPERTS, T)
        iog, ioe, one64 = rpart(EXPERTS), rpart(EXPERTS), rpart(EXPERTS)
        cnt, ob, obe, obs = (rpart(EXPERTS) for _ in range(4))
        gm8, em8 = rpart(8 * T, T), rpart(8 * T, T)
        gsel, gwt = rpart(T), rpart(T)
        gexp = rpart(T * GROUPS, T)
        esel, gates, rk, stt, qq, bl, q1, desf = (rpart(2 * T) for _ in range(8))
        xw = rpart(2 * T)
        iob, iow = rpart(NB), rpart(C)
        ohw = rpart(2 * T * C, 2 * T)
        tabf, tabm = rpart(NB), rpart(NB)
        ovf, ovc = rpart(SPILL + 1), rpart(SPILL)
        assert arena_at[0] <= 4096
        ohb = xn_t[:, 0:2 * T * NB].rearrange("p (a n) -> p a n", a=2 * T)
        ohall = arena[:, 640 + T * NR:640 + T * NR + 2 * T * EXPERTS].rearrange("p (a n) -> p a n", a=2 * T)
        ohp = xn_t[:, 2 * T * NB:2 * T * NB + 2 * T * EXPERTS].rearrange("p (a n) -> p a n", a=2 * T)
        ovm = mkv[:, 0:SPILL * EXPERTS].rearrange("p (i n) -> p i n", n=EXPERTS)
        ohc = arena[:, 4480:4480 + (T + 1) * EXPERTS]
        dtab = arena[:, 4224:4224 + NB].bitcast(I32)
        ttab = arena[:, 4352:4352 + NB].bitcast(I32)
        gi_u = sb("gi_u", 8 * T, U32)
        ei_u = sb("ei_u", 8 * T, U32)
        ovf_i = sb("ovf_i", SPILL + 1, I32)
        gidx = sb("gidx", 4, I32)
        sidx = sb("sidx", 4, I32)

        @block.sync
        def _(sp):
            for t in range(T):
                sp.dma_start(xres[:, t, :], x[0, t * P:(t + 1) * P, :]).then_inc(s_x[t], 16)
            for w, (slot, dmas, release) in enumerate(tiles):
                if w >= W_SLOTS:
                    sp.wait_ge(*tiles[w - W_SLOTS][2])
                for dst, src in dmas:
                    sp.dma_start(dst, src).then_inc(s_w[slot], 16)

            def expert(e, j, last=None):
                w13, w2 = eslot(j)
                if last is not None:
                    sp.wait_ge(s_gu, last)
                for g, src in enumerate((W1, W3)):
                    sp.dma_start(w13[:, g, :, :].rearrange("p k n -> p (k n)"), src[e]).then_inc(s_ew[j], 16)
                if last is not None:
                    sp.wait_ge(s_my, last)
                sp.dma_start(w2, WW2[e]).then_inc(s_ew[j], 16)

            sp.wait_ge(s_go, GH * T)
            expert(0, 0)
            expert(1, 1)
            sp.wait_ge(s_rt, 1)
            expert(2, 2)
            expert(3, 3)
            with sp.Fori(1, EXPERTS // E_SLOTS) as it:
                for j in range(E_SLOTS):
                    expert(it * E_SLOTS + j, j, it * E_SLOTS + (j + 1 - E_SLOTS))
            sp.wait_ge(s_tabs, 2)
            n_over = sp.value_load(ovf_i[0:1, SPILL:SPILL + 1], min_val=0, max_val=SPILL)
            with sp.If(n_over > 0):
                with sp.Fori(0, n_over) as i:
                    sp.wait_ge(s_my, i + EXPERTS)
                    e = sp.value_load(ovf_i[0:1, bass.ds(i, 1)], min_val=0, max_val=EXPERTS - 1)
                    expert(e, 0)
            sp.wait_ge(s_fin, 1)
            for t in range(T):
                sp.wait_ge(s_fin, t + 1)
                sp.dma_start(out[0, t * P:(t + 1) * P, :], xres[:, t, :]).then_inc(s_out, 16)
            sp.wait_ge(s_out, 16 * T)

        @block.scalar
        def _(act):
            me = Count(act, s_act)
            small = [
                (gcols[:, KD:2 * KD], ffn_norm[0].rearrange("(k p) -> p k", p=P)),
                (gcols[:, 2 * KD:3 * KD], attn_norm_2[0].rearrange("(k p) -> p k", p=P)),
                (qgain[0:HD, :], fox_q_norm.rearrange("a p -> p a")),
                (kgain[0:HD, :], fox_k_norm.rearrange("a p -> p a")),
                (bgate[:, :], gla_b_gate[0].rearrange("(k p) -> p k", p=P)),
                (bf[:, :], fox_b_f.to_broadcast([P, HEADS])),
                (outn[:, :], gla_out_norm.to_broadcast([P, GV])),
                (wgate[0:RANK, :], gla_w_gate[0]),
            ]
            act.dma_start(metax, meta_tokens).then_inc(s_meta, 16)
            with nc.allow_non_contiguous_dma("small gains, once"):
                act.dma_start(gcols[:, 0:KD], attn_norm[0].rearrange("(k p) -> p k", p=P)).then_inc(s_gain, 16)
                for dst, src in small:
                    act.dma_start(dst, src).then_inc(s_small, 16)
            act.dma_start(gainrow[:, :], final_norm.rearrange("(a n) -> a n", a=1).to_broadcast([P, D])).then_inc(s_row, 16)

            squared = [0]

            def squares(n, t, src, rows=P):
                n = squared[0]
                squared[0] += 1
                wait(act, s_ss, n - 1)
                act.activation(scr[n % 2][0:rows, :], src, ACT.Square, accum_out=ss[0:rows, t:t + 1]).then_inc(s_ss, 1)

            def tp_out(n, gain):
                for k in range(KD) if n < 5 else range(0, KD, 2):
                    act.wait_ge(s_tp, KD * n + (n > 0) + k + 1)
                    act.activation(hTh[k] if n < 5 else hT[:, k, :], bank(k), ACT.Copy,
                                   scale=gain[:, k:k + 1] if gain is not None else 1.0).then_inc(s_tpA, 1)

            def high_halves(first, end, before):
                for c in range(first, end):
                    before(c)
                    high_half(act, c)

            for t in range(T):
                act.wait_ge(s_x[t], 16)
                squares(0, t, xres[:, t, :])
            act.wait_ge(s_meta, 16)
            squares(0, T, metax, META)
            high_halves(0, CK_SLOTS, lambda c: None)
            act.wait_ge(s_gain, 16)
            tp_out(0, gcols[:, 0:KD])
            act.wait_ge(s_small, 16 * len(small))

            def headsq(n, src, rows=P):
                if n >= 2:
                    act.wait_ge(s_rs, n - 1)
                act.activation(scr[n % 2][0:rows, :], src, ACT.Square).then_inc(s_sqh, 1)

            def proj_out(tile):
                for u, (name, j, t, eng) in enumerate(unitsB):
                    if eng == "A" and (name, j) == tile:
                        act.wait_ge(s_mB, u + 1)
                        o = {"q": 0, "k": D, "v": 2 * D}[name] + j * 512
                        if t == T:
                            act.copy(mkv[0:META, o - D:o - D + 512], bank(u % 8)[0:META, :]).then_inc(s_eA, 1)
                        else:
                            act.copy(qkvg[:, t, o:o + 512], bank(u % 8)).then_inc(s_eA, 1)

            q_end = chunk_at["f0"] - 1

            def before_chunk(c):
                for tile in (("k", 0), ("k", 1), ("q", 0), ("q", 1), ("v", 0)):
                    if chunk_at[f"{tile[0]}{tile[1]}"] + KD - 1 + CK_SLOTS == c:
                        proj_out(tile)
                n = c - (q_end + CK_SLOTS + 1)
                if n == 1:
                    act.wait_ge(s_lf, 1)
                    act.activation(zt[:, :], zt[:, :], ACT.Exp).then_inc(s_lf, 1)
                    act.wait_ge(s_lf, 2)
                    act.activation(zt[:, :], zt[:, :], ACT.Ln, bias=1.0).then_inc(s_lf, 1)
                if n == 0:
                    act.wait_ge(s_eA, sum(v[3] == "A" and v[0] in "qk" for v in unitsB))
                    act.wait_ge(s_eD, sum(v[3] == "D" and v[0] in "qk" for v in unitsB))
                n = c - (q_end + CK_SLOTS + 4)
                if 0 <= n < 2 * T:
                    headsq(n, qkvg[:, n % T, n // T * D:(n // T + 1) * D])
                elif n == 2 * T:
                    headsq(n, mkv[0:META, 0:D], META)

            high_halves(CK_SLOTS, attn_end, before_chunk)
            act.wait_ge(s_rs, 10)
            act.activation(rsq[:, :], ssq[:, :], ACT.Ln).then_inc(s_hr, 1)
            act.wait_ge(s_hr, 1)
            act.activation(rsq[:, :], rsq[:, :], ACT.Exp, scale=-0.5).then_inc(s_hr, 1)
            proj_out(("v", 1))

            NS = HEADS * T

            def qk_out(h, i):
                act.wait_ge(s_qkt, 3 * h + i + 1)
                if h >= 2 and i == 0:
                    act.wait_ge(s_S, T * (h - 1))
                dst, gain, n = ((QT[h % 2][0:HA, :], qgain, SEQ), (KT[h % 2][0:HA, META:META + SEQ], kgain, SEQ),
                                (KT[h % 2][0:HA, 0:META], kgain, META))[i]
                act.activation(dst, bank(QB)[0:HA, 0:n], ACT.Copy, scale=gain[0:HA, :]).then_inc(s_qkA, 1)

            def exps(s):
                i = s % T
                n = META + P * (i + 1)
                act.wait_ge(s_mx, s + 1)
                if s >= 3:
                    act.wait_ge(s_T, s - 2)
                act.activation(Pb[s % 3][:, 0:n], sbank(s, 0, n), ACT.Exp,
                               bias=mxn[:, 64 + s:65 + s], accum_out=rsum[:, s:s + 1]).then_inc(s_exp, 1)

            def pt_out(s):
                i = s % T
                act.wait_ge(s_T, s + 1)
                if s >= 2:
                    act.wait_ge(s_pv, s - 1)
                act.copy(PT[s % 2][0:META, 0:P], ps[0:META, PTB:PTB + P])
                act.copy(PT[s % 2][:, P:P * (i + 2)], ps[:, PTB + P:PTB + P * (i + 2)]).then_inc(s_ptA, 1)

            act.wait_ge(s_rs, 9)
            act.wait_ge(s_c, 1)
            for i in range(3):
                qk_out(0, i)
            exps(0)
            for s in range(NS):
                if s % T < 3 and s // T + 1 < HEADS:
                    qk_out(s // T + 1, s % T)
                if s + 1 < NS:
                    exps(s + 1)
                pt_out(s)
            for t in range(T):
                act.wait_ge(s_eg, T + t + 1)
                act.activation(qkvg[:, t, 3 * D:], qkvg[:, t, 3 * D:], ACT.Sigmoid).then_inc(s_sig, 1)
            high_halves(attn_end, attn_end + CK_SLOTS, lambda c: None)
            tp_out(1, None)

            def norm(n, done):
                for t in range(T):
                    act.wait_ge(*done(t))
                    squares(n, t, xres[:, t, :])

            high_halves(attn_end + CK_SLOTS, wo_end, lambda c: None)
            norm(2, lambda t: (s_res, 5 + t))
            high_halves(wo_end, wo_end + CK_SLOTS, lambda c: None)
            tp_out(2, gcols[:, KD:2 * KD])

            def silus(c):
                for j in range(FT // 2):
                    if chunk_at[f"in{j}"] + KD - 1 + CK_SLOTS == c:
                        for f in (2 * j, 2 * j + 1):
                            act.wait_ge(s_mH, f + 1)
                            if f >= 2:
                                act.wait_ge(s_hid, f - 1)
                            act.activation(sg[f % 2], bank((2 * f) % 8), ACT.Silu).then_inc(s_silu, 1)

            high_halves(wo_end + CK_SLOTS, ffn_end, silus)
            for second, t in NORMS:
                if second:
                    act.wait_ge(s_x2, t + 1)
                else:
                    act.wait_ge(s_res, 21 + t)
                squares(3 + second, t, xres[:, t, :])
            high_halves(ffn_end, ffn_end + CK_SLOTS, lambda c: None)
            tp_out(3, gcols[:, 2 * KD:3 * KD])

            def gla_proj_out(kind):
                for u, (name, j, t, eng) in enumerate(unitsG):
                    if name == kind:
                        act.wait_ge(s_mG, u + 1)
                        if name == "q":
                            act.activation(qT[:, t, :], bank(u % 8), ACT.Copy, scale=float(GK) ** -0.5).then_inc(s_gA, 1)
                        else:
                            act.activation(gz[:, t, :], bank(u % 8), ACT.Identity, bias=bgate[:, t:t + 1]).then_inc(s_gA, 1)

            def factors(h):
                act.wait_ge(s_gdv, 3 * h + 1)
                act.activation(tmp1, tmp1, ACT.Exp).then_inc(s_gac, 1)
                act.wait_ge(s_gac, 7 * h + 1)
                act.activation(tmp1, tmp1, ACT.Ln, bias=1.0).then_inc(s_gac, 1)
                act.wait_ge(s_gdv, 3 * h + 3)
                if h >= 1:
                    act.wait_ge(s_gpl, h)
                act.activation(Ex[0], D1, ACT.Exp, scale=1 / TAU).then_inc(s_gac, 1)
                act.activation(Ex[1], D1, ACT.Exp, scale=-1 / TAU).then_inc(s_gac, 1)
                act.activation(Ex[2], gg[:, h, :], ACT.Exp, scale=1 / TAU).then_inc(s_gac, 1)
                act.activation(Ex[3], D2, ACT.Exp, scale=1 / TAU).then_inc(s_gac, 1)
                act.activation(decay[:, h * NCH:(h + 1) * NCH].rearrange("p (c a) -> p c a", a=1),
                               gg[:, h, :].rearrange("p (c s) -> p c s", c=NCH)[:, :, CH - 1:CH],
                               ACT.Exp, scale=1 / TAU).then_inc(s_gac, 1)

            def before_gla(c):
                c -= ffn_end
                if c == KD + CK_SLOTS:
                    gla_proj_out("q")
                    gla_proj_out("z")
                if c in F_ACT:
                    factors(F_ACT.index(c))

            high_halves(ffn_end + CK_SLOTS, gla_end, before_gla)
            for h in range(GH):
                act.wait_ge(s_gU, 2 * h + 1)
                act.copy(kst[:, h, :, :], bank(h).rearrange("p (t d) -> p t d", t=T)).then_inc(s_kst, 1)
            for t in range(T):
                for j in range(2):
                    act.wait_ge(s_mr, 2 * t + j + 1)
                    act.activation(gr[:, t, j * 512:(j + 1) * 512], bank(6 + j), ACT.Silu).then_inc(s_er, 1)
                for h in range(GH):
                    act.wait_ge(s_in, (2 * t + 2) * GH)
                    n = t * GH + h
                    wait(act, s_gss, n - 1)
                    act.activation(arena[:, 2048 + (n % 2) * GV:2048 + (n % 2 + 1) * GV], obank(h, t), ACT.Square,
                                   accum_out=ssg[:, n:n + 1]).then_inc(s_gss, 1)
            high_halves(gla_end, gla_end + CK_SLOTS, lambda c: None)
            tp_out(4, None)
            high_halves(gla_end + CK_SLOTS, len(chunks), lambda c: None)
            for t in range(T):
                act.wait_ge(s_res, 29 + t)
                squares(5, t, xres[:, t, :])
            tp_out(5, None)

            act.wait_ge(s_oh, 1)
            for t in range(T):
                act.activation(gexp[:, t, :], lg[:, t, 0:GROUPS], ACT.Exp, bias=xw[:, t:t + 1],
                               accum_out=gwt[:, t:t + 1]).then_inc(s_rte, 1)
            act.activation(xw[:, T:2 * T], xw[:, T:2 * T], ACT.Exp).then_inc(s_rte, 1)

            def xT_out(b, j):
                act.wait_ge(s_mx1, b + 1)
                wait(act, s_gu, b - 1)
                act.copy(xeT[j % 2].rearrange("p k c -> p (k c)"), bank(j % 2)[:, 0:KD * C]).then_inc(s_mxA, 1)

            def silu(b, j):
                act.wait_ge(s_gu, b + 1)
                wait(act, s_mhid, b - 1)
                act.activation(msg[j % 2][0:C, :], bank(2 + j % 2)[0:C, 0:P], ACT.Silu)
                act.activation(msg[j % 2][G2:G2 + C, :], bank(2 + j % 2)[G2:G2 + C, 0:P], ACT.Silu).then_inc(s_msl, 1)

            def y_out(b, j):
                act.wait_ge(s_my, b + 1)
                if not isinstance(b, int) or b >= 2:
                    act.wait_ge(s_ys[j % 2], (b - j % 2) * 8)
                act.copy(ye[j % 2][0:C, 0:512], bank(6 + j % 2)[0:C, :]).then_inc(s_myA, 1)

            def block_(base, j, first):
                silu(base + j, j)
                xT_out(base + j + 1, j + 1)
                if not first:
                    y_out(base + j - 1, j - 1)

            xT_out(0, 0)
            for j in range(E_SLOTS):
                block_(0, j, j == 0)
            with act.Fori(1, EXPERTS // E_SLOTS) as it:
                for j in range(E_SLOTS):
                    block_(it * E_SLOTS, j, False)
            y_out(EXPERTS - 1, E_SLOTS - 1)

            act.wait_ge(s_tabs, 2)
            n_over = act.value_load(ovf_i[0:1, SPILL:SPILL + 1], min_val=0, max_val=SPILL)
            with act.If(n_over > 0):
                with act.Fori(0, n_over) as i:
                    act.wait_ge(s_mx1, i + (EXPERTS + 2))
                    act.copy(xeT[0].rearrange("p k c -> p (k c)"), bank(0)[:, 0:KD * C]).then_inc(s_mxA, 1)
                    act.wait_ge(s_gu, i + (EXPERTS + 1))
                    act.activation(msg[0][0:C, :], bank(2)[0:C, 0:P], ACT.Silu)
                    act.activation(msg[0][G2:G2 + C, :], bank(2)[G2:G2 + C, 0:P], ACT.Silu).then_inc(s_msl, 1)
                    act.wait_ge(s_my, i + (EXPERTS + 1))
                    act.wait_ge(s_ys[0], i * 16 + 8 * EXPERTS)
                    act.copy(ye[0][0:C, 0:512], bank(6)[0:C, :]).then_inc(s_myA, 1)
            for t in range(T):
                act.wait_ge(s_x2, T + t + 1)
                squares(6, t, xres[:, t, :])

        @block.tensor
        def _(pe):
            def transposes(n, ready, added=0):
                if added:
                    pe.wait_ge(s_res, added)
                for t in range(T):
                    pe.wait_ge(*ready(t))
                    for k in range(KD):
                        last = pe.transpose(bank(k)[:, t * P:(t + 1) * P], xn[:, t, k * P:(k + 1) * P], ident[:, :])
                        if t == T - 1:
                            last.then_inc(s_tp, 1)

            def halves_ready(n, k):
                pe.wait_ge(s_tpD, KD * n + (n > 0) + min(KD, k + 4) if n else KD + 1)

            def three(out, lhs, rhs, start, stop):
                pe.matmul(out, lhs[1], rhs[0], start=start, stop=False)
                pe.matmul(out, lhs[0], rhs[1], start=False, stop=False)
                return pe.matmul(out, lhs[0], rhs[0], start=False, stop=stop)

            def chunk(name, k):
                c = chunk_at[name] + (k or 0)
                pe.wait_ge(s_lo, c + 1)
                return chunk_views(c)[1:]

            def cut(halves, a, b):
                return tuple(v[:, a:b] for v in halves)

            pe.wait_ge(s_cst, 1)
            transposes(0, lambda t: (s_xn, t + 1))
            pe.wait_ge(s_xn, T + 1)
            pe.wait_ge(s_tpD, 1)
            for k in range(KD):
                last = pe.transpose(bank(0)[:, k * META:(k + 1) * META], metan[:, k * P:(k + 1) * P], ident[0:META, 0:META])
            last.then_inc(s_tp, 1)

            def free(units, u, sA, sD):
                if u >= 8:
                    v = u - 8
                    pe.wait_ge(sA if units[v][3] == "A" else sD, evacs(units, v))

            def project(units, first, name, j, n, hTl, moving, sA, sD, done):
                mine = [u for u, v in enumerate(units) if v[:2] == (name, j)]
                tile = ("g" if n else "") + f"{name}{j}"
                for k in range(KD):
                    w = chunk(tile, k)
                    if first:
                        halves_ready(n, k)
                    for u in mine:
                        t = units[u][2]
                        if k == 0:
                            free(units, u, sA, sD)
                        x = ((hTh[k][:, t * P:(t + 1) * P], hTl[k][:, t * P:(t + 1) * P]) if t < T else
                             (hTm_h[:, k, :], hTm_l[:, k, :]))
                        if moving:
                            last = three(bank(u % 8)[0:P if t < T else META, :], x, w, k == 0, k == KD - 1)
                        else:
                            last = three(bank(u % 8), cut(w, t * P, (t + 1) * P), (hTh[k], hTl[k]), k == 0, k == KD - 1)
                        if k == KD - 1:
                            last.then_inc(done, 1)
                    if k < KD - 1:
                        last.then_inc(s_ck, 1)

            def cumulated():
                pe.wait_ge(s_lf, 4)
                u = [v[0] for v in unitsB].index("c")
                free(unitsB, u, s_eA, s_eD)
                b = bank(u % 8)
                H = HEADS
                for t in range(T):
                    o = b[:, t * H:(t + 1) * H]
                    pe.matmul(o, ones[0:META, :], zf[0:META, T * H:(T + 1) * H], start=True, stop=False)
                    for j in range(t):
                        pe.matmul(o, ones[:, :], zf[:, j * H:(j + 1) * H], start=False, stop=False)
                    pe.matmul(o, tri[:, :], zf[:, t * H:(t + 1) * H], start=False, stop=True)
                pe.matmul(b[0:META, T * H:(T + 1) * H], tri[0:META, 0:META], zf[0:META, T * H:(T + 1) * H],
                          start=True, stop=True).then_inc(s_mB, 1)

            for name, j in (("k", 0), ("k", 1), ("q", 0), ("q", 1), ("f", 0), ("v", 0), ("c", 0), ("v", 1)):
                if name == "c":
                    cumulated()
                    continue
                if name != "f":
                    project(unitsB, (name, j) == ("k", 0), name, j, 0, hTl_first, True, s_eA, s_eD, s_mB)
                    continue
                u = [v[0] for v in unitsB].index("f")
                w = chunk("f0", None)
                free(unitsB, u, s_eA, s_eD)
                for t in range(T + 1):
                    for k in range(KD):
                        x = (hTh[k][:, t * P:(t + 1) * P], hTl_first[k][:, t * P:(t + 1) * P]) if t < T else (hTm_h[:, k, :], hTm_l[:, k, :])
                        last = three(bank(u % 8)[0:P if t < T else META, t * HEADS:(t + 1) * HEADS], x,
                                     tuple(v[:, k, :] for v in w), k == 0, k == KD - 1)
                last.then_inc(s_mB, 1)

            def banks_free(units, sA, sD):
                pe.wait_ge(sA, sum(v[3] == "A" for v in units))
                pe.wait_ge(sD, sum(v[3] == "D" for v in units))

            banks_free(unitsB, s_eA, s_eD)
            NS = HEADS * T

            def qk(h, i):
                if i == 0:
                    pe.wait_ge(s_stage, h + 1)
                wait(pe, s_qkA, 3 * h + i)
                if i == 2:
                    last = pe.transpose(bank(QB)[0:HA, 0:META], kam[h % 2][0:META, :], ident[0:META, 0:META])
                else:
                    for t in range(T):
                        last = pe.transpose(bank(QB)[0:HA, t * P:(t + 1) * P], (qa, ka)[i][h % 2][:, t, :], ident[:, :])
                last.then_inc(s_qkt, 1)

            def scores(s):
                h, i = divmod(s, T)
                n = META + P * (i + 1)
                if i == 0:
                    pe.wait_ge(s_qkA, 3 * h + 3)
                if s >= 2:
                    pe.wait_ge(s_exp, s - 1)
                lhs = QT[h % 2][0:HA, i * P:(i + 1) * P]
                last = pe.matmul(sbank(s, 0, min(n, 512)), lhs, KT[h % 2][0:HA, 0:min(n, 512)], start=True, stop=True)
                if n > 512:
                    last = pe.matmul(sbank(s, 512, n), lhs, KT[h % 2][0:HA, 512:n], start=True, stop=True)
                last.then_inc(s_S, 1)

            def ptrans(s):
                i = s % T
                pe.wait_ge(s_exp, s + 1)
                if s:
                    pe.wait_ge(s_ptA, s)
                pe.transpose(ps[0:META, PTB:PTB + P], Pb[s % 3][:, 0:META], ident[:, :])
                for j in range(i + 1):
                    last = pe.transpose(ps[:, PTB + P * (j + 1):PTB + P * (j + 2)], Pb[s % 3][:, META + P * j:META + P * (j + 1)], ident[:, :])
                last.then_inc(s_T, 1)

            def pv(s):
                h, i = divmod(s, T)
                pe.wait_ge(s_ptA, s + 1)
                wait(pe, s_o, s)
                o = bank(OB)[:, 0:HD]
                pe.matmul(o, PT[s % 2][0:META, 0:P], mkv[0:META, D + h * HD:D + (h + 1) * HD], start=True, stop=False)
                for j in range(i + 1):
                    last = pe.matmul(o, PT[s % 2][:, P * (j + 1):P * (j + 2)],
                                     qkvg[:, j, 2 * D + h * HD:2 * D + (h + 1) * HD], start=False, stop=(j == i))
                last.then_inc(s_pv, 1)

            def gate_step(s):
                g, k = divmod(s, KD)
                j, t = divmod(g, T)
                w = tile_at[f"g{j}"]
                if s % (T * KD) == 0:
                    tile_wait(pe, f"g{j}")
                if k == 0:
                    wait(pe, s_eg, g)
                if g == 0:
                    pe.wait_ge(s_hf, k + 1)
                last = pe.matmul(bank(GB), hT[:, k, t * P:(t + 1) * P], w[:, k, :], start=(k == 0), stop=(k == KD - 1))
                if k == KD - 1:
                    last.then_inc(s_mg, 1)

            for i in range(3):
                qk(0, i)
            scores(0)
            for s in range(NS):
                if s % T < 3 and s // T + 1 < HEADS:
                    qk(s // T + 1, s % T)
                if s + 1 < NS:
                    scores(s + 1)
                gate_step(s)
                ptrans(s)
                if s:
                    pv(s - 1)
            pv(NS - 1)

            def output_sums(group, items, banks_ready, done=None, together=False):
                n = len(items)
                body = items[:n - CK_SLOTS] if together else items
                for i, (name, k, x, ready) in enumerate(body):
                    w = chunk(name, k)
                    ready()
                    if i == 0:
                        banks_ready()
                    for t in range(T):
                        last = three(bank(4 * group + t), cut(x, t * P, (t + 1) * P), w, i == 0, i == n - 1)
                        if i == n - 1:
                            last.then_inc(s_mO, 1)
                    if i < n - 1:
                        last.then_inc(s_ck, 1)
                if together:
                    ws = [chunk(name, k) for name, k, _, _ in items[len(body):]]
                    for _, _, _, ready in items[len(body):]:
                        ready()
                    for t in range(T):
                        for i, w in enumerate(ws):
                            last = three(bank(4 * group + t), cut(items[len(body) + i][2], t * P, (t + 1) * P), w,
                                         False, i == CK_SLOTS - 1)
                        last.then_inc(s_mO, 1)

            def out_projection(n, name):
                for j in range(2):
                    output_sums(j, [(f"{name}{j}", k, (hTh[k], hTl_later[k]), (lambda k=k: halves_ready(n, k)) if j == 0 else lambda: None)
                                    for k in range(KD)],
                                lambda: pe.wait_ge(s_tpD, KD * (n + 1) + 1) if j else None, together=j == 1)

            transposes(1, lambda t: (s_og, t + 1))
            out_projection(1, "wo")
            transposes(2, lambda t: (s_xn, T + 2 + t), 8)
            for f0, f1 in halves:
                for i in range(f0 // 2, f1 // 2):
                    for k in range(KD):
                        w = chunk(f"in{i}", k)
                        if i == 0:
                            halves_ready(2, k)
                        if k == 0:
                            if i == 1:
                                pe.wait_ge(s_tpD, 3 * KD + 1)
                            elif 2 * i - f0 < 4 and f0:
                                pe.wait_ge(s_res, 8 + (2 * i - f0) * 2 + 4)
                            elif i > 1:
                                pe.wait_ge(s_hid, 2 * i - 2)
                        for q in range(4):
                            c = (q % 2) * 256 + (q // 2) * P
                            last = three(bank((4 * i + q) % 8), cut(w, c, c + P), (hTh[k], hTl_later[k]), k == 0, k == KD - 1)
                            if k == KD - 1 and q % 2:
                                last.then_inc(s_mH, 1)
                        if k < KD - 1:
                            last.then_inc(s_ck, 1)
                for j in range(2):
                    output_sums(j ^ (f0 > 0), [(name, k, (act_h[a - f0 + k], act_l[a - f0 + k]), lambda f=a + k: pe.wait_ge(s_act, f + 1))
                                               for name, a, n in out_tiles[f0, j] for k in range(n)],
                                lambda: pe.wait_ge(s_hid, f1 - 2 + 2 * j),
                                together=j == 1 and f0 > 0)
            transposes(3, lambda t: (s_xn, 3 * T + 1 - 3 + t), 24)

            w = chunk("ga0", None)
            for k in range(KD):
                halves_ready(3, k)
                last = three(bank(0)[0:RANK, :], tuple(v[:, k, :] for v in w), (hTh[k], hTl_later[k]), k == 0, k == KD - 1)
            last.then_inc(s_mG, 1)
            project(unitsG, False, "q", 0, 3, hTl_later, False, s_gA, s_gD, s_mG)
            for u, (name, j, t, eng) in enumerate(unitsG):
                if name == "z":
                    free(unitsG, u, s_gA, s_gD)
                    pe.wait_ge(s_gD, 1)
                    pe.matmul(bank(u % 8), wgate[0:RANK, t * P:(t + 1) * P], alrT[0:RANK, :], start=True, stop=True).then_inc(s_mG, 1)
            project(unitsG, False, "k", 0, 3, hTl_later, False, s_gA, s_gD, s_mG)
            for j in range(2):
                project(unitsG, False, "v", j, 3, hTl_later, True, s_gA, s_gD, s_mG)
            banks_free(unitsG, s_gA, s_gD)
            for h in range(GH):
                pe.wait_ge(s_gpl, h + 1)
                for t in range(T):
                    last = pe.transpose(bank(h)[:, t * P:(t + 1) * P], ksT[:, h, t * P:(t + 1) * P], ident[:, :])
                last.then_inc(s_gU, 1)
                for t in range(T):
                    last = pe.matmul(bank(4 + h)[:, t * P:(t + 1) * P], kT[:, h, t * P:(t + 1) * P], qT[:, h, t * P:(t + 1) * P],
                                     start=True, stop=True)
                last.then_inc(s_gU, 1)

            def gate_products(i):
                return min(2 * T * KD, 2 * i + min(i, 8))

            pe.wait_ge(s_kst, GH)
            pe.wait_ge(s_gq, GH)
            pe.wait_ge(s_atm, GH)
            for c in range(NCH):
                t, r = divmod(c, 2)
                rows = slice(r * CH, (r + 1) * CH)
                for h in range(GH):
                    if c < NCH - 1:
                        if c >= 1:
                            pe.wait_ge(s_S2, (c - 1) * GH + (h | 1) + 1)
                        pe.matmul(ubank(h, c), kst[rows, h, t, :],
                                  gv[rows, t, h * GV:(h + 1) * GV], start=True, stop=True).then_inc(s_U, 1)
                    o = obank(h, t)
                    if r == 0:
                        if t >= 2:
                            pe.wait_ge(s_go, (t - 2) * GH + (h | 1) + 1)
                        last = pe.matmul(o, atm[:, h, t, :], gv[:, t, h * GV:(h + 1) * GV], start=(h % 2 == 0), stop=False,
                                         skip_group_check=True)
                    if c:
                        pe.wait_ge(s_S2, (c - 1) * GH + h + 1)
                        last = pe.matmul(o[rows, :], qiT[:, h, c * CH:(c + 1) * CH], St[:, h, c % 2, :],
                                         start=False, stop=(r == 1), skip_group_check=True)
                    last.then_inc(s_in, 1)
                    i = c * GH + h
                    for n in range(gate_products(i), gate_products(i + 1)):
                        u, k = divmod(n, KD)
                        tr, jr = divmod(u, 2)
                        if n in (0, KD):
                            tile_wait(pe, f"gr{jr}")
                        if k == 0:
                            wait(pe, s_er, u - 1)
                        if u == 0:
                            pe.wait_ge(s_hf, KD + k + 1)
                        last = pe.matmul(bank(6 + jr), hT[:, k, tr * P:(tr + 1) * P], tile_at[f"gr{jr}"][:, k, :],
                                         start=(k == 0), stop=(k == KD - 1))
                        if k == KD - 1:
                            last.then_inc(s_mr, 1)
            transposes(4, lambda t: (s_go, GH * T))
            out_projection(4, "gwo")
            transposes(5, lambda t: (s_hnrow, t + 1), 32)
            tile_wait(pe, "rt")
            w = tile_at["rt"]
            for k in range(KD):
                if k % 2:
                    pe.wait_ge(s_tpD, KD * 5 + 1 + (k + 1) // 2)
                else:
                    pe.wait_ge(s_tpA, KD * 5 + k // 2 + 1)
                last = pe.matmul(bank(0)[0:NR, :], w[:, k, :], hT[:, k, :], start=(k == 0), stop=(k == KD - 1))
            last.then_inc(s_rt, 1)
            pe.wait_ge(s_lgT, 1)
            for t in range(T):
                last = pe.transpose(bank(1)[:, t * NR:(t + 1) * NR], lgT[:, t * P:(t + 1) * P], ident[0:NR, 0:NR])
            last.then_inc(s_lg, 1)
            pe.wait_ge(s_oh, 2)
            n = T * EXPERTS
            pe.matmul(bank(1)[:, 0:n], strict[:, :], ohs.rearrange("p t n -> p (t n)"), start=True, stop=False)
            pe.wait_ge(s_oh, 3)
            pe.matmul(bank(1)[:, 0:n], ones[:, :], ohc[:, 0:n], start=False, stop=True)
            pe.matmul(bank(1)[:, n:n + EXPERTS], ones[:, :], ohc[:, n:n + EXPERTS], start=True, stop=True).then_inc(s_pre, 1)
            pe.wait_ge(s_idx, 1)
            for a in range(2 * T):
                last = pe.matmul(bank(2)[0:C, 0:NB], ohw[:, a, :], ohb[:, a, :], start=(a == 0), stop=(a == 2 * T - 1))
            last.then_inc(s_tab, 1)

            def tokens(j, buf):
                pe.sem_inc(s_tick, 1)
                v = xe[buf].rearrange("p (m k) -> p k m", k=KD)
                for k in range(KD):
                    last = pe.transpose(bank(j % 2)[:, k * C:(k + 1) * C], v[0:C, k, :], ident[0:C, 0:C])
                last.then_inc(s_mx1, 1)

            def A(b, j, n):
                pe.wait_ge(s_xe[j % 4], n)
                wait(pe, s_mxA, b - 1)
                tokens(j, j % 4)

            def gate_up(j, slot):
                w13, _ = eslot(slot)
                g = bank(2 + j % 2)
                for k in range(KD):
                    for q in range(2):
                        last = pe.matmul(g[q * G2:q * G2 + C, 0:2 * P], xeT[j % 2][:, k, :], w13[:, :, k, q * P:(q + 1) * P],
                                         start=(k == 0), stop=(k == KD - 1), skip_group_check=True)
                last.then_inc(s_gu, 1)

            def B(b, j, n_w):
                pe.wait_ge(s_ew[j], n_w)
                pe.wait_ge(s_mxA, b + 1)
                wait(pe, s_mhid, b - 1)
                gate_up(j, j)

            def hidden(j):
                pe.sem_inc(s_tick, 1)
                for q in range(2):
                    r = slice(q * G2, q * G2 + C)
                    last = pe.transpose(bank(4 + q)[:, 0:C], mhid[j % 2][r, :], ident[r, r])
                last.then_inc(s_mhT, 1)

            def Ct(b, j):
                pe.wait_ge(s_mhid, b + 1)
                wait(pe, s_mhTe, b)
                hidden(j)

            def expert_down(j, slot):
                w2 = eslot(slot)[1]
                for k in range(KF):
                    for n in range(2):
                        last = pe.matmul(bank(6 + j % 2)[n * G2:n * G2 + C, :], mhT[j % 2][:, k, :], w2[:, k, n * 512:(n + 1) * 512],
                                         start=(k == 0), stop=(k == KF - 1), skip_group_check=True)
                last.then_inc(s_my, 1)

            def Dy(b, j):
                pe.wait_ge(s_mhTe, b + 1)
                wait(pe, s_myA, b - 1)
                wait(pe, s_myD, b - 1)
                expert_down(j, j % 4)

            def block_(base, j, first, n_w):
                B(base + j, j, n_w)
                A(base + j + 1, j + 1, n_w // 3 + (16 if j == 3 else 0) if isinstance(n_w, int) else base * 4 + (16 if j < 3 else 32))
                if not first:
                    Dy(base + j - 1, (j - 1) % 4)
                Ct(base + j, j)

            pe.wait_ge(s_tabs, 1)
            A(0, 0, 16)
            for j in range(E_SLOTS):
                block_(0, j, j == 0, 48)
            with pe.Fori(1, EXPERTS // E_SLOTS) as it:
                for j in range(E_SLOTS):
                    block_(it * E_SLOTS, j, False, it * 48 + 48)
            Dy(EXPERTS - 1, E_SLOTS - 1)
            pe.wait_ge(s_tabs, 2)
            n_over = pe.value_load(ovf_i[0:1, SPILL:SPILL + 1], min_val=0, max_val=SPILL)
            with pe.If(n_over > 0):
                with pe.Fori(0, n_over) as i:
                    pe.wait_ge(s_xe[0], i * 16 + 4 * (EXPERTS + 4) + 16)
                    pe.wait_ge(s_mxA, i + (EXPERTS + 1))
                    tokens(0, 0)
                    pe.wait_ge(s_ew[0], i * 48 + 48 * (EXPERTS // 4 + 1))
                    pe.wait_ge(s_mxA, i + (EXPERTS + 2))
                    pe.wait_ge(s_mhid, i + EXPERTS)
                    gate_up(0, 0)
                    pe.wait_ge(s_mhid, i + (EXPERTS + 1))
                    hidden(0)
                    pe.wait_ge(s_mhTe, i + (EXPERTS + 1))
                    pe.wait_ge(s_myA, i + EXPERTS)
                    pe.wait_ge(s_myD, i + EXPERTS)
                    expert_down(0, 0)

        @block.vector
        def _(dve):
            me = Count(dve, s_dve)

            roots = Count(dve, s_ms)

            def rms_scale(dst, src, n):
                roots.inc(dve.tensor_scalar(dst, src, 1.0 / n, EPS, ALU.mult, ALU.add))
                dve.wait_ge(s_pw, roots.n)

            def tp_out(n, gain):
                for k in range(KD):
                    dve.wait_ge(s_tpA, KD * n + k + 1)
                    lo = (hTl_later if n else hTl_first)[k]
                    if gain is not None:
                        dve.scalar_tensor_tensor(out=lo, in0=bank(k), scalar=gain[:, k:k + 1], in1=hTh[k], op0=ALU.mult,
                                                 op1=ALU.subtract).then_inc(s_tpD, 1)
                    else:
                        dve.tensor_tensor(lo, bank(k), hTh[k], ALU.subtract).then_inc(s_tpD, 1)

            def whole_hT(lows, which=range(KD)):
                for k in which:
                    dve.tensor_tensor(hT[:, k, :], hTh[k], lows[k], ALU.add).then_inc(s_hf, 1)

            def normed_tile(t, n_ss):
                dve.wait_ge(s_ss, n_ss)
                rms_scale(rstd[:, t:t + 1], ss[:, t:t + 1], D)
                dve.tensor_scalar(xn[:, t, :], xres[:, t, :], rstd[:, t:t + 1], None, ALU.mult).then_inc(s_xn, 1)

            for t in range(T):
                normed_tile(t, t + 1)
            dve.wait_ge(s_ss, T + 1)
            rms_scale(rstd[0:META, T:T + 1], ss[0:META, T:T + 1], D)
            dve.tensor_scalar(metan, metax, rstd[0:META, T:T + 1], None, ALU.mult).then_inc(s_xn, 1)
            dve.wait_ge(s_gain, 16)
            tp_out(0, gcols[:, 0:KD])
            dve.wait_ge(s_tp, KD + 1)
            me.link(dve.tensor_tensor(hTm, bank(0)[:, 0:KD * META].rearrange("p (k s) -> p k s", k=KD),
                                      gcols[:, 0:KD].unsqueeze(2).to_broadcast([P, KD, META]), ALU.mult))
            me.link(dve.tensor_copy(hTm_h, hTm))
            dve.tensor_tensor(hTm_l, hTm, hTm_h, ALU.subtract).then_inc(s_tpD, 1)
            H = HEADS
            me.link(dve.memset(zf[:, :], 0.0))
            me.link(dve.memset(ssq[:, :], 1.0))
            dve.wait_ge(s_small, 16 * 8)
            me.link(dve.memset(qgain[HD:P, :], 1.0))
            me.link(dve.memset(kgain[HD:P, :], 1.0))
            me.link(dve.tensor_scalar(qgain[0:HD, :], qgain[0:HD, :], float(HD) ** -0.5, None, ALU.mult))
            for u, (name, j, t, eng) in enumerate(unitsB):
                if eng != "D":
                    continue
                dve.wait_ge(s_mB, u + 1)
                b = bank(u % 8)
                if name == "f":
                    dve.tensor_tensor(zf[0:META, T * H:], b[0:META, T * H:(T + 1) * H], bf[0:META, :], ALU.add)
                    dve.tensor_tensor(zf[:, 0:T * H].rearrange("p (t h) -> p t h", t=T), b[:, 0:T * H].rearrange("p (t h) -> p t h", t=T),
                                      bf[:, :].unsqueeze(1).to_broadcast([P, T, H]), ALU.add).then_inc(s_eD, 1)
                    dve.wait_ge(s_eD, evacs(unitsB, u))
                    dve.scalar_tensor_tensor(out=zt[:, :], in0=zf[:, :], scalar=-1.0, in1=zf[:, :], op0=ALU.mult, op1=ALU.min).then_inc(s_lf, 1)
                    dve.wait_ge(s_lf, 3)
                    dve.scalar_tensor_tensor(out=zf[:, :], in0=zf[:, :], scalar=0.0, in1=zt[:, :], op0=ALU.min, op1=ALU.subtract).then_inc(s_lf, 1)
                elif name == "c":
                    n = T * H
                    me.link(dve.memset(cc[:, :], 0.0))
                    dve.tensor_copy(cc[:, 0:n], b[:, 0:n])
                    dve.tensor_copy(cc[0:META, n:], b[0:META, n:n + H]).then_inc(s_eD, 1)
                    dve.wait_ge(s_eD, evacs(unitsB, u))
                    dve.tensor_scalar(ncc[:, :], cc[:, :], -1.0, None, ALU.mult).then_inc(s_c, 1)
                    for n in range(9):
                        rows = P if n < 8 else META
                        dve.wait_ge(s_sqh, n + 1)
                        dve.tensor_reduce(ssq[0:rows, n * H:(n + 1) * H], scr[n % 2][0:rows, :].rearrange("p (h d) -> p h d", h=H),
                                          AX, ALU.add).then_inc(s_rs, 1)
                    dve.wait_ge(s_rs, 9)
                    dve.tensor_scalar(ssq[:, :], ssq[:, :], 1.0 / HD, EPS, ALU.mult, ALU.add).then_inc(s_rs, 1)
                    dve.wait_ge(s_hr, 2)
                    me.link(dve.tensor_tensor(newton, rsq[:, :], rsq[:, :], ALU.mult))
                    me.link(dve.tensor_tensor(newton, newton, ssq[:, :], ALU.mult))
                    me.link(dve.tensor_scalar(newton, newton, -0.5, 1.5, ALU.mult, ALU.add))
                    dve.tensor_tensor(rsq[:, :], rsq[:, :], newton, ALU.mult).then_inc(s_hr, 1)
                else:
                    o = {"q": 0, "k": D, "v": 2 * D}[name] + j * 512
                    if t == T:
                        dve.tensor_copy(mkv[0:META, o - D:o - D + 512], b[0:META, :]).then_inc(s_eD, 1)
                    else:
                        dve.tensor_copy(qkvg[:, t, o:o + 512], b).then_inc(s_eD, 1)

            NS = HEADS * T
            dve.wait_ge(s_cst, 1)

            def rowmax(s):
                i = s % T
                n = META + P * (i + 1)
                dve.wait_ge(s_S, s + 1)
                me.link(dve.tensor_tensor(sbank(s, n - P, n), sbank(s, n - P, n), amask[:, :], ALU.add))
                me.link(dve.tensor_reduce(mxn[:, s:s + 1], sbank(s, 0, n), AX, ALU.max))
                dve.tensor_scalar(mxn[:, 64 + s:65 + s], mxn[:, s:s + 1], -1.0, None, ALU.mult).then_inc(s_mx, 1)

            def attn_out(s):
                h, i = divmod(s, T)
                me.link(dve.reciprocal(rinv[:, s:s + 1], rsum[:, s:s + 1]))
                dve.wait_ge(s_pv, s + 1)
                dve.tensor_scalar(xn[:, i, h * HD:(h + 1) * HD], bank(OB)[:, 0:HD], rinv[:, s:s + 1], None, ALU.mult).then_inc(s_o, 1)

            def gate_out(g):
                j, t = divmod(g, T)
                dve.wait_ge(s_mg, g + 1)
                dve.tensor_copy(qkvg[:, t, 3 * D + j * 512:3 * D + (j + 1) * 512], bank(GB)).then_inc(s_eg, 1)

            rowmax(0)
            whole_hT(hTl_first, range(1))
            for s in range(NS):
                if s % KD == 0 and s:
                    gate_out(s // KD - 1)
                if s + 1 < NS:
                    rowmax(s + 1)
                if s + 1 < KD:
                    whole_hT(hTl_first, range(s + 1, s + 2))
                if s:
                    attn_out(s - 1)
            attn_out(NS - 1)
            gate_out(2 * T - 1)
            dve.wait_ge(s_o, NS)
            for t in range(T):
                dve.wait_ge(s_sig, t + 1)
                dve.tensor_tensor(xn[:, t, :], xn[:, t, :], qkvg[:, t, 3 * D:], ALU.mult).then_inc(s_og, 1)
            tp_out(1, None)

            def residual(base, norm, swap=0):
                for j in range(2):
                    for t in range(T):
                        dve.wait_ge(s_mO, base + j * T + t + 1)
                        d = xres[:, t, j * 512:(j + 1) * 512]
                        dve.tensor_tensor(d, d, bank(4 * (j ^ swap) + t), ALU.add).then_inc(s_res, 1)
                        if j and t and norm:
                            norm(t - 1)
                if norm:
                    norm(T - 1)

            def norm_tile(n_ss, n_res):
                def norm(t):
                    dve.wait_ge(s_res, n_res + T + t + 1)
                    dve.wait_ge(s_ss, n_ss + t + 1)
                    rms_scale(rstd[:, t:t + 1], ss[:, t:t + 1], D)
                    dve.tensor_scalar(xn[:, t, :], xres[:, t, :], rstd[:, t:t + 1], None, ALU.mult).then_inc(s_xn, 1)
                return norm

            residual(0, norm_tile(5, 0))
            tp_out(2, gcols[:, KD:2 * KD])

            def hidden_values(f0, f1):
                for f in range(f0, f1):
                    dve.wait_ge(s_silu, f + 1)
                    wait(dve, s_act, f - 1)
                    dve.tensor_tensor(prod[f % 2], sg[f % 2], bank((2 * f + 1) % 8), ALU.mult).then_inc(s_hid, 1)
                    dve.wait_ge(s_hid, f + 1)
                    me.link(dve.tensor_copy(act_h[f - f0], prod[f % 2]))
                    dve.tensor_tensor(act_l[f - f0], prod[f % 2], act_h[f - f0], ALU.subtract).then_inc(s_act, 1)

            def second_input(t):
                dve.wait_ge(s_row, 16)
                dve.wait_ge(s_res, 16 + T + t + 1)
                dve.wait_ge(s_ss, 10 + NORMS.index((0, t)))
                rms_scale(rstd[:, t:t + 1], ss[:, t:t + 1], D)
                dve.scalar_tensor_tensor(out=xres[:, t, :], in0=xres[:, t, :], scalar=rstd[:, t:t + 1], in1=gainrow[:, :],
                                         op0=ALU.mult, op1=ALU.mult).then_inc(s_x2, 1)
                if t:
                    normed_tile(t - 1, 10 + NORMS.index((1, t - 1)))

            hidden_values(*halves[0])
            residual(8, None)
            hidden_values(*halves[1])
            residual(16, second_input, 1)
            normed_tile(T - 1, 10 + NORMS.index((1, T - 1)))
            tp_out(3, gcols[:, 2 * KD:3 * KD])

            def gla_proj_out(kind, jj):
                for u, (name, j, t, eng) in enumerate(unitsG):
                    if (name, j) != (kind, jj):
                        continue
                    dve.wait_ge(s_mG, u + 1)
                    b = bank(u % 8)
                    if name == "a":
                        dve.tensor_copy(alrT[0:RANK, :], b[0:RANK, :]).then_inc(s_gD, 1)
                    elif name == "k":
                        dve.tensor_copy(kT[:, t, :], b).then_inc(s_gD, 1)
                    else:
                        dve.tensor_copy(gv[:, t, j * 512:(j + 1) * 512], b).then_inc(s_gD, 1)

            def logs(h):
                if h:
                    dve.wait_ge(s_gac, 7 * h)
                dve.scalar_tensor_tensor(out=tmp1, in0=gz[:, h, :], scalar=-1.0, in1=gz[:, h, :], op0=ALU.mult, op1=ALU.min).then_inc(s_gdv, 1)
                dve.wait_ge(s_gac, 7 * h + 2)
                me.link(dve.scalar_tensor_tensor(out=gz[:, h, :], in0=gz[:, h, :], scalar=0.0, in1=tmp1, op0=ALU.min, op1=ALU.subtract))
                me.link(dve.tensor_tensor_scan(gg[:, h, :], reset[:, :], gz[:, h, :], 0.0, ALU.mult, ALU.add))
                g3 = gg[:, h, :].rearrange("p (c s) -> p c s", c=NCH)
                dve.tensor_tensor(D1.rearrange("p (c s) -> p c s", c=NCH), g3, g3[:, :, CH // 2:CH // 2 + 1].to_broadcast([P, NCH, CH]),
                                  ALU.subtract).then_inc(s_gdv, 1)
                dve.tensor_tensor(D2.rearrange("p (c s) -> p c s", c=NCH), g3[:, :, CH - 1:CH].to_broadcast([P, NCH, CH]), g3,
                                  ALU.subtract).then_inc(s_gdv, 1)

            def decayed_q(h):
                dve.wait_ge(s_gac, 7 * h + 7)
                dve.tensor_tensor(qiT[:, h, :], qT[:, h, :], Ex[2], ALU.mult).then_inc(s_gq, 1)

            gla_proj_out("a", 0)
            zl = max(u for u, v in enumerate(unitsG) if v[0] == "z")
            dve.wait_ge(s_gA, evacs(unitsG, zl))
            dve.wait_ge(s_reset, 1)
            logs(0)
            decayed_q(0)
            gla_proj_out("k", 0)
            logs(1)
            decayed_q(1)
            logs(2)
            decayed_q(2)
            gla_proj_out("v", 0)
            logs(3)
            decayed_q(3)
            gla_proj_out("v", 1)
            whole_hT(hTl_later)
            dve.wait_ge(s_gpl, GH)
            for h in range(GH):
                dve.wait_ge(s_gU, 2 * h + 2)
                dve.tensor_tensor(atm[:, h, :, :], bank(4 + h).rearrange("p (t s) -> p t s", t=T),
                                  gmask[:, :].unsqueeze(1).to_broadcast([P, T, P]), ALU.mult).then_inc(s_atm, 1)

            def gla_out(t):
                dve.wait_ge(s_gss, (t + 1) * GH)
                rms_scale(ssg[:, 32 + t * GH:32 + (t + 1) * GH], ssg[:, t * GH:(t + 1) * GH], GV)
                dve.wait_ge(s_gr, t + 1)
                for h in range(GH):
                    n = t * GH + h
                    dve.scalar_tensor_tensor(out=xn[:, t, h * GV:(h + 1) * GV], in0=obank(h, t),
                                             scalar=ssg[:, 32 + n:33 + n], in1=gr[:, t, h * GV:(h + 1) * GV],
                                             op0=ALU.mult, op1=ALU.mult).then_inc(s_go, 1)

            for c in range(NCH):
                if c < NCH - 1:
                    for h in range(GH):
                        dve.wait_ge(s_U, c * GH + (h | 1) + 1)
                        if c >= 1:
                            dve.wait_ge(s_in, (c - 1) * GH + h + 1)
                            dve.wait_ge(s_S2, (c - 1) * GH + h + 1)
                        u = ubank(h, c)
                        if c == 0:
                            dve.tensor_copy(St[:, h, 1, :], u).then_inc(s_S2, 1)
                        else:
                            dve.scalar_tensor_tensor(out=St[:, h, (c + 1) % 2, :], in0=St[:, h, c % 2, :],
                                                     scalar=decay[:, h * NCH + c:h * NCH + c + 1], in1=u,
                                                     op0=ALU.mult, op1=ALU.add).then_inc(s_S2, 1)
                if c >= 3 and c % 2 == 1:
                    gla_out(c // 2 - 1)
            gla_out(T - 1)
            tp_out(4, None)

            def moe_input(t):
                dve.wait_ge(s_row2, 16)
                dve.wait_ge(s_res, 24 + T + t + 1)
                dve.wait_ge(s_ss, 17 + t + 1)
                rms_scale(rstd[:, t:t + 1], ss[:, t:t + 1], D)
                dve.scalar_tensor_tensor(out=xn[:, t, :], in0=xres[:, t, :], scalar=rstd[:, t:t + 1], in1=gainrow[:, :],
                                         op0=ALU.mult, op1=ALU.mult).then_inc(s_hnrow, 1)

            residual(24, moe_input)
            for k in range(1, KD, 2):
                dve.wait_ge(s_tp, KD * 5 + 1 + k + 1)
                dve.tensor_copy(hT[:, k, :], bank(k)).then_inc(s_tpD, 1)

            def over(v, n):
                return v.unsqueeze(1).to_broadcast([v.shape[0], n, v.shape[1]])

            def along(v, n):
                return v.unsqueeze(2).to_broadcast([v.shape[0], v.shape[1], n])

            def blocks_before(dst, v, less):
                me.link(dve.tensor_scalar(dst, v, 1.0 / C, 0.5 / C - 0.5 - less / C, ALU.mult, ALU.add))
                me.link(dve.tensor_scalar(dst, dst, 1.5 * 2 ** 23, None, ALU.add))
                me.link(dve.tensor_scalar(dst, dst, -1.5 * 2 ** 23, None, ALU.add))

            dve.wait_ge(s_rt, 1)
            dve.tensor_copy(lgT, bank(0)[0:NR, :]).then_inc(s_lgT, 1)
            dve.wait_ge(s_lg, 1)
            me.link(dve.tensor_copy(lg.rearrange("p t n -> p (t n)"), bank(1)[:, 0:T * NR]))
            dve.wait_ge(s_cst, 2)
            for t in range(T):
                me.inc(dve.max(gm8[:, t, :], lg[:, t, 0:GROUPS]))
            me.wait()
            for t in range(T):
                me.inc(dve.max_index(gi_u[:, t * 8:t * 8 + 8], gm8[:, t, :], lg[:, t, 0:GROUPS]))
            me.wait()
            me.link(dve.tensor_copy(gsel, gi_u[:, :].rearrange("p (t n) -> p t n", t=T)[:, :, 0]))
            me.link(dve.tensor_tensor(rtm, over(iog, T), along(gsel, EXPERTS), ALU.is_equal))
            me.link(dve.tensor_tensor(em, lg[:, :, GROUPS:NR], rtm, ALU.mult))
            me.link(dve.tensor_scalar(rtm, rtm, -1.0, -NEG, ALU.add, ALU.mult))
            me.link(dve.tensor_tensor(em, em, rtm, ALU.add))
            for t in range(T):
                me.inc(dve.max(em8[:, t, :], em[:, t, :]))
            me.wait()
            for t in range(T):
                me.inc(dve.max_index(ei_u[:, t * 8:t * 8 + 8], em8[:, t, :], em[:, t, :]))
            me.inc(dve.tensor_scalar(xw[:, 0:T], gm8[:, :, 0], -1.0, None, ALU.mult))
            me.wait()
            dve.tensor_tensor(xw[:, T:2 * T], em8[:, :, 1], em8[:, :, 0], ALU.subtract).then_inc(s_oh, 1)
            me.link(dve.tensor_copy(esel.rearrange("p (k t) -> p t k", k=2), ei_u[:, :].rearrange("p (t n) -> p t n", t=T)[:, :, 0:2]))
            me.link(dve.tensor_tensor(ohall, over(ioe, 2 * T), along(esel, EXPERTS), ALU.is_equal))
            dve.wait_ge(s_oh, 1)
            dve.tensor_tensor(ohs, oh[0], oh[1], ALU.add).then_inc(s_oh, 1)
            me.inc(dve.memset(ohc[:, 0:EXPERTS], 0.0))
            dve.wait_ge(s_oh, 2)
            me.link(dve.tensor_copy(ohc[:, EXPERTS:2 * EXPERTS], ohs[:, 0, :]))
            for t in range(1, T):
                e = dve.tensor_tensor(ohc[:, (t + 1) * EXPERTS:(t + 2) * EXPERTS], ohc[:, t * EXPERTS:(t + 1) * EXPERTS], ohs[:, t, :], ALU.add)
                if t < T - 1:
                    me.link(e)
            e.then_inc(s_oh, 1)
            me.link(dve.memset(one64, 1.0))
            dve.wait_ge(s_pre, 1)
            me.inc(dve.tensor_copy(pre.rearrange("p t n -> p (t n)"), bank(1)[:, 0:T * EXPERTS]))
            me.link(dve.tensor_copy(cnt, bank(1)[:, T * EXPERTS:(T + 1) * EXPERTS]))
            blocks_before(ob, cnt, 1)
            me.link(dve.tensor_scalar(ob, ob, 0.0, None, ALU.max))
            me.link(dve.tensor_tensor_scan(obe, one64, ob, 0.0, ALU.mult, ALU.add))
            me.link(dve.tensor_tensor(obs, obe, ob, ALU.subtract))
            dve.wait_ge(s_hnd, 16 * T)
            for k in range(2):
                me.inc(dve.tensor_tensor(ohp[:, k * T:(k + 1) * T, :], oh[k], pre, ALU.mult))
            me.wait()
            me.link(dve.tensor_reduce(rk, ohp, AX, ALU.add))
            me.link(dve.tensor_tensor(ohp, ohall, over(obs, 2 * T), ALU.mult))
            me.link(dve.tensor_reduce(stt, ohp, AX, ALU.add))
            me.inc(dve.tensor_scalar(q1, rk, C - 0.5, None, ALU.is_ge))
            blocks_before(qq, rk, 0)
            me.link(dve.tensor_tensor(bl, stt, qq, ALU.add))
            me.link(dve.scalar_tensor_tensor(out=bl, in0=bl, scalar=EXPERTS - 1.0, in1=esel, op0=ALU.add, op1=ALU.subtract))
            me.link(dve.tensor_tensor(bl, bl, q1, ALU.mult))
            me.inc(dve.tensor_tensor(bl, bl, esel, ALU.add))
            me.inc(dve.scalar_tensor_tensor(out=rk, in0=qq, scalar=-float(C), in1=rk, op0=ALU.mult, op1=ALU.add))
            me.wait()
            me.link(dve.tensor_tensor(ohw, over(iow, 2 * T), along(rk, C), ALU.is_equal))
            me.link(dve.tensor_tensor(ohw, ohw, along(desf, C), ALU.mult))
            dve.tensor_tensor(ohb, over(iob, 2 * T), along(bl, NB), ALU.is_equal).then_inc(s_idx, 1)
            dve.wait_ge(s_rte, T + 1)
            x1 = xw[:, T:2 * T]
            me.link(dve.tensor_scalar(gsel, x1, 1.0, None, ALU.add))
            me.link(dve.tensor_tensor(gsel, gsel, gwt, ALU.mult))
            me.link(dve.reciprocal(gates[:, 0:T], gsel))
            me.link(dve.tensor_tensor(gates[:, T:2 * T], gates[:, 0:T], x1, ALU.mult))
            dve.wait_ge(s_tab, 1)
            me.link(dve.tensor_copy(tabf[0:C, :], bank(2)[0:C, 0:NB]))
            me.link(dve.tensor_scalar(tabm[0:C, :], tabf[0:C, :], 0.5, float(SKIP), ALU.is_lt, ALU.mult))
            me.link(dve.scalar_tensor_tensor(out=tabf[0:C, :], in0=tabf[0:C, :], scalar=-1.0, in1=tabm[0:C, :], op0=ALU.add, op1=ALU.add))
            me.inc(dve.tensor_copy(dtab[0:C, :], tabf[0:C, :]))
            me.link(dve.tensor_scalar(tabm[0:C, :], tabf[0:C, :], SEQ - 0.5, -float(SEQ), ALU.is_ge, ALU.mult))
            me.link(dve.tensor_tensor(tabf[0:C, :], tabf[0:C, :], tabm[0:C, :], ALU.add))
            me.inc(dve.tensor_copy(ttab[0:C, :], tabf[0:C, :]))
            me.wait()
            dve.memset(q1[:, 0:1], 0.0).then_inc(s_tabs, 1)
            me.link(dve.tensor_tensor(ovm[0:1, :, :], over(obe[0:1, :], SPILL), along(ovc[0:1, :], EXPERTS), ALU.is_lt))
            me.link(dve.tensor_reduce(ovf[0:1, 0:SPILL], ovm[0:1, :, :], AX, ALU.add))
            me.link(dve.tensor_scalar(ovf_i[0:1, 0:SPILL], ovf[0:1, 0:SPILL], EXPERTS - 1.0, None, ALU.min))
            dve.tensor_copy(ovf_i[0:1, SPILL:SPILL + 1], obe[0:1, EXPERTS - 1:EXPERTS]).then_inc(s_tabs, 1)

            def hid(b, j):
                dve.wait_ge(s_msl, b + 1)
                wait(dve, s_mhT, b - 1)
                hidden(j)

            def hidden(j):
                for q in range(2):
                    r = slice(q * G2, q * G2 + C)
                    last = dve.tensor_tensor(mhid[j % 2][r, :], msg[j % 2][r, :], bank(2 + j % 2)[r, P:2 * P], ALU.mult)
                last.then_inc(s_mhid, 1)

            def y_out(b, j):
                dve.wait_ge(s_my, b + 1)
                if not isinstance(b, int) or b >= 2:
                    dve.wait_ge(s_ys[j % 2], (b - j % 2) * 8)
                dve.tensor_copy(ye[j % 2][0:C, 512:1024], bank(6 + j % 2)[G2:G2 + C, :]).then_inc(s_myD, 1)

            def hT_out(b, j):
                dve.wait_ge(s_mhT, b + 1)
                wait(dve, s_my, b - 1)
                dve.tensor_copy(mhT[j % 2], hbanks).then_inc(s_mhTe, 1)

            def block_(base, j, first):
                hid(base + j, j)
                if not first:
                    y_out(base + j - 1, j - 1)
                hT_out(base + j, j)

            for j in range(E_SLOTS):
                block_(0, j, j == 0)
            with dve.Fori(1, EXPERTS // E_SLOTS) as it:
                for j in range(E_SLOTS):
                    block_(it * E_SLOTS, j, False)
            y_out(EXPERTS - 1, E_SLOTS - 1)
            dve.wait_ge(s_tabs, 2)
            n_over = dve.value_load(ovf_i[0:1, SPILL:SPILL + 1], min_val=0, max_val=SPILL)
            with dve.If(n_over > 0):
                with dve.Fori(0, n_over) as i:
                    dve.wait_ge(s_msl, i + (EXPERTS + 1))
                    hidden(0)
                    dve.wait_ge(s_mhT, i + (EXPERTS + 1))
                    dve.tensor_copy(mhT[0], hbanks).then_inc(s_mhTe, 1)
                    dve.wait_ge(s_my, i + (EXPERTS + 1))
                    dve.wait_ge(s_ys[0], i * 16 + 8 * EXPERTS)
                    dve.tensor_copy(ye[0][0:C, 512:1024], bank(6)[G2:G2 + C, :]).then_inc(s_myD, 1)

            dve.wait_ge(s_row2, 32)
            yv = big[:, 0:2 * T * D].rearrange("p (k t d) -> p k t d", k=2, t=T)
            def finish(t):
                dve.wait_ge(s_x2, T + t + 1)
                dve.wait_ge(s_pw, roots.n)
                dve.scalar_tensor_tensor(out=xres[:, t, :], in0=xres[:, t, :], scalar=rstd[:, t:t + 1], in1=gainrow[:, :],
                                         op0=ALU.mult, op1=ALU.mult).then_inc(s_fin, 1)

            def mean_square(t):
                dve.wait_ge(s_ss, 21 + t + 1)
                roots.inc(dve.tensor_scalar(rstd[:, t:t + 1], ss[:, t:t + 1], 1.0 / D, EPS, ALU.mult, ALU.add))

            for t in range(T):
                dve.wait_ge(s_yl[t], 32)
                me.link(dve.scalar_tensor_tensor(out=xres[:, t, :], in0=yv[:, 0, t, :], scalar=gates[:, t:t + 1], in1=xres[:, t, :],
                                                 op0=ALU.mult, op1=ALU.add))
                if t:
                    mean_square(t - 1)
                dve.scalar_tensor_tensor(out=xres[:, t, :], in0=yv[:, 1, t, :], scalar=gates[:, T + t:T + t + 1], in1=xres[:, t, :],
                                         op0=ALU.mult, op1=ALU.add).then_inc(s_x2, 1)
                if t:
                    finish(t - 1)
            mean_square(T - 1)
            finish(T - 1)

        @block.gpsimd
        def _(pool):
            me = Count(pool, s_pool)
            me.inc(pool.memset(ident[:, :], 0.0))
            me.inc(pool.memset(tri[:, :], 1.0))
            me.inc(pool.memset(strict[:, :], 1.0))
            me.inc(pool.memset(ones[:, :], 1.0))
            me.inc(pool.memset(amask[:, :], 0.0))
            me.inc(pool.memset(gmask[:, :], 1.0))
            me.inc(pool.memset(half[:, :], -0.5))
            me.wait()
            one_row = [[1, P]]
            me.inc(pool.affine_select(out=ident[:, :], in_=ident[:, :], compare_op=ALU.not_equal, fill=1.0, base=0,
                                      pattern=[[-1, P]], channel_multiplier=1))
            me.inc(pool.affine_select(out=tri[:, :], in_=tri[:, :], compare_op=ALU.is_ge, fill=0.0, base=0,
                                      pattern=one_row, channel_multiplier=-1))
            me.inc(pool.affine_select(out=strict[:, :], in_=strict[:, :], compare_op=ALU.is_gt, fill=0.0, base=0,
                                      pattern=one_row, channel_multiplier=-1))
            me.inc(pool.affine_select(out=amask[:, :], in_=amask[:, :], compare_op=ALU.is_ge, fill=NEG, base=0,
                                      pattern=[[-1, P]], channel_multiplier=1))
            me.inc(pool.affine_select(out=gmask[:, :], in_=gmask[:, :], compare_op=ALU.is_ge, fill=0.0, base=0,
                                      pattern=one_row, channel_multiplier=-1))
            me.wait()
            me.inc(pool.memset(gmask[0:CH, CH:P], 0.0))
            me.wait()
            pool.memset(ss[:, 7:8], 0.0).then_inc(s_cst, 1)

            rooted = Count(pool, s_pw)

            def root(v):
                pool.wait_ge(s_ms, rooted.n + 1)
                rooted.inc(pool.tensor_tensor(v, v, half[0:v.shape[0], 0:v.shape[1]], ALU.pow))

            def row_roots():
                for t in range(T):
                    root(rstd[:, t:t + 1])

            row_roots()
            root(rstd[0:META, T:T + 1])

            def low_halves(first, end):
                for c in range(first, end):
                    low_half(pool, c)

            low_halves(0, attn_end)

            H = HEADS
            pool.wait_ge(s_rs, 9)
            for b in range(2):
                me.inc(pool.memset(qa[b][:, :, HD:HD + 1], 1.0))
                me.inc(pool.memset(ka[b][:, :, HD + 1:HA], 1.0))
                me.inc(pool.memset(kam[b][0:META, HD + 1:HA], 1.0))
            me.wait()
            pool.wait_ge(s_hr, 3)
            pool.wait_ge(s_c, 1)
            rq = rsq[:, 0:4 * H].rearrange("p (t h) -> p t h", t=T)
            rk_ = rsq[:, 4 * H:8 * H].rearrange("p (t h) -> p t h", t=T)
            c3 = cc[:, 0:T * H].rearrange("p (t h) -> p t h", t=T)
            n3 = ncc[:, 0:T * H].rearrange("p (t h) -> p t h", t=T)
            for h in range(H):
                if h >= 2:
                    pool.wait_ge(s_qkt, 3 * (h - 1))
                b = h % 2
                pool.tensor_tensor(qa[b][:, :, 0:HD], qkvg[:, :, h * HD:(h + 1) * HD],
                                   rq[:, :, h:h + 1].to_broadcast([P, T, HD]), ALU.mult)
                pool.tensor_copy(qa[b][:, :, HD + 1:HA], c3[:, :, h:h + 1])
                pool.tensor_tensor(ka[b][:, :, 0:HD], qkvg[:, :, D + h * HD:D + (h + 1) * HD],
                                   rk_[:, :, h:h + 1].to_broadcast([P, T, HD]), ALU.mult)
                pool.tensor_copy(ka[b][:, :, HD:HD + 1], n3[:, :, h:h + 1])
                pool.tensor_tensor(kam[b][0:META, 0:HD], mkv[0:META, h * HD:(h + 1) * HD],
                                   rsq[0:META, 8 * H + h:8 * H + h + 1].to_broadcast([META, HD]), ALU.mult)
                pool.tensor_copy(kam[b][0:META, HD:HD + 1], ncc[0:META, T * H + h:T * H + h + 1]).then_inc(s_stage, 1)

            low_halves(attn_end, wo_end)
            row_roots()
            low_halves(wo_end, ffn_end)
            for _, t in NORMS:
                root(rstd[:, t:t + 1])
            low_halves(ffn_end, ffn_end + CK_SLOTS)

            pool.wait_ge(s_x2, T)
            pool.dma_start(gainrow[:, :], ffn_norm_2.to_broadcast([P, D])).then_inc(s_row2, 16)

            pool.wait_ge(s_tp, KD * 4 + 1)
            me.link(pool.memset(reset[:, :], 1.0))
            pool.memset(reset[:, :].rearrange("p (c s) -> p c s", c=NCH)[:, :, 0:1], 0.0).then_inc(s_reset, 1)

            kl = max(u for u, v in enumerate(unitsG) if v[0] == "k")
            ends = [ffn_end + c for c in F_POOL] + [gla_end]
            for h in range(GH):
                low_halves(ends[h - 1] if h else ffn_end + CK_SLOTS, ends[h])
                if h == 0:
                    pool.wait_ge(s_gD, evacs(unitsG, kl))
                pool.wait_ge(s_gac, 7 * h + 7)
                me.link(pool.tensor_tensor(ksT[:, h, :], kT[:, h, :], Ex[3], ALU.mult))
                pool.wait_ge(s_gq, h + 1)
                pool.tensor_tensor(qT[:, h, :], qT[:, h, :], Ex[0], ALU.mult)
                pool.tensor_tensor(kT[:, h, :], kT[:, h, :], Ex[1], ALU.mult).then_inc(s_gpl, 1)
            for t in range(T):
                pool.wait_ge(s_er, 2 * t + 2)
                v = gr[:, t, :].rearrange("p (h n) -> p h n", h=GH)
                pool.tensor_tensor(v, v, outn[:, :].unsqueeze(1).to_broadcast([P, GH, GV]), ALU.mult).then_inc(s_gr, 1)
                root(ssg[:, 32 + t * GH:32 + (t + 1) * GH])

            low_halves(gla_end, len(chunks))
            row_roots()
            for t in range(T):
                pool.wait_ge(s_hnrow, t + 1)
                pool.dma_start(hn_dram[t * P:(t + 1) * P, :], xn[:, t, :]).then_inc(s_hnd, 16)
            pool.dma_start(gainrow[:, :], final_norm_2.rearrange("(a n) -> a n", a=1).to_broadcast([P, D])).then_inc(s_row2, 16)

            pool.wait_ge(s_tp, KD * 5 + 1)
            small = dict(base=0, allow_small_or_imprecise_dtypes=True)
            me.inc(pool.iota(desf.rearrange("p (k t) -> p k t", k=2), pattern=[[SEQ, 2], [P, T]], channel_multiplier=1, base=1,
                             allow_small_or_imprecise_dtypes=True))
            me.inc(pool.iota(iog, pattern=[[1, GROUPS], [0, PER]], channel_multiplier=0, **small))
            me.inc(pool.iota(ioe, pattern=[[1, EXPERTS]], channel_multiplier=0, **small))
            me.inc(pool.iota(iob, pattern=[[1, NB]], channel_multiplier=0, **small))
            me.inc(pool.iota(iow, pattern=[[1, C]], channel_multiplier=0, **small))
            me.link(pool.iota(ovc, pattern=[[1, SPILL]], channel_multiplier=0, **small))
            pool.tensor_scalar(ovc, ovc, 0.5, None, ALU.add).then_inc(s_cst, 1)
            pool.wait_ge(s_rt, 1)
            for i in range(4):
                pool.memset(xe[i], 0.0).then_inc(s_xz, 1)
            pool.wait_ge(s_tabs, 1)
            pool.wait_ge(s_hnd, 16 * T)
            pool.wait_ge(s_xz, 4)
            bound_x = pool.to_reg(SEQ - 1)
            bound_y = pool.to_reg(ASG - 1)

            def gather(b, j, n):
                j = j % 4
                wait(pool, s_mx1, b - 3)
                col = ttab[0:C, b:b + 1] if isinstance(b, int) else ttab[0:C, bass.ds(b, 1)]
                pool.tensor_copy(gidx[0:C, j:j + 1], col).then_inc(s_ic, 1)
                pool.wait_ge(s_ic, n)
                pool.sem_inc(s_tick, 1)
                pool.indirect_dma_start(out=xe[j][0:C, :], out_offset=None, in_=hn_dram[:, :],
                                        in_offset=bass.IndirectOffsetOnAxis(ap=gidx[0:C, j:j + 1], axis=0),
                                        bounds_check=bound_x, oob_is_err=False).then_inc(s_xe[j], 16)

            def scatter(b, j, n):
                j = j % 4
                col = dtab[0:C, b:b + 1] if isinstance(b, int) else dtab[0:C, bass.ds(b, 1)]
                pool.tensor_copy(sidx[0:C, j:j + 1], col).then_inc(s_ic, 1)
                pool.wait_ge(s_ic, n)
                pool.wait_ge(s_myA, b + 1)
                pool.wait_ge(s_myD, b + 1)
                pool.sem_inc(s_tick, 1)
                pool.indirect_dma_start(out=y_dram[:, :], out_offset=bass.IndirectOffsetOnAxis(ap=sidx[0:C, j:j + 1], axis=0),
                                        in_=ye[j % 2][0:C, :], in_offset=None,
                                        bounds_check=bound_y, oob_is_err=False).then_inc(s_ys[j % 2], 16)

            gather(0, 0, 1)
            gather(1, 1, 2)
            n = 2
            for j in range(E_SLOTS):
                n += 1
                gather(j + 2, j + 2, n)
                if j:
                    n += 1
                    scatter(j - 1, j - 1, n)
            with pool.Fori(1, EXPERTS // E_SLOTS) as it:
                for j in range(E_SLOTS):
                    gather(it * E_SLOTS + (j + 2), j + 2, it * (2 * E_SLOTS) + (2 * j + 2))
                    scatter(it * E_SLOTS + (j - 1), j - 1, it * (2 * E_SLOTS) + (2 * j + 3))
            scatter(EXPERTS - 1, E_SLOTS - 1, 2 * EXPERTS + 2)
            n_ic = 2 * EXPERTS + 2
            pool.wait_ge(s_tabs, 2)
            n_over = pool.value_load(ovf_i[0:1, SPILL:SPILL + 1], min_val=0, max_val=SPILL)
            with pool.If(n_over > 0):
                with pool.Fori(0, n_over) as i:
                    pool.wait_ge(s_mx1, i + (EXPERTS + 1))
                    pool.tensor_copy(gidx[0:C, 0:1], ttab[0:C, bass.ds(i + EXPERTS, 1)]).then_inc(s_ic, 1)
                    pool.wait_ge(s_ic, i * 2 + (n_ic + 1))
                    pool.sem_inc(s_tick, 1)
                    pool.indirect_dma_start(out=xe[0][0:C, :], out_offset=None, in_=hn_dram[:, :],
                                            in_offset=bass.IndirectOffsetOnAxis(ap=gidx[0:C, 0:1], axis=0),
                                            bounds_check=bound_x, oob_is_err=False).then_inc(s_xe[0], 16)
                    pool.tensor_copy(sidx[0:C, 0:1], dtab[0:C, bass.ds(i + EXPERTS, 1)]).then_inc(s_ic, 1)
                    pool.wait_ge(s_ic, i * 2 + (n_ic + 2))
                    pool.wait_ge(s_myA, i + (EXPERTS + 1))
                    pool.wait_ge(s_myD, i + (EXPERTS + 1))
                    pool.sem_inc(s_tick, 1)
                    pool.indirect_dma_start(out=y_dram[:, :], out_offset=bass.IndirectOffsetOnAxis(ap=sidx[0:C, 0:1], axis=0),
                                            in_=ye[0][0:C, :], in_offset=None,
                                            bounds_check=bound_y, oob_is_err=False).then_inc(s_ys[0], 16)
                    pool.wait_ge(s_ys[0], i * 16 + (8 * EXPERTS + 16))
            pool.wait_ge(s_ys[0], 8 * EXPERTS)
            pool.wait_ge(s_ys[1], 8 * EXPERTS)
            pool.wait_ge(s_my, EXPERTS)
            for t in range(T):
                for k in range(2):
                    o = (k * T + t) * D
                    pool.dma_start(big[:, o:o + D], y_dram[k * SEQ + t * P:k * SEQ + (t + 1) * P, :]).then_inc(s_yl[t], 16)
            row_roots()


_INS = ['x', 'meta_tokens', 'attn_norm', 'ffn_norm', 'final_norm', 'fox_w_in', 'fox_b_f', 'fox_q_norm', 'fox_k_norm',
        'fox_w_out', 'ffn_w_in', 'ffn_w_out', 'attn_norm_2', 'ffn_norm_2', 'final_norm_2', 'gla_w_in_2',
        'gla_w_gate_2', 'gla_b_gate_2', 'gla_out_norm_2', 'gla_w_o_2', 'moe_w_group_2', 'moe_w_expert_2',
        'moe_w1_2', 'moe_w3_2', 'moe_w2_2']


def kernel(**inputs):
    import numpy as _np
    import concourse.bacc as _bacc
    from concourse import mybir as _mybir
    from concourse.bass_utils import run_bass_kernel_spmd as _run

    nc = _bacc.Bacc("TRN2", target_bir_lowering=False, num_devices=1)
    arrays, args = {}, []
    for name in _INS:
        a = _np.ascontiguousarray(inputs[name])
        arrays[f"in_{name}_dram"] = a
        args.append(nc.dram_tensor(f"in_{name}_dram", a.shape, _mybir.dt.from_np(a.dtype), kind="ExternalInput").ap())
    args.append(nc.dram_tensor("out_0_dram", inputs["x"].shape, _mybir.dt.float32, kind="ExternalOutput").ap())
    program(nc, *args)
    r = _run(nc, [arrays], core_ids=[0])
    return r.results[0]["out_0_dram"]
```
